# Optimizing a Trainium2 kernel written in Bass

```python
import jax
import jax.numpy as jnp
from jax import lax
import jax, jax.numpy as jnp
import numpy as np

D_MODEL = 1024
BATCH = 1
SEQ = 512
DEPTH = 1

HEAD_DIM = 64
NSA_HEADS = 8
NSA_KV = 2
SWA_HEADS = 8
SWA_KV = 1
CMP_STRIDE = 16
CMP_LEN = 2 * CMP_STRIDE
CMP_HIDDEN = 256
SEL_LEN = 64
SEL_TOPN = 16
SEL_LOCAL = 2
NSA_WINDOW = 512
SWA_WINDOW = 128
Q_BLOCK = 128
D_FF = 2816
ROPE_THETA = 10000.0
RMS_EPS = 1e-6
FFN_HALF = 0.5
NEG_INF = -1e30
FORCE = 1e9

NSA_Q_W = NSA_HEADS * HEAD_DIM
NSA_KV_W = NSA_KV * HEAD_DIM
NSA_GATE_W = 3 * NSA_HEADS
SWA_Q_W = SWA_HEADS * HEAD_DIM
SWA_KV_W = SWA_KV * HEAD_DIM
IN_WIDTHS = (NSA_Q_W, NSA_KV_W, NSA_KV_W, NSA_KV_W, NSA_KV_W, NSA_KV_W, NSA_KV_W, NSA_GATE_W,
             SWA_Q_W, SWA_KV_W, SWA_KV_W, D_MODEL, D_MODEL)


def _split_points():
    pts, acc = [], 0
    for w in IN_WIDTHS[:-1]:
        acc += w
        pts.append(acc)
    return pts

def _rmsnorm(x, g):
    xf = x.astype(jnp.float32)
    y = xf * lax.rsqrt(jnp.mean(xf * xf, axis=-1, keepdims=True) + RMS_EPS)
    return (y * g.astype(jnp.float32)).astype(x.dtype)

def _swiglu(x, w_gate, w_up, w_down):
    return (jax.nn.silu(x @ w_gate) * (x @ w_up)) @ w_down

def _rope(x, pos):
    half = HEAD_DIM // 2
    inv_freq = ROPE_THETA ** (-jnp.arange(half, dtype=jnp.float32) / half)
    ang = pos.astype(jnp.float32)[..., None] * inv_freq
    cos = jnp.cos(ang)[:, :, None, :]
    sin = jnp.sin(ang)[:, :, None, :]
    xf = x.astype(jnp.float32)
    x1, x2 = xf[..., :half], xf[..., half:]
    return jnp.concatenate([x1 * cos - x2 * sin, x2 * cos + x1 * sin], axis=-1).astype(x.dtype)

def _banded_attention(q, k, v, window, sink):
    B, S, H, D = q.shape
    G = k.shape[2]
    R = H // G
    nb = S // Q_BLOCK
    pad = -(-window // Q_BLOCK) * Q_BLOCK
    L = pad + Q_BLOCK
    kp = jnp.pad(k, ((0, 0), (pad, 0), (0, 0), (0, 0)))
    vp = jnp.pad(v, ((0, 0), (pad, 0), (0, 0), (0, 0)))
    idx = jnp.arange(nb)[:, None] * Q_BLOCK + jnp.arange(L)[None, :]
    kb = kp[:, idx]
    vb = vp[:, idx]
    qb = q.reshape(B, nb, Q_BLOCK, G, R, D)
    s = jnp.einsum('bnqgrd,bnkgd->bngrqk', qb, kb).astype(jnp.float32) * (D ** -0.5)
    qpos = jnp.arange(nb)[:, None] * Q_BLOCK + jnp.arange(Q_BLOCK)[None, :]
    kpos = idx - pad
    diff = qpos[:, :, None] - kpos[:, None, :]
    mask = (diff >= 0) & (diff < window) & (kpos[:, None, :] >= 0)
    s = jnp.where(mask[None, :, None, None], s, NEG_INF)
    if sink is None:
        p = jax.nn.softmax(s, axis=-1)
    else:
        sk = sink.astype(jnp.float32).reshape(G, R)[None, None, :, :, None, None]
        m = jnp.maximum(jnp.max(s, axis=-1, keepdims=True), sk)
        e = jnp.exp(s - m)
        p = e / (jnp.sum(e, axis=-1, keepdims=True) + jnp.exp(sk - m))
    o = jnp.einsum('bngrqk,bnkgd->bnqgrd', p.astype(vb.dtype), vb)
    return o.reshape(B, S, H, D)

def _compress(kv, pe, w1, w2):
    B, S, G, D = kv.shape
    c = kv.reshape(B, S // CMP_STRIDE, CMP_STRIDE, G, D)
    blocks = jnp.concatenate([c[:, :-1], c[:, 1:]], axis=2)
    blocks = blocks + pe[None, None, :, None, :]
    n_cmp = blocks.shape[1]
    flat = blocks.transpose(0, 1, 3, 2, 4).reshape(B, n_cmp, G, CMP_LEN * D)
    return jax.nn.gelu(flat @ w1) @ w2

def _nsa(q, k_cmp, v_cmp, k_slc, v_slc, k_win, v_win, gates, pos, pe_k, wk1, wk2, pe_v, wv1, wv2):
    B, S, H, D = q.shape
    G = NSA_KV
    R = H // G
    scale = D ** -0.5
    n_sel = S // SEL_LEN
    n_top = min(SEL_TOPN, n_sel)
    nb = S // Q_BLOCK
    qg = q.reshape(B, S, G, R, D)
    t = jnp.arange(S)

    kc = _compress(k_cmp, pe_k, wk1, wk2)
    vc = _compress(v_cmp, pe_v, wv1, wv2)
    n_cmp = kc.shape[1]
    kc = _rope(kc, pos[:, CMP_LEN - 1::CMP_STRIDE])
    end = jnp.arange(n_cmp) * CMP_STRIDE + CMP_LEN - 1
    vis = end[None, :] <= t[:, None]
    s = jnp.einsum('bsgrd,bcgd->bgrsc', qg, kc).astype(jnp.float32) * scale
    s = jnp.where(vis, s, NEG_INF)
    p_cmp = jnp.where(vis, jax.nn.softmax(s, axis=-1), 0.0)
    o_cmp = jnp.einsum('bgrsc,bcgd->bsgrd', p_cmp.astype(vc.dtype), vc)

    cs = jnp.arange(n_cmp) * CMP_STRIDE
    ss = jnp.arange(n_sel) * SEL_LEN
    overlap = jnp.clip(jnp.minimum(cs[:, None] + CMP_LEN, ss[None, :] + SEL_LEN)
                       - jnp.maximum(cs[:, None], ss[None, :]), 0, None).astype(jnp.float32) / CMP_LEN
    imp = jnp.einsum('bgrsc,cj->bgsj', p_cmp, overlap)
    blk = jnp.arange(n_sel)[None, :]
    tb = (t // SEL_LEN)[:, None]
    forced = (blk == 0) | ((tb - blk >= 0) & (tb - blk < SEL_LOCAL))
    imp = jnp.where(forced, FORCE, jnp.where(blk > tb, -FORCE, imp))
    _, sel = lax.top_k(imp, n_top)

    kT = k_slc.transpose(0, 2, 1, 3)
    vT = v_slc.transpose(0, 2, 1, 3)
    offs = jnp.arange(SEL_LEN)
    gather = jax.vmap(jax.vmap(lambda a, i: a[i]))

    def one_block(args):
        qb, selb, tq = args
        idx = (selb[..., None] * SEL_LEN + offs).reshape(B, G, Q_BLOCK, n_top * SEL_LEN)
        kb = gather(kT, idx)
        vb = gather(vT, idx)
        sc = jnp.einsum('bqgrd,bgqtd->bgrqt', qb, kb).astype(jnp.float32) * scale
        m = (idx <= tq[None, None, :, None])[:, :, None]
        pr = jax.nn.softmax(jnp.where(m, sc, NEG_INF), axis=-1)
        return jnp.einsum('bgrqt,bgqtd->bqgrd', pr.astype(vb.dtype), vb)

    qs = qg.reshape(B, nb, Q_BLOCK, G, R, D).transpose(1, 0, 2, 3, 4, 5)
    sels = sel.reshape(B, G, nb, Q_BLOCK, n_top).transpose(2, 0, 1, 3, 4)
    tqs = t.reshape(nb, Q_BLOCK)
    o_slc = lax.map(one_block, (qs, sels, tqs))
    o_slc = o_slc.transpose(1, 0, 2, 3, 4, 5).reshape(B, S, G, R, D)

    o_win = _banded_attention(q, k_win, v_win, NSA_WINDOW, None).reshape(B, S, G, R, D)

    g = jax.nn.sigmoid(gates.astype(jnp.float32)).reshape(B, S, 3, G, R, 1)
    o = (g[:, :, 0] * o_cmp.astype(jnp.float32) + g[:, :, 1] * o_slc.astype(jnp.float32)
         + g[:, :, 2] * o_win.astype(jnp.float32))
    return o.astype(q.dtype).reshape(B, S, H * D)

def first_inputs(seed: int = 0) -> dict:
    key = jax.random.key(seed)
    ks = jax.random.split(key, 24)
    f32 = jnp.float32

    def w(k, shape, fan_in):
        return jax.random.normal(k, shape, f32) * fan_in ** -0.5

    def gain(k, shape):
        return 1.0 + 0.02 * jax.random.normal(k, shape, f32)

    w_in_width = sum(IN_WIDTHS)
    return {
        'x': jax.random.normal(ks[0], (BATCH, SEQ, D_MODEL), f32),
        'positions': jnp.broadcast_to(jnp.arange(SEQ, dtype=jnp.int32), (BATCH, SEQ)),
        'norm_ffn1': gain(ks[1], (DEPTH, D_MODEL)),
        'ffn1_gate': w(ks[2], (DEPTH, D_MODEL, D_FF), D_MODEL),
        'ffn1_up': w(ks[3], (DEPTH, D_MODEL, D_FF), D_MODEL),
        'ffn1_down': w(ks[4], (DEPTH, D_FF, D_MODEL), D_FF),
        'norm_mix': gain(ks[5], (DEPTH, D_MODEL)),
        'w_in': w(ks[6], (DEPTH, D_MODEL, w_in_width), D_MODEL),
        'cmp_pe_k': 0.1 * jax.random.normal(ks[7], (DEPTH, CMP_LEN, HEAD_DIM), f32),
        'cmp_k_w1': w(ks[8], (DEPTH, CMP_LEN * HEAD_DIM, CMP_HIDDEN), CMP_LEN * HEAD_DIM),
        'cmp_k_w2': w(ks[9], (DEPTH, CMP_HIDDEN, HEAD_DIM), CMP_HIDDEN),
        'cmp_pe_v': 0.1 * jax.random.normal(ks[10], (DEPTH, CMP_LEN, HEAD_DIM), f32),
        'cmp_v_w1': w(ks[11], (DEPTH, CMP_LEN * HEAD_DIM, CMP_HIDDEN), CMP_LEN * HEAD_DIM),
        'cmp_v_w2': w(ks[12], (DEPTH, CMP_HIDDEN, HEAD_DIM), CMP_HIDDEN),
        'swa_sinks': jax.random.normal(ks[13], (DEPTH, SWA_HEADS), f32),
        'w_branch_a': w(ks[14], (DEPTH, NSA_Q_W, D_MODEL), NSA_Q_W),
        'w_branch_b': w(ks[15], (DEPTH, SWA_Q_W, D_MODEL), SWA_Q_W),
        'w_out': w(ks[16], (DEPTH, D_MODEL, D_MODEL), D_MODEL),
        'norm_ffn2': gain(ks[17], (DEPTH, D_MODEL)),
        'ffn2_gate': w(ks[18], (DEPTH, D_MODEL, D_FF), D_MODEL),
        'ffn2_up': w(ks[19], (DEPTH, D_MODEL, D_FF), D_MODEL),
        'ffn2_down': w(ks[20], (DEPTH, D_FF, D_MODEL), D_FF),
        'norm_final': gain(ks[21], (D_MODEL,)),
    }

def first_block(x, positions, norm_ffn1, ffn1_gate, ffn1_up, ffn1_down, norm_mix, w_in,
              cmp_pe_k, cmp_k_w1, cmp_k_w2, cmp_pe_v, cmp_v_w1, cmp_v_w2, swa_sinks,
              w_branch_a, w_branch_b, w_out, norm_ffn2, ffn2_gate, ffn2_up, ffn2_down, norm_final):
    B, S, _ = x.shape
    pts = _split_points()
    h = x
    for i in range(DEPTH):
        h = h + FFN_HALF * _swiglu(_rmsnorm(h, norm_ffn1[i]), ffn1_gate[i], ffn1_up[i], ffn1_down[i])

        u = _rmsnorm(h, norm_mix[i])
        (nq, kc, vc, ksl, vsl, kwn, vwn, ng, sq, sk, sv, ga, gb) = jnp.split(u @ w_in[i], pts, axis=-1)
        nq = _rope(nq.reshape(B, S, NSA_HEADS, HEAD_DIM), positions)
        kc = kc.reshape(B, S, NSA_KV, HEAD_DIM)
        vc = vc.reshape(B, S, NSA_KV, HEAD_DIM)
        ksl = _rope(ksl.reshape(B, S, NSA_KV, HEAD_DIM), positions)
        vsl = vsl.reshape(B, S, NSA_KV, HEAD_DIM)
        kwn = _rope(kwn.reshape(B, S, NSA_KV, HEAD_DIM), positions)
        vwn = vwn.reshape(B, S, NSA_KV, HEAD_DIM)
        o_a = _nsa(nq, kc, vc, ksl, vsl, kwn, vwn, ng, positions,
                   cmp_pe_k[i], cmp_k_w1[i], cmp_k_w2[i], cmp_pe_v[i], cmp_v_w1[i], cmp_v_w2[i])

        sq = _rope(sq.reshape(B, S, SWA_HEADS, HEAD_DIM), positions)
        sk = _rope(sk.reshape(B, S, SWA_KV, HEAD_DIM), positions)
        sv = sv.reshape(B, S, SWA_KV, HEAD_DIM)
        o_b = _banded_attention(sq, sk, sv, SWA_WINDOW, swa_sinks[i]).reshape(B, S, SWA_Q_W)

        merged = jax.nn.sigmoid(ga) * (o_a @ w_branch_a[i]) + jax.nn.sigmoid(gb) * (o_b @ w_branch_b[i])
        h = h + merged @ w_out[i]

        h = h + FFN_HALF * _swiglu(_rmsnorm(h, norm_ffn2[i]), ffn2_gate[i], ffn2_up[i], ffn2_down[i])
    return _rmsnorm(h, norm_final)


DEPTH_2 = 2

DN_HEADS = 4
DN_DK = 128
DN_DV = 128
DN_QK = DN_HEADS * DN_DK
DN_V = DN_HEADS * DN_DV
DN_CONV = 5
CHUNK = 64
N_DIR = 2
CF_WIDTH = 512
CF_CONV = 31
N_BRANCH = 2
EPS = 1e-6

SIZES = (2 * DN_QK + DN_V,
         DN_V,
         N_DIR * DN_HEADS,
         N_DIR * DN_HEADS,
         CF_WIDTH,
         CF_WIDTH,
         CF_WIDTH,
         N_BRANCH * D_MODEL)
D_IN = sum(SIZES)


def rms_norm(x, w):
    xf = x.astype(jnp.float32)
    y = xf * lax.rsqrt(jnp.mean(xf * xf, axis=-1, keepdims=True) + EPS)
    return (y * w.astype(jnp.float32)).astype(x.dtype)

def layer_norm(x, w, b):
    xf = x.astype(jnp.float32)
    mu = jnp.mean(xf, axis=-1, keepdims=True)
    xc = xf - mu
    y = xc * lax.rsqrt(jnp.mean(xc * xc, axis=-1, keepdims=True) + EPS)
    return (y * w.astype(jnp.float32) + b.astype(jnp.float32)).astype(x.dtype)

def l2_normalize(t):
    return t * lax.rsqrt(jnp.sum(t * t, axis=-1, keepdims=True) + EPS)

def depthwise_conv_centred(u, w):
    k = w.shape[0]
    return lax.conv_general_dilated(
        u, w[:, None, :].astype(u.dtype), window_strides=(1,),
        padding=[(k // 2, k // 2)], dimension_numbers=('NWC', 'WIO', 'NWC'),
        feature_group_count=u.shape[-1])

def gated_delta_chunked(q, k, v, g, beta):
    bsz, seq, nh, dk = q.shape
    dv = v.shape[-1]
    n = seq // CHUNK
    q = q.reshape(bsz, n, CHUNK, nh, dk).transpose(0, 3, 1, 2, 4) * (dk ** -0.5)
    k = k.reshape(bsz, n, CHUNK, nh, dk).transpose(0, 3, 1, 2, 4)
    v = v.reshape(bsz, n, CHUNK, nh, dv).transpose(0, 3, 1, 2, 4)
    g = jnp.cumsum(g.reshape(bsz, n, CHUNK, nh).transpose(0, 3, 1, 2), axis=-1)
    beta = beta.reshape(bsz, n, CHUNK, nh).transpose(0, 3, 1, 2)

    incl = jnp.tril(jnp.ones((CHUNK, CHUNK), dtype=bool))
    strict = jnp.tril(jnp.ones((CHUNK, CHUNK), dtype=bool), k=-1)
    diff = g[..., :, None] - g[..., None, :]
    decay = jnp.where(incl, jnp.exp(jnp.where(incl, diff, 0.0)), 0.0)

    k_beta = k * beta[..., None]
    lmat = jnp.where(strict, jnp.einsum('bhncd,bhnsd->bhncs', k_beta, k) * decay, 0.0)
    eye = jnp.eye(CHUNK, dtype=jnp.float32)
    rhs = jnp.concatenate([v * beta[..., None], k_beta * jnp.exp(g)[..., None]], axis=-1)
    sol = lax.linalg.triangular_solve(eye + lmat, rhs, left_side=True, lower=True,
                                      unit_diagonal=True)
    value, k_cum = sol[..., :dv], sol[..., dv:]

    attn = jnp.einsum('bhncd,bhnsd->bhncs', q, k) * decay
    q_dec = q * jnp.exp(g)[..., None]
    g_last = g[..., -1]
    k_dec = k * jnp.exp(g_last[..., None] - g)[..., None]

    xs = (jnp.moveaxis(value, 2, 0), jnp.moveaxis(k_cum, 2, 0), jnp.moveaxis(attn, 2, 0),
          jnp.moveaxis(q_dec, 2, 0), jnp.moveaxis(k_dec, 2, 0),
          jnp.moveaxis(jnp.exp(g_last), 2, 0))

    def step(state, inp):
        val_n, kc_n, a_n, qd_n, kd_n, dl_n = inp
        v_new = val_n - jnp.einsum('bhcd,bhde->bhce', kc_n, state)
        o_n = jnp.einsum('bhcd,bhde->bhce', qd_n, state) + jnp.einsum('bhcs,bhse->bhce', a_n, v_new)
        state = state * dl_n[..., None, None] + jnp.einsum('bhcd,bhce->bhde', kd_n, v_new)
        return state, o_n

    s0 = jnp.zeros((bsz, nh, dk, dv), dtype=jnp.float32)
    _, o = lax.scan(step, s0, xs)
    return o.transpose(1, 0, 3, 2, 4).reshape(bsz, seq, nh, dv)

def hybrid_mixer(h, w_in, qkv_conv_w, a_log, dt_bias, dn_norm_w, w_dn_out,
                 cf_conv_w, cf_conv_b, cf_ln_w, cf_ln_b, w_cf_out, gate_b, w_out):
    bsz, seq, _ = h.shape
    pts = []
    acc = 0
    for s in SIZES[:-1]:
        acc += s
        pts.append(acc)
    proj = h @ w_in
    qkv, z_a, a_lg, b_lg, cf_val, cf_glu, z_b, gate_lg = jnp.split(proj, pts, axis=-1)

    qkv = jax.nn.silu(depthwise_conv_centred(qkv, qkv_conv_w))
    q = qkv[..., :DN_QK].astype(jnp.float32).reshape(bsz, seq, DN_HEADS, DN_DK)
    k = qkv[..., DN_QK:2 * DN_QK].astype(jnp.float32).reshape(bsz, seq, DN_HEADS, DN_DK)
    v = qkv[..., 2 * DN_QK:].astype(jnp.float32).reshape(bsz, seq, DN_HEADS, DN_DV)
    q = l2_normalize(q)
    k = l2_normalize(k)
    a_lg = a_lg.astype(jnp.float32).reshape(bsz, seq, N_DIR, DN_HEADS)
    g = -jnp.exp(a_log.astype(jnp.float32)) * jax.nn.softplus(a_lg + dt_bias.astype(jnp.float32))
    beta = jax.nn.sigmoid(b_lg.astype(jnp.float32).reshape(bsz, seq, N_DIR, DN_HEADS))
    o_fwd = gated_delta_chunked(q, k, v, g[:, :, 0], beta[:, :, 0])
    flip = lambda t: jnp.flip(t, axis=1)
    o_bwd = flip(gated_delta_chunked(flip(q), flip(k), flip(v), flip(g[:, :, 1]), flip(beta[:, :, 1])))
    o = o_fwd + o_bwd
    o = o * lax.rsqrt(jnp.mean(o * o, axis=-1, keepdims=True) + EPS) * dn_norm_w.astype(jnp.float32)
    o = o * jax.nn.silu(z_a.astype(jnp.float32).reshape(bsz, seq, DN_HEADS, DN_DV))
    y_a = o.reshape(bsz, seq, DN_V).astype(h.dtype) @ w_dn_out

    u = cf_val * jax.nn.sigmoid(cf_glu)
    u = depthwise_conv_centred(u, cf_conv_w) + cf_conv_b
    u = jax.nn.silu(layer_norm(u, cf_ln_w, cf_ln_b))
    y_b = (u * jax.nn.silu(z_b)) @ w_cf_out

    gate = jax.nn.sigmoid(gate_lg + gate_b).reshape(bsz, seq, N_BRANCH, D_MODEL)
    y = gate[:, :, 0] * y_a + gate[:, :, 1] * y_b
    return y @ w_out

def second_inputs(seed: int = 0) -> dict:
    key = jax.random.key(seed)
    ks = jax.random.split(key, 17)
    nrm = jax.random.normal
    x = nrm(ks[0], (BATCH, SEQ, D_MODEL), jnp.float32)
    norm_w = 1.0 + 0.05 * nrm(ks[1], (DEPTH_2, D_MODEL), jnp.float32)
    w_in = nrm(ks[2], (DEPTH_2, D_MODEL, D_IN), jnp.float32) * D_MODEL ** -0.5
    qkv_conv_w = nrm(ks[3], (DEPTH_2, DN_CONV, 2 * DN_QK + DN_V), jnp.float32) * DN_CONV ** -0.5
    a_log = jnp.log(jax.random.uniform(ks[4], (DEPTH_2, N_DIR, DN_HEADS), jnp.float32, 1.0, 16.0))
    dt = jnp.exp(jax.random.uniform(ks[5], (DEPTH_2, N_DIR, DN_HEADS), jnp.float32,
                                    float(np.log(1e-3)), float(np.log(1e-1))))
    dt_bias = dt + jnp.log(-jnp.expm1(-dt))
    dn_norm_w = 1.0 + 0.05 * nrm(ks[6], (DEPTH_2, DN_DV), jnp.float32)
    w_dn_out = nrm(ks[7], (DEPTH_2, DN_V, D_MODEL), jnp.float32) * DN_V ** -0.5
    cf_conv_w = nrm(ks[8], (DEPTH_2, CF_CONV, CF_WIDTH), jnp.float32) * CF_CONV ** -0.5
    cf_conv_b = 0.02 * nrm(ks[9], (DEPTH_2, CF_WIDTH), jnp.float32)
    cf_ln_w = 1.0 + 0.05 * nrm(ks[10], (DEPTH_2, CF_WIDTH), jnp.float32)
    cf_ln_b = 0.02 * nrm(ks[11], (DEPTH_2, CF_WIDTH), jnp.float32)
    w_cf_out = nrm(ks[12], (DEPTH_2, CF_WIDTH, D_MODEL), jnp.float32) * CF_WIDTH ** -0.5
    gate_b = 0.02 * nrm(ks[13], (DEPTH_2, N_BRANCH * D_MODEL), jnp.float32)
    w_out = nrm(ks[14], (DEPTH_2, D_MODEL, D_MODEL), jnp.float32) * D_MODEL ** -0.5
    final_norm_w = 1.0 + 0.05 * nrm(ks[15], (D_MODEL,), jnp.float32)
    return {'x': x, 'norm_w': norm_w, 'w_in': w_in, 'qkv_conv_w': qkv_conv_w,
            'a_log': a_log, 'dt_bias': dt_bias, 'dn_norm_w': dn_norm_w, 'w_dn_out': w_dn_out,
            'cf_conv_w': cf_conv_w, 'cf_conv_b': cf_conv_b, 'cf_ln_w': cf_ln_w, 'cf_ln_b': cf_ln_b,
            'w_cf_out': w_cf_out, 'gate_b': gate_b, 'w_out': w_out, 'final_norm_w': final_norm_w}

def second_block(x, norm_w, w_in, qkv_conv_w, a_log, dt_bias, dn_norm_w, w_dn_out,
              cf_conv_w, cf_conv_b, cf_ln_w, cf_ln_b, w_cf_out, gate_b, w_out, final_norm_w):
    for l in range(DEPTH_2):
        h = rms_norm(x, norm_w[l])
        x = x + hybrid_mixer(h, w_in[l], qkv_conv_w[l], a_log[l], dt_bias[l], dn_norm_w[l],
                             w_dn_out[l], cf_conv_w[l], cf_conv_b[l], cf_ln_w[l], cf_ln_b[l],
                             w_cf_out[l], gate_b[l], w_out[l])
    return rms_norm(x, final_norm_w)


def setup_inputs(seed=0):
    out = dict(first_inputs(seed))
    for name, value in second_inputs(seed + 1).items():
        if name != "x":
            out[name + "_2"] = value
    return out


def reference(
    x, positions, norm_ffn1, ffn1_gate, ffn1_up, ffn1_down, norm_mix, w_in, cmp_pe_k, cmp_k_w1,
    cmp_k_w2, cmp_pe_v, cmp_v_w1, cmp_v_w2, swa_sinks, w_branch_a, w_branch_b, w_out, norm_ffn2,
    ffn2_gate, ffn2_up, ffn2_down, norm_final, norm_w_2, w_in_2, qkv_conv_w_2, a_log_2,
    dt_bias_2, dn_norm_w_2, w_dn_out_2, cf_conv_w_2, cf_conv_b_2, cf_ln_w_2, cf_ln_b_2,
    w_cf_out_2, gate_b_2, w_out_2, final_norm_w_2,
):
    x = first_block(
        x, positions, norm_ffn1, ffn1_gate, ffn1_up, ffn1_down, norm_mix, w_in, cmp_pe_k,
        cmp_k_w1, cmp_k_w2, cmp_pe_v, cmp_v_w1, cmp_v_w2, swa_sinks, w_branch_a, w_branch_b,
        w_out, norm_ffn2, ffn2_gate, ffn2_up, ffn2_down, norm_final,
    )
    return second_block(
        x, norm_w_2, w_in_2, qkv_conv_w_2, a_log_2, dt_bias_2, dn_norm_w_2, w_dn_out_2,
        cf_conv_w_2, cf_conv_b_2, cf_ln_w_2, cf_ln_b_2, w_cf_out_2, gate_b_2, w_out_2,
        final_norm_w_2,
    )


_drawn_inputs = setup_inputs


def setup_inputs(seed=0):
    import zlib

    import numpy as np

    out = dict(_drawn_inputs(seed))
    spreads = {}
    factors = {'norm_ffn1': 5.194,
     'norm_mix': 8.0,
     'cmp_pe_k': 8.0,
     'cmp_pe_v': 11.509,
     'swa_sinks': 41.733,
     'norm_ffn2': 6.222,
     'cf_conv_b_2': 5.419,
     'cf_ln_w_2': 3.728,
     'cf_ln_b_2': 8.0,
     'gate_b_2': 8.0,
     'dn_norm_w_2': 3.007}
    for name, (base, spread) in spreads.items():
        noise = np.random.default_rng([zlib.crc32(name.encode()), seed]).standard_normal(out[name].shape)
        drawn = base * np.exp(spread * noise) if base else spread * noise
        out[name] = jnp.asarray(drawn.astype(out[name].dtype))
    for name, factor in factors.items():
        out[name] = (out[name] * factor).astype(out[name].dtype)
    return out
```

```python
from contextlib import ExitStack, contextmanager

import numpy as np

import concourse.bass as bass
from concourse import mybir

F32 = mybir.dt.float32
F32R = mybir.dt.float32r
I32 = mybir.dt.int32
U8 = mybir.dt.uint8
ALU = mybir.AluOpType
ACT = mybir.ActivationFunctionType
AX = mybir.AxisListType

P = 128
S = 512
NT = S // P
D = 1024
KD = D // P
FF = 2816
NF = FF // P
HD = 64
EPS = 1e-6
NEG = -1e30
SCALE = HD ** -0.5
CMP_N = 31
DN_H = 4
CF_TAPS = 31
CF_PAD = CF_TAPS // 2
QKV_TAPS = 5
QKV_PAD = QKV_TAPS // 2
N_LAYER = 2

UNIT = 8 * P
RING = 4
AHEAD = 2
U_FFN = 3 * NF
U_MIX = 8 + 8 + 24 + 8
U_LAYER = 8 + 8 + 12 + 24 + 8
N_UNITS = 2 * U_FFN + U_MIX + N_LAYER * U_LAYER
SPARE = RING + AHEAD

COLS = {}
_at = 0
for _name, _n in (("norm_ffn1", 8), ("norm_mix", 8), ("norm_ffn2", 8), ("norm_final", 8), ("final2", 8),
                  ("sinks", 8), ("pe_k", 16), ("pe_v", 16), ("inv_freq", 1)):
    COLS[_name] = (_at, _n)
    _at += _n
N_COLS = _at
LCOLS = {}
_at = 0
for _name, _n in (("norm", 8), ("qkv_w", 12 * QKV_TAPS), ("cf_w", 4 * CF_TAPS), ("cf_b", 4), ("ln_w", 4),
                  ("ln_b", 4), ("gate_b", 16), ("dn_w", 1), ("a_log", 8), ("dt_bias", 8)):
    LCOLS[_name] = (_at, _n)
    _at += _n
N_LCOLS = _at
MATS = ["ident", "ones", "rot", "tri_f", "tri_b", "negstrict_f", "negstrict_b"]
LEVELS = [1, 2, 4, 8, 16, 32, 64]


class Lin:

    def __init__(self, const=0, terms=()):
        self.const, self.terms = const, tuple(terms)

    def add(self, n):
        return Lin(self.const + n, self.terms)

    def term(self, reg, n):
        return Lin(self.const, self.terms + ((reg, n),)) if n else self

    def value(self, div=1):
        v = self.const // div
        for reg, n in self.terms:
            assert n % div == 0
            v = reg * (n // div) + v
        return v


class Tok:

    def __init__(self, key, lin):
        self.key, self.lin = key, lin


class Counter:

    BIAS = 256

    def __init__(self, nc, sems, steps):
        self.nc, self.sems, self.steps = nc, sems, steps
        self.count = {k: Lin(self.BIAS) for k in sems}
        self.count["unit"] = Lin(0)
        self.loops = []
        self.settle = None
        self.found = {}

    def inc(self, key, ins, n=1):
        ins.then_inc(self.sems[key], n)
        self.count[key] = self.count[key].add(n)
        return Tok(key, self.count[key])

    def wait(self, eng, *toks):
        for t in toks:
            if t is not None:
                assert t.lin.const >= 0, (t.key, t.lin.const)
                eng.wait_ge(self.sems[t.key], t.lin.value())

    def now(self, *keys):
        return [Tok(k, self.count[k]) for k in keys]

    def mark(self, name, tok):
        start = self.loops[-1][1]
        self.loops[-1][2][name] = (tok.key, tok.lin.const - start[tok.key].const)

    def prev(self, name):
        loop, start, _, reg = self.loops[-1]
        key, off = self.steps.get(loop, {}).get("marks", {}).get(name, ("pe", 0))
        per = self.steps.get(loop, {}).get("per", {}).get(key, 0)
        return Tok(key, start[key].add(off - per).term(reg, per))

    @contextmanager
    def loop(self, name, n):
        per = self.steps.get(name, {}).get("per", {})
        start = dict(self.count)
        if self.loops:
            self.settle()
            start = dict(self.count)
        with self.nc.Fori(0, n) as reg:
            self.count = {k: c.term(reg, per.get(k, 0)) for k, c in start.items()}
            marks = {}
            self.loops.append((name, start, marks, reg))
            yield reg
            self.loops.pop()
            self.found[name] = {
                "per": {k: c.const - start[k].const for k, c in self.count.items()}, "marks": marks}
        self.count = {k: c.add(n * per.get(k, 0)) for k, c in start.items()}


def program(nc, a, steps):
    pe, act, dve, pool, sp = nc.tensor, nc.scalar, nc.vector, nc.gpsimd, nc.sync
    top = ExitStack()

    def sb(name, shape, dt=F32, ctx=None, side=None):
        return (ctx or top).enter_context(nc.sbuf_tensor(name, shape, dt, side=side))

    names = ["pe", "act", "dve", "pool", "whi", "wlo", "used"]
    sems = {k: top.enter_context(nc.semaphore("s_" + k)) for k in names}
    landed = [top.enter_context(nc.semaphore(f"s_landed{i}")) for i in range(RING)]
    s_par = top.enter_context(nc.semaphore("s_par"))
    s_lpar = top.enter_context(nc.semaphore("s_lpar"))
    s_aux = top.enter_context(nc.semaphore("s_aux"))
    s_out = top.enter_context(nc.semaphore("s_out"))
    C = Counter(nc, sems, steps)
    bias_eng = {"pe": pe, "used": pe, "act": act, "whi": act, "dve": dve, "pool": pool, "wlo": pool}
    for k in names:
        bias_eng[k].sem_inc(sems[k], C.BIAS)

    C.settle = lambda: settle_all()

    def PE(ins): return C.inc("pe", ins)
    def A(ins): return C.inc("act", ins)
    def V(ins): return C.inc("dve", ins)
    def G(ins): return C.inc("pool", ins)
    def need(eng, *toks): C.wait(eng, *toks)

    def settle_all():
        settle_pe()
        settle_dve(2)
        G(pool.tensor_tensor(epsc[:, 5:6], epsc[:, 0:1], epsc[:, 0:1], ALU.add))

    def settle_pe():
        pe.matmul(ps[:, 7, 0:2], mat("ident"), mats[:, 0, 0:2], start=True, stop=True)

    def settle_dve(n):
        V(dve.tensor_copy(epsc[:, 2 + n:3 + n], epsc[:, 0:1]))

    def rendezvous():
        for eng, own in ((pe, "pe"), (act, "act"), (dve, "dve"), (pool, "pool")):
            need(eng, *C.now(*[k for k in ("pe", "act", "dve", "pool", "used")]))

    h = sb("h", [P, KD, S])
    xh = sb("xh", [P, KD, S], F32R)
    xl = sb("xl", [P, KD, S], F32R)
    raw = sb("raw", [P, RING, UNIT])
    whi = sb("whi", [P, RING, UNIT], F32R)
    wlo = sb("wlo", [P, RING, UNIT], F32R)
    cols = sb("cols", [P, N_COLS])
    mats = sb("mats", [P, len(MATS), P])
    lcol = sb("lcol", [P, N_LCOLS])
    lcols = sb("lcols", [P, N_LAYER, N_LCOLS])
    rt = sb("rt", [P, 4, S])
    epsc = sb("epsc", [P, 6])
    ps = top.enter_context(nc.psum_tensor("ps", [P, 8, S], F32))

    def col(name, i=0, n=1):
        return cols[:, COLS[name][0] + i:COLS[name][0] + i + n]

    def lcl(name, i=0, n=1):
        return lcol[:, LCOLS[name][0] + i:LCOLS[name][0] + i + n]

    def mat(name):
        return mats[:, MATS.index(name), :]

    for i in range(RING):
        sp.dma_start(raw[:, i, :], a["stream"][i]).then_inc(landed[i], 16)
    act.dma_start(h[:], a["xT"]).then_inc(s_par, 16)
    act.dma_start(cols[:], a["cols"]).then_inc(s_par, 16)
    act.dma_start(mats[:], a["mats"]).then_inc(s_par, 16)
    act.dma_start(lcols[:], a["lcols"]).then_inc(s_par, 16)
    c0 = V(dve.memset(epsc[:, 0:1], EPS))
    c0 = V(dve.memset(epsc[:, 1:2], 1.0))
    for eng in (pe, act, dve, pool):
        eng.wait_ge(s_par, 64)
        need(eng, c0)

    def split_unit(unit):
        slot = unit.const % RING
        act.wait_ge(landed[slot], unit.add(RING).value(RING) * 16)
        need(act, Tok("used", unit.add(C.BIAS + 1 - RING)))
        C.inc("whi", act.copy(whi[:, slot, :], raw[:, slot, :]))
        hi = Tok("whi", unit.add(C.BIAS + 1))
        need(pool, hi)
        C.inc("wlo", pool.tensor_tensor(wlo[:, slot, :], raw[:, slot, :], whi[:, slot, :].bitcast(F32),
                                        ALU.subtract))
        need(sp, Tok("wlo", unit.add(C.BIAS + 1)))
        sp.dma_start(raw[:, slot, :], a["stream"][unit.add(RING).value()]).then_inc(landed[slot], 16)

    for i in range(AHEAD):
        split_unit(Lin(i))

    def stream(tiles):
        unit = C.count["unit"]
        split_unit(unit.add(AHEAD))
        slot = unit.const % RING
        need(pe, Tok("wlo", unit.add(C.BIAS + 1)))
        for t, (out, hi, lo, first, last, waits) in enumerate(tiles):
            need(pe, *waits)
            wh, wl = whi[:, slot, t * P:(t + 1) * P], wlo[:, slot, t * P:(t + 1) * P]
            m = out.shape[0]
            pe.matmul(out, wh[:, 0:m], hi, start=first, stop=False)
            pe.matmul(out, wh[:, 0:m], lo, start=False, stop=False)
            ins = pe.matmul(out, wl[:, 0:m], hi, start=False, stop=last)
        C.count["unit"] = unit.add(1)
        return C.inc("used", ins)

    def stream_x(out, waits=(), ready=None):
        tiles = [(out, xh[:, k, :], xl[:, k, :], k == 0, k == KD - 1,
                  (list(waits) if k == 0 else []) + ([ready[k]] if ready else [])) for k in range(KD)]
        return stream(tiles)

    def rms_scale(src, n, total, psb, deps):
        acc = None
        sq_done, add_done = [], []
        for k in range(n):
            if k >= 2:
                need(act, add_done[k - 2])
            need(act, *deps(k))
            sq_done.append(A(act.activation(rt[:, k % 2, :], src(k), ACT.Square)))
            need(dve, sq_done[k])
            if k == 0:
                acc = V(dve.tensor_copy(rt[:, 2, :], rt[:, 0, :]))
            else:
                need(dve, acc)
                acc = V(dve.tensor_tensor(rt[:, 2, :], rt[:, 2, :], rt[:, k % 2, :], ALU.add))
            add_done.append(acc)
        need(pe, acc)
        t = PE(pe.matmul(psb, mat("ones"), rt[:, 2, :], start=True, stop=True))
        need(act, t)
        t = A(act.activation(rt[:, 0, :], psb, ACT.Sqrt, bias=epsc[:, 0:1], scale=1.0 / total))
        need(dve, t)
        return V(dve.reciprocal(rt[:, 3, :], rt[:, 0, :]))

    def norm_to_x(gain):
        rendezvous()
        rs = rms_scale(lambda k: h[:, k, :], KD, D, ps[:, 7, :], lambda k: ())
        need(dve, rs)
        lo, ready = [], []
        for k in range(KD):
            if k >= 2:
                need(dve, lo[k - 2])
            y = V(dve.scalar_tensor_tensor(out=rt[:, k % 2, :], in0=h[:, k, :], scalar=gain(k),
                                           in1=rt[:, 3, :], op0=ALU.mult, op1=ALU.mult))
            need(act, y)
            hi = A(act.copy(xh[:, k, :], rt[:, k % 2, :]))
            need(dve, hi)
            lo.append(V(dve.tensor_tensor(xl[:, k, :], rt[:, k % 2, :], xh[:, k, :].bitcast(F32),
                                          ALU.subtract)))
            ready.append(lo[-1])
        return ready

    def split_into(hi, lo, srcs):
        for k, src in enumerate(srcs):
            t = A(act.copy(hi[:, k, :], src))
            need(dve, t)
            V(dve.tensor_tensor(lo[:, k, :], src, hi[:, k, :].bitcast(F32), ALU.subtract))

    def ffn(name, gain):
        ready = norm_to_x(lambda k: col(gain, k))
        with ExitStack() as mem:
            mid = sb(name + "_mid", [P, NF, S], ctx=mem)
            sil = sb(name + "_sil", [P, 2, S], ctx=mem)
            mh = sb(name + "_mh", [P, 2, S], F32R, ctx=mem)
            ml = sb(name + "_ml", [P, 2, S], F32R, ctx=mem)
            last = None
            with C.loop(name + "_up", NF // 2) as i:
                for s in range(2):
                    g, u = ps[:, 2 * s, :], ps[:, 2 * s + 1, :]
                    free = C.prev(f"mid{s}")
                    tg = stream_x(g, [free], ready if s == 0 else None)
                    need(act, tg, free)
                    ts = A(act.activation(sil[:, s, :], g, ACT.Silu))
                    tu = stream_x(u)
                    need(dve, ts, tu)
                    last = V(dve.tensor_tensor(mid[:, i * 2 + s, :], sil[:, s, :], u, ALU.mult))
                    C.mark(f"mid{s}", last)
            rendezvous()

            def down(f, s, first, last_f, free):
                need(act, free)
                hi = A(act.copy(mh[:, s, :], mid[:, f, :]))
                need(dve, hi)
                lo = V(dve.tensor_tensor(ml[:, s, :], mid[:, f, :], mh[:, s, :].bitcast(F32), ALU.subtract))
                return stream([(ps[:, d, :], mh[:, s, :], ml[:, s, :], first, last_f, [lo] if d == 0 else [])
                               for d in range(KD)])

            down(0, 0, True, False, None)
            down(1, 1, False, False, None)
            with C.loop(name + "_down", (NF - 6) // 4) as i:
                t = []
                for s in range(4):
                    free = C.prev(f"u{s + 2}") if s < 2 else t[s - 2]
                    t.append(down(i * 4 + 2 + s, s % 2, False, False, free))
                    C.mark(f"u{s}", t[-1])
            used = C.count["used"]
            t = [Tok("used", used.add(-1)), Tok("used", used)]
            for s in range(4):
                t.append(down(NF - 4 + s, s % 2, False, s == 3, t[s]))
            done = C.now("used")
            for d in range(KD):
                need(dve, *done)
                V(dve.scalar_tensor_tensor(out=h[:, d, :], in0=ps[:, d, :], scalar=0.5, in1=h[:, d, :],
                                           op0=ALU.mult, op1=ALU.add))
            rendezvous()

    def store_h():
        rendezvous()
        need(sp, *C.now("pe", "act", "dve", "pool"))
        sp.dma_start(a["outT"], h[:]).then_inc(s_out, 16)
        sp.wait_ge(s_out, 16)
        for i in range(RING):
            sp.wait_ge(landed[i], 16 * ((C.count["unit"].const + SPARE - 1 - i) // RING + 1))

    def rope_tables(cosT, sinT, tmp):
        posi = tmp[:, 0, :].bitcast(I32)
        act.dma_start(posi, a["pos"]).then_inc(s_aux, 16)
        dve.wait_ge(s_aux, 16)
        t = V(dve.tensor_copy(tmp[:, 1, :], posi))
        need(dve, t)
        t = V(dve.tensor_scalar(tmp[:, 1, :], tmp[:, 1, :], col("inv_freq"), None, ALU.mult))
        need(dve, t)
        two_pi = 2 * np.pi
        c1 = float(np.float32(6.28125))
        c2 = float(np.float32(two_pi - c1))
        c3 = float(np.float32(two_pi - c1 - float(np.float32(c2))))
        magic = 1.5 * 2.0 ** 23
        for out, shift in ((sinT, 0.0), (cosT, 0.25)):
            t = V(dve.tensor_scalar(tmp[:, 2, :], tmp[:, 1, :], 1 / two_pi, shift, ALU.mult, ALU.add))
            need(dve, t)
            t = V(dve.tensor_scalar(tmp[:, 2, :], tmp[:, 2, :], magic, -magic, ALU.add, ALU.add))
            need(dve, t)
            src = tmp[:, 1, :]
            for cc in (c1, c2, c3):
                t = V(dve.scalar_tensor_tensor(out=tmp[:, 3, :], in0=tmp[:, 2, :], scalar=-cc, in1=src,
                                               op0=ALU.mult, op1=ALU.add))
                need(dve, t)
                src = tmp[:, 3, :]
            t = V(dve.tensor_scalar(tmp[:, 3, :], tmp[:, 3, :], shift * two_pi, float(np.float32(np.pi)),
                                    ALU.add, ALU.min))
            need(dve, t)
            t = V(dve.tensor_scalar(tmp[:, 3, :], tmp[:, 3, :], -float(np.float32(np.pi)), None, ALU.max))
            need(act, t)
            t = A(act.activation(out, tmp[:, 3, :], ACT.Sin))
            need(dve, t)

    def mixer():
        ready = norm_to_x(lambda k: col("norm_mix", k))
        mem = ExitStack()
        qall = sb("qall", [P, 8, S], ctx=mem)
        m_att = ExitStack()
        kd = sb("kd", [P, 5, S], ctx=m_att)
        kcc = sb("kcc", [P, 2, 32], ctx=m_att)
        vcc = sb("vcc", [32, 2, HD], ctx=m_att)
        vtok = sb("vtok", [P, NT, 2, P], ctx=m_att)
        vsw = sb("vsw", [P, NT, P], ctx=m_att)
        gts = sb("gts", [P, NT, 24], ctx=m_att)
        msk = sb("msk", [P, 3 * P + NT * 32 + NT], ctx=m_att)
        causal, band = msk[:, 0:P], msk[:, P:3 * P]
        vis = msk[:, 3 * P:3 * P + NT * 32].rearrange("p (t n) -> p t n", t=NT)
        valid = msk[:, 3 * P + NT * 32:]
        m_prj = ExitStack()
        cosT = sb("cosT", [P, S], ctx=m_prj)
        sinT = sb("sinT", [P, S], ctx=m_prj)
        w1 = sb("w1", [P, 16, 2 * P], ctx=m_prj)
        w2k = sb("w2k", [P, 2, P], ctx=m_prj)
        w2v = sb("w2v", [P, 2, HD], ctx=m_prj)
        kc2 = sb("kc2", [P, 2, 2, S // 2], ctx=m_prj)
        blk = sb("blk", [P, 16, 2, 32], ctx=m_prj)
        hid = sb("hid", [P, 2, 64], ctx=m_prj)
        hid2 = sb("hid2", [P, 2, 64], ctx=m_prj)
        hid3 = sb("hid3", [P, 2, 64], ctx=m_prj)
        xr = sb("xr", [P, 2, S], ctx=m_prj)
        tmp = sb("tmpp", [P, 4, S], ctx=m_prj)
        act.dma_start(msk[:], a["masks"]).then_inc(s_lpar, 16)
        act.dma_start(w1[:], a["w1"][0]).then_inc(s_lpar, 16)
        act.dma_start(w2k[:], a["w2k"]).then_inc(s_lpar, 16)
        act.dma_start(w2v[:], a["w2v"]).then_inc(s_lpar, 16)
        rope_tables(cosT[:], sinT[:], tmp)
        for eng in (pe, act, dve, pool):
            eng.wait_ge(s_lpar, 64)
        rendezvous()

        def rope(src, out, s, freed):
            t = A(act.copy(xr[:, s, :], src))
            need(pe, t, freed)
            r = PE(pe.matmul(ps[:, 4 + s, :], mat("rot"), xr[:, s, :], start=True, stop=True))
            need(dve, t, freed)
            t1 = V(dve.tensor_tensor(tmp[:, 2 * s, :], xr[:, s, :], cosT[:], ALU.mult))
            need(dve, r)
            t2 = V(dve.tensor_tensor(tmp[:, 2 * s + 1, :], ps[:, 4 + s, :], sinT[:], ALU.mult))
            need(dve, t1, t2)
            return out(tmp[:, 2 * s, :], tmp[:, 2 * s + 1, :])

        with C.loop("q_proj", 2) as i:
            done = []
            for s in range(4):
                free = C.prev(f"q{s}")
                t = stream_x(ps[:, s, :], [free], ready if s == 0 else None)
                need(act, t, done[s - 2] if s >= 2 else C.prev(f"q{s + 2}"))
                done.append(rope(ps[:, s, :], lambda x, y: V(dve.tensor_tensor(
                    qall[:, i * 4 + s, :], x, y, ALU.add)), s % 2, done[s - 2] if s >= 2 else C.prev(f"q{s + 2}")))
                C.mark(f"q{s}", done[-1])
        rendezvous()
        done = []
        for s in range(3):
            t = stream_x(ps[:, s, :])
            free = done[s - 2] if s >= 2 else None
            need(act, t, free)

            def out(x, y, s=s):
                if s == 2:
                    return V(dve.tensor_tensor(kd[:, 4, :], x, y, ALU.add))
                for g in range(2):
                    for half in range(2):
                        t = V(dve.tensor_tensor(kd[64 * half:64 * half + 64, 2 * s + g, :],
                                                x[64 * g:64 * g + 64, :], y[64 * g:64 * g + 64, :], ALU.add))
                return t
            done.append(rope(ps[:, s, :], out, s % 2, free))
        for s in range(2):
            t = stream_x(ps[:, 3 * (1 - s), :], [done[0]] if s else [])
            need(act, t)
            for g in range(2):
                for par in range(2):
                    A(act.copy(kc2[64 * par:64 * par + 64, s, g, :],
                               ps[64 * g:64 * g + 64, 3 * (1 - s), par:S:2]))
        kc_ready = C.now("act")
        for s in range(3):
            t = stream_x(ps[:, 1 + s, :], [done[1 if s == 0 else 2]] + kc_ready)
            need(act, t, *done, *C.now("pe"))
            t = A(act.copy(xr[:, s % 2, :], ps[:, 1 + s, :]))
            need(pe, t, *C.now("act", "dve"))
            for j in range(NT):
                t = PE(pe.transpose(ps[:, 4 + s, j * P:(j + 1) * P], xr[:, s % 2, j * P:(j + 1) * P], mat("ident")))
            need(act, t)
            pt = ps[:, 4 + s, :].rearrange("p (j c) -> p j c", j=NT)
            A(act.copy(vtok[:, :, s, :] if s < 2 else vsw[:], pt))
        need(act, *C.now("act"))
        t = A(act.activation(gts[:], vsw[:, :, HD:HD + 24], ACT.Sigmoid))
        need(dve, t)
        for j in range(NT):
            V(dve.tensor_scalar(gts[:, j, 0:8], gts[:, j, 0:8], valid[:, j:j + 1], None, ALU.mult))

        for w in range(2):
            if w == 1:
                need(act, *C.now("pe"))
                act.dma_start(w1[:], a["w1"][1]).then_inc(s_lpar, 16)
                pe.wait_ge(s_lpar, 80)
            need(dve, *C.now("act", "pe"))
            for g in range(2):
                for lp in range(16):
                    V(dve.tensor_scalar(blk[:, lp, g, 0:CMP_N], kc2[:, w, g, lp:lp + 8 * (CMP_N - 1) + 1:8],
                                        col("pe_k" if w == 0 else "pe_v", lp), None, ALU.add))
            need(pe, *C.now("dve", "act"))
            for m in range(2):
                for lp in range(16):
                    ins = pe.matmul(ps[:, 7, m * 64:m * 64 + 62], w1[:, lp, m * P:(m + 1) * P],
                                    blk[:, lp, :, 0:CMP_N], start=lp == 0, stop=lp == 15)
                t = PE(ins)
            z = ps[:, 7, 0:128].rearrange("p (m n) -> p m n", m=2)[:, :, 0:62]
            x1, x2, x3 = hid[:, :, 0:62], hid2[:, :, 0:62], hid3[:, :, 0:62]
            need(act, t)
            t = A(act.copy(x1, z))
            need(dve, t)
            t = V(dve.tensor_tensor(x2, x1, x1, ALU.mult))
            need(dve, t)
            t = V(dve.tensor_scalar(x2, x2, 0.044715, 1.0, ALU.mult, ALU.add))
            need(dve, t)
            t = V(dve.tensor_tensor(x2, x2, x1, ALU.mult))
            need(act, t)
            t = A(act.activation(x3, x2, ACT.Tanh, scale=float(np.sqrt(2 / np.pi))))
            need(dve, t)
            t = V(dve.tensor_scalar(x3, x3, 0.5, 0.5, ALU.mult, ALU.add))
            need(dve, t)
            t = V(dve.tensor_tensor(x1, x3, x1, ALU.mult))
            need(pe, t)
            if w == 0:
                for m in range(2):
                    ins = pe.matmul(ps[:, 6, 0:62], w2k[:, m, :], hid[:, m, 0:62], start=m == 0, stop=m == 1)
                t = PE(ins)
                need(act, t)
                t = A(act.copy(xr[:, 0, 0:62], ps[:, 6, 0:62]))
                need(pe, t)
                r = PE(pe.matmul(ps[:, 6, 64:126], mat("rot"), xr[:, 0, 0:62], start=True, stop=True))
                need(dve, r)
                for g in range(2):
                    o = 31 * g
                    t1 = V(dve.tensor_tensor(tmp[:, 0, o:o + 31], xr[:, 0, o:o + 31], cosT[:, 31:S:16], ALU.mult))
                    t2 = V(dve.tensor_tensor(tmp[:, 1, o:o + 31], ps[:, 6, 64 + o:64 + o + 31],
                                             sinT[:, 31:S:16], ALU.mult))
                    need(dve, t1, t2)
                    V(dve.tensor_tensor(kcc[:, g, 0:31], tmp[:, 0, o:o + 31], tmp[:, 1, o:o + 31], ALU.add))
            else:
                for g in range(2):
                    for m in range(2):
                        ins = pe.matmul(ps[0:31, 5 - g, 0:HD], hid[:, m, 31 * g:31 * g + 31],
                                        w2v[:, m, :], start=m == 0, stop=m == 1)
                    t = PE(ins)
                    need(act, t)
                    A(act.copy(vcc[0:31, g, :], ps[0:31, 5 - g, 0:HD]))
        rendezvous()
        m_prj.close()
        pr = sb("pr", [P, 2, 2 * S], ctx=m_att)
        pt = sb("pt", [P, 2, 2, S], ctx=m_att)
        ptc = sb("ptc", [32, 2, S], ctx=m_att)
        ce = sb("ce", [P, 2, NT, 32], ctx=m_att)
        cst = sb("cst", [P, 3, 2, NT], ctx=m_att)
        qS, kS = rt[:, 0, :], rt[:, 1:3, :]
        kcS = sb("kcS", [P, 32], ctx=m_att)
        vS = sb("vS", [P, NT, 2, HD], ctx=m_att)
        vcS = sb("vcS", [32, HD], ctx=m_att)
        gS = sb("gS", [P, NT, 3, 2], ctx=m_att)
        skS = sb("skS", [P, 2], ctx=m_att)
        st = sb("st", [P, 2, 5, 4], ctx=m_att)

        def heads(branches, qchunk):
            steps_ = [(hh, i) for hh in range(2) for i in range(NT)]
            nsa = branches == 3
            scored, probs, turned, evacd, pved = {}, {}, {}, {}, {}

            def spans(i):
                return (0, i + 1) if nsa else (max(i - 1, 0), i + 1)

            def score(n):
                hh, i = steps_[n]
                b, p = 64 * hh, n % 2
                j0, j1 = spans(i)
                if n >= 2:
                    need(pe, probs[n - 2])
                q = qS[b:b + 64, i * P:(i + 1) * P]
                for br in range(2 if nsa else 1):
                    ins = pe.matmul(ps[:, 2 * p + br, 0:(j1 - j0) * P], q, kS[b:b + 64, br, j0 * P:j1 * P],
                                    start=True, stop=True)
                scored[n] = PE(ins)

            def softmax(n):
                hh, i = steps_[n]
                p = n % 2
                j0, j1 = spans(i)
                w = (j1 - j0) * P
                if n >= 2:
                    need(dve, turned[n - 2])
                    need(act, turned[n - 2])
                need(dve, scored[n])
                if nsa:
                    banks = ps[:, 2 * p:2 * p + 2, :]
                    last = banks[:, :, w - P:w]
                    mask = causal.unsqueeze(1).broadcast_to([P, 2, P])
                else:
                    banks = ps[:, 2 * p:2 * p + 1, :]
                    last = banks[:, 0, 0:w]
                    mask = band[:, 2 * P - w:]
                nb = 2 if nsa else 1
                srcs = [(ps[:, 2 * p + br, 0:w], pr[:, p, br * S:br * S + w]) for br in range(nb)]
                mx, nm, sm, rs, wt = (st[:, p, r, :] for r in range(5))
                t = V(dve.tensor_tensor(last, last, mask, ALU.add))
                need(dve, t)
                t = V(dve.tensor_reduce(mx[:, 0:nb], banks[:, :, 0:w], AX.X, ALU.max))
                need(dve, t)
                if nsa:
                    t = V(dve.tensor_scalar(nm[:, 0:nb], mx[:, 0:nb], -SCALE, None, ALU.mult))
                else:
                    t = V(dve.tensor_scalar(mx[:, 1:2], mx[:, 0:1], SCALE, skS[:, hh:hh + 1], ALU.mult, ALU.max))
                    need(dve, t)
                    t = V(dve.tensor_scalar(nm[:, 0:1], mx[:, 1:2], -1.0, None, ALU.mult))
                need(act, t)
                for br, (src, dst) in enumerate(srcs):
                    t = A(act.activation(dst, src, ACT.Exp, bias=nm[:, br:br + 1], scale=SCALE,
                                         accum_out=sm[:, br:br + 1]))
                if not nsa:
                    t = A(act.activation(sm[:, 1:2], skS[:, hh:hh + 1], ACT.Exp, bias=nm[:, 0:1]))
                    need(dve, t)
                    t = V(dve.tensor_tensor(sm[:, 0:1], sm[:, 0:1], sm[:, 1:2], ALU.add))
                need(dve, t)
                t = V(dve.reciprocal(rs[:, 0:nb], sm[:, 0:nb]))
                need(dve, t)
                if nsa:
                    t = V(dve.tensor_tensor(wt[:, 0:nb], rs[:, 0:nb], gS[:, i, 0:2, hh], ALU.mult))
                    need(dve, t)
                for br, (_, dst) in enumerate(srcs):
                    sc = wt[:, br:br + 1] if nsa else rs[:, 0:1]
                    t = V(dve.tensor_scalar(dst, dst, sc, None, ALU.mult))
                probs[n] = t

            def turn(n):
                hh, i = steps_[n]
                p = n % 2
                j0, j1 = spans(i)
                need(pe, probs[n])
                if n >= 1:
                    need(pe, *evacd[n - 1])
                for br in range(2 if nsa else 1):
                    for j in range(j1 - j0):
                        ins = pe.transpose(ps[:, 5 + br, j * P:(j + 1) * P],
                                           pr[:, p, br * S + j * P:br * S + (j + 1) * P], mat("ident"))
                turned[n] = PE(ins)
                w = (j1 - j0) * P
                need(act, turned[n], pved.get(n - 2))
                t = A(act.copy(pt[:, p, 0, 0:w], ps[:, 5, 0:w]))
                ev = [t]
                if nsa:
                    need(dve, turned[n], pved.get(n - 2))
                    ev.append(V(dve.tensor_copy(pt[:, p, 1, 0:w], ps[:, 6, 0:w])))
                evacd[n] = ev

            def apply(n):
                hh, i = steps_[n]
                b, p = 64 * hh, n % 2
                j0, j1 = spans(i)
                need(pe, *evacd[n])
                out = ps[b:b + 64, 7, i * P:(i + 1) * P]
                terms = [(vS[:, j0 + j, br, :], pt[:, p, br, j * P:(j + 1) * P])
                         for br in range(2 if nsa else 1) for j in range(j1 - j0)]
                if nsa:
                    terms.append((vcS[0:31, :], ptc[0:31, hh, i * P:(i + 1) * P]))
                for k, (v, w) in enumerate(terms):
                    ins = pe.matmul(out, v, w, start=k == 0, stop=k == len(terms) - 1)
                pved[n] = PE(ins)

            def compressed():
                for hh in range(2):
                    for i in range(NT):
                        ins = pe.matmul(ps[:, 4 + 3 * hh, 32 * i:32 * i + CMP_N], qS[64 * hh:64 * hh + 64, i * P:(i + 1) * P],
                                        kcS[64 * hh:64 * hh + 64, 0:CMP_N], start=True, stop=True)
                t = PE(ins)
                need(dve, t)
                for hh in range(2):
                    t = V(dve.tensor_tensor(ce[:, hh, :, 0:CMP_N], ps[:, 4 + 3 * hh, 0:P].rearrange(
                        "p (i n) -> p i n", i=NT)[:, :, 0:CMP_N], vis[:, :, 0:CMP_N], ALU.add))
                need(dve, t)
                e = ce[:, :, :, 0:CMP_N]
                bc = lambda r: cst[:, r, :, :].unsqueeze(3).broadcast_to([P, 2, NT, CMP_N])
                t = V(dve.tensor_reduce(cst[:, 0, :, :], e, AX.X, ALU.max))
                need(dve, t)
                t = V(dve.tensor_tensor(e, e, bc(0), ALU.subtract))
                need(act, t)
                t = A(act.activation(e, e, ACT.Exp, scale=SCALE))
                need(dve, t)
                t = V(dve.tensor_reduce(cst[:, 1, :, :], e, AX.X, ALU.add))
                need(dve, t)
                t = V(dve.reciprocal(cst[:, 2, :, :], cst[:, 1, :, :]))
                need(dve, t)
                t = V(dve.tensor_tensor(cst[:, 1, :, :], cst[:, 2, :, :], gS[:, :, 2, :].rearrange("p t h -> p h t"),
                                        ALU.mult))
                need(dve, t)
                t = V(dve.tensor_tensor(e, e, bc(1), ALU.mult))
                need(pe, t)
                for hh in range(2):
                    for i in range(NT):
                        ins = pe.transpose(ps[0:31, 5 + hh, i * P:(i + 1) * P], ce[:, hh, i, 0:CMP_N], mat("ident"))
                t = PE(ins)
                need(act, t)
                for hh in range(2):
                    t = A(act.copy(ptc[0:31, hh, :], ps[0:31, 5 + hh, :]))
                return t

            score(0)
            score(1)
            softmax(0)
            if nsa:
                need(pe, compressed())
            for n in range(8):
                if n + 1 < 8:
                    softmax(n + 1)
                turn(n)
                if n + 2 < 8:
                    score(n + 2)
                apply(n)
            need(act, pved[7])
            A(act.copy(qall[:, qchunk, :], ps[:, 7, :]))

        gts_v = gts[:].rearrange("p t (b h) -> p t b h", b=3)
        vtok_v = vtok[:].rearrange("p t b (g d) -> p t b g d", g=2)
        with C.loop("nsa_group", 2) as g:
            rendezvous()
            G(pool.tensor_copy(kS[:, 0, :], kd[:, g, :]))
            G(pool.tensor_copy(kS[:, 1, :], kd[:, g + 2, :]))
            G(pool.tensor_copy(kcS[:, 0:CMP_N], kcc[:, g, 0:CMP_N]))
            V(dve.tensor_copy(vcS[0:31, :], vcc[0:31, g, :]))
            for br in range(2):
                V(dve.tensor_copy(vS[:, :, br, :], vtok_v[:, :, br, g, :]))
            with C.loop("nsa_pair", 2) as c:
                rendezvous()
                G(pool.tensor_copy(qS, qall[:, g * 2 + c, :]))
                for dst, br in ((2, 0), (0, 1), (1, 2)):
                    V(dve.tensor_copy(gS[:, :, dst, :], gts_v[:, :, br, bass.ds(g * 4 + c * 2, 2)]))
                rendezvous()
                heads(3, g * 2 + c)
        rendezvous()
        G(pool.tensor_copy(kS[:, 0, :], kd[:, 4, :]))
        V(dve.tensor_copy(vS[:, :, 0, :], vsw[:, :, 0:HD]))
        with C.loop("swa_pair", 4) as c:
            rendezvous()
            G(pool.tensor_copy(qS, qall[:, c + 4, :]))
            V(dve.tensor_copy(skS[:], cols[:, bass.ds(c * 2 + COLS["sinks"][0], 2)]))
            rendezvous()
            heads(1, c + 4)
        rendezvous()
        m_att.close()
        oh = sb("oh", [P, 8, S], F32R, mem)
        ol = sb("ol", [P, 8, S], F32R, mem)
        split_into(oh, ol, [qall[:, c, :] for c in range(8)])
        merge("m1", oh, ol, None)
        mem.close()

    def merge(name, fh, fl, gate_b):
        with ExitStack() as mem:
            yh = sb(name + "_yh", [P, KD, S], F32R, mem)
            yl = sb(name + "_yl", [P, KD, S], F32R, mem)
            sg = sb(name + "_sg", [P, 2, 2, S], ctx=mem)
            gb = sb(name + "_gb", [P, 2, 4], ctx=mem)
            ym = rt
            rendezvous()
            with C.loop(name + "_gate", 2) as i:
                if gate_b:
                    for r in range(2):
                        need(dve, *C.now("act"))
                        tb = V(dve.tensor_copy(gb[:, r, :], gate_b(r, i)))
                    need(act, tb)
                done = []
                for s in range(4):
                    p = s % 2
                    free = done[s - 2] if s >= 2 else C.prev(f"y{s + 2}")
                    bank = 4 * p
                    for r in range(2):
                        t = stream_x(ps[:, bank + r, :], [free])
                        need(act, t, free)
                        ts = A(act.activation(sg[:, p, r, :], ps[:, bank + r, :], ACT.Sigmoid,
                                              bias=gb[:, r, s:s + 1] if gate_b else 0.0))
                    tiles = [(ps[:, bank + 2 + r, :], fh[:, 4 * r + k, :], fl[:, 4 * r + k, :], k == 0, k == 3, [])
                             for r in range(2) for k in range(4)]
                    t = stream(tiles)
                    need(dve, ts, t)
                    t0 = V(dve.tensor_tensor(sg[:, p, 0, :], sg[:, p, 0, :], ps[:, bank + 2, :], ALU.mult))
                    t1 = V(dve.tensor_tensor(sg[:, p, 1, :], sg[:, p, 1, :], ps[:, bank + 3, :], ALU.mult))
                    need(dve, t0, t1)
                    t0 = V(dve.tensor_tensor(ym[:, p, :], sg[:, p, 0, :], sg[:, p, 1, :], ALU.add))
                    need(act, t0)
                    t = A(act.copy(yh[:, i * 4 + s, :], ym[:, p, :]))
                    need(dve, t)
                    done.append(V(dve.tensor_tensor(yl[:, i * 4 + s, :], ym[:, p, :],
                                                    yh[:, i * 4 + s, :].bitcast(F32), ALU.subtract)))
                    C.mark(f"y{s}", done[-1])
            rendezvous()
            with C.loop(name + "_out", 2) as i:
                for s in range(4):
                    t = stream([(ps[:, s, :], yh[:, k, :], yl[:, k, :], k == 0, k == KD - 1,
                                 [C.prev(f"h{s}")] if k == 0 else []) for k in range(KD)])
                    need(dve, t)
                    C.mark(f"h{s}", V(dve.tensor_tensor(h[:, i * 4 + s, :], h[:, i * 4 + s, :], ps[:, s, :],
                                                        ALU.add)))
            rendezvous()

    def norm_h(gain):
        rendezvous()
        rs = rms_scale(lambda k: h[:, k, :], KD, D, ps[:, 7, :], lambda k: ())
        need(dve, rs)
        for k in range(KD):
            V(dve.scalar_tensor_tensor(out=h[:, k, :], in0=h[:, k, :], scalar=gain(k), in1=rt[:, 3, :],
                                       op0=ALU.mult, op1=ALU.mult))
        rendezvous()

    def lane_scale(src, p, total, deps):
        need(act, *deps)
        t = A(act.activation(rt[:, p, :], src, ACT.Square))
        need(pe, t)
        t = PE(pe.matmul(ps[:, 4 + p, :], mat("ones"), rt[:, p, :], start=True, stop=True))
        need(act, t)
        t = A(act.activation(rt[:, p, :], ps[:, 4 + p, :], ACT.Sqrt, bias=epsc[:, 0:1], scale=1.0 / total))
        need(dve, t)
        return V(dve.reciprocal(rt[:, p, :], rt[:, p, :]))

    def heads4(row):
        return row.unsqueeze(2).broadcast_to([P, DN_H, P])

    def all_heads(m):
        return m.unsqueeze(1).broadcast_to([P, DN_H, P])

    def layer(l, wab, levels):
        t = V(dve.tensor_copy(lcol[:], lcols[:, l, :]))
        for eng in (act, pool):
            need(eng, t)
        need(dve, t)
        ready = norm_to_x(lambda k: lcl("norm", k))
        keep, wide = ExitStack(), ExitStack()
        za = sb("za", [P, 4, S], ctx=keep)
        zb = sb("zb", [P, 4, S], ctx=keep)
        cu = sb("cu", [P, 4, S], ctx=keep)
        o = sb("o", [P, 4, S], ctx=keep)
        small = sb("small", [P, 10, NT, 8], ctx=keep)
        gl, bt = small[:, 8], small[:, 9]
        qkv = sb("qkv", [P, 12, S], ctx=wide, side="right")
        m_prj = ExitStack()
        up = sb("up", [P, 4, S + 2 * CF_PAD], ctx=m_prj)
        cp = sb("cp", [P, 2, S + 2 * QKV_PAD], ctx=m_prj)
        acc = sb("acc", [P, 4, S], ctx=m_prj)
        wabh = sb("wabh", [P, KD, 16], F32R, m_prj)
        wabl = sb("wabl", [P, KD, 16], F32R, m_prj)
        tap = sb("tap", [P, 4 * QKV_TAPS], ctx=m_prj)
        z0 = V(dve.memset(up[:], 0.0))
        z0 = V(dve.memset(cp[:], 0.0))
        V(dve.memset(o[:], 0.0))

        wsrc = wab[:, l, :].rearrange("p (k n) -> p k n", k=KD)
        t = V(dve.tensor_copy(wabh[:], wsrc))
        need(dve, t)
        t = V(dve.tensor_tensor(wabl[:], wsrc, wabh[:].bitcast(F32), ALU.subtract))
        need(pe, t, *ready, *C.now("act", "dve"))
        for j in range(NT):
            out = ps[:, 6, 16 * j:16 * j + 16]
            for k in range(KD):
                xa, xb = xh[:, k, j * P:(j + 1) * P], xl[:, k, j * P:(j + 1) * P]
                pe.matmul(out, xa, wabh[:, k, :], start=k == 0, stop=False)
                pe.matmul(out, xa, wabl[:, k, :], start=False, stop=False)
                ins = pe.matmul(out, xb, wabh[:, k, :], start=False, stop=k == KD - 1)
        ab_done = PE(ins)

        need(act, z0)
        need(dve, z0)
        with C.loop("glu", 2) as i:
            for s in range(2):
                free = C.prev(f"u{s}")
                tg = stream_x(ps[:, 2 * s, :], [free])
                need(act, tg, free)
                ts = A(act.activation(acc[:, s, :], ps[:, 2 * s, :], ACT.Sigmoid))
                tv = stream_x(ps[:, 2 * s + 1, :])
                need(dve, ts, tv)
                C.mark(f"u{s}", V(dve.tensor_tensor(up[:, i * 2 + s, CF_PAD:CF_PAD + S], acc[:, s, :],
                                                    ps[:, 2 * s + 1, :], ALU.mult)))
        raw_ab = ps[:, 6, 0:16 * NT].rearrange("p (t n) -> p t n", t=NT)
        v = [small[:, n] for n in range(8)]
        tok8 = lambda c: c.unsqueeze(1).broadcast_to([P, NT, 8])
        need(act, ab_done)
        A(act.activation(bt, raw_ab[:, :, 8:16], ACT.Sigmoid))
        t = A(act.activation(v[7][:, 0, :], lcl("a_log", 0, 8), ACT.Exp))
        need(dve, t)
        chain = [
            lambda: V(dve.tensor_tensor(v[0], raw_ab[:, :, 0:8], tok8(lcl("dt_bias", 0, 8)), ALU.add)),
            lambda: V(dve.tensor_scalar(v[1], v[0], -1.0, None, ALU.mult)),
            lambda: V(dve.tensor_tensor(v[1], v[0], v[1], ALU.max)),
            lambda: A(act.activation(v[2], v[1], ACT.Exp, scale=-1.0)),
            lambda: V(dve.tensor_scalar(v[3], v[2], 1.0, None, ALU.add)),
            lambda: V(dve.tensor_scalar(v[4], v[3], -1.0, 1e-30, ALU.add, ALU.add)),
            lambda: V(dve.reciprocal(v[4], v[4])),
            lambda: A(act.activation(v[5], v[3], ACT.Ln)),
            lambda: V(dve.scalar_tensor_tensor(out=v[5], in0=v[5], scalar=1e-30, in1=v[4], op0=ALU.add,
                                               op1=ALU.mult)),
            lambda: V(dve.tensor_tensor(v[5], v[5], v[2], ALU.mult)),
            lambda: V(dve.scalar_tensor_tensor(out=v[5], in0=v[0], scalar=0.0, in1=v[5], op0=ALU.max, op1=ALU.add)),
            lambda: V(dve.scalar_tensor_tensor(out=gl, in0=v[5], scalar=-1.0, in1=tok8(v[7][:, 0, :]), op0=ALU.mult,
                                               op1=ALU.mult)),
        ]
        for f in chain:
            t = f()
            need(act, t)
            need(dve, t)

        rendezvous()
        zs = []
        for part, z in enumerate((za, zb)):
            for s in range(4):
                t = stream_x(ps[:, s, :], [zs[s]] if part else [])
                need(act, t)
                zs.append(A(act.activation(z[:, s, :], ps[:, s, :], ACT.Silu)))
            last = {}
            for k in range(CF_TAPS):
                for c in (2 * part, 2 * part + 1):
                    src, w = up[:, c, k:k + S], lcl("cf_w", CF_TAPS * c + k)
                    if k == 0:
                        last[c] = V(dve.tensor_scalar(cu[:, c, :], src, w, lcl("cf_b", c), ALU.mult, ALU.add))
                    else:
                        need(dve, last[c])
                        last[c] = V(dve.scalar_tensor_tensor(out=cu[:, c, :], in0=src, scalar=w, in1=cu[:, c, :],
                                                             op0=ALU.mult, op1=ALU.add))

        need(pe, *zs[4:])
        with C.loop("qkv", 3) as i:
            need(dve, *C.now("act", "dve"))
            tw = V(dve.tensor_copy(tap[:, 0:4 * QKV_TAPS],
                                   lcol[:, bass.ds(i * (4 * QKV_TAPS) + LCOLS["qkv_w"][0], 4 * QKV_TAPS)]))
            need(dve, tw)
            conv, outs = [], []
            for s in range(4):
                p = s % 2
                t = stream_x(ps[:, s, :], [C.prev(f"cp{s}")])
                need(act, t, conv[s - 2] if s >= 2 else C.prev(f"conv{s + 2}"))
                t = A(act.copy(cp[:, p, QKV_PAD:QKV_PAD + S], ps[:, s, :]))
                C.mark(f"cp{s}", t)
                need(dve, t, outs[s - 2] if s >= 2 else C.prev(f"out{s + 2}"))
                for k in range(QKV_TAPS):
                    w = tap[:, s * QKV_TAPS + k:s * QKV_TAPS + k + 1]
                    if k == 0:
                        t = V(dve.tensor_scalar(acc[:, p, :], cp[:, p, k:k + S], w, None, ALU.mult))
                    else:
                        need(dve, t)
                        t = V(dve.scalar_tensor_tensor(out=acc[:, p, :], in0=cp[:, p, k:k + S], scalar=w,
                                                       in1=acc[:, p, :], op0=ALU.mult, op1=ALU.add))
                conv.append(t)
                C.mark(f"conv{s}", t)
                need(act, t)
                outs.append(A(act.activation(qkv[:, i * 4 + s, :], acc[:, p, :], ACT.Silu)))
                C.mark(f"out{s}", outs[-1])
        rendezvous()
        for c in range(8):
            t = lane_scale(qkv[:, c, :], c % 2, 1.0, C.now("dve") if c >= 2 else [])
            need(dve, t)
            V(dve.scalar_tensor_tensor(out=qkv[:, c, :], in0=qkv[:, c, :], scalar=P ** -0.5 if c < 4 else 1.0,
                                       in1=rt[:, c % 2, :], op0=ALU.mult, op1=ALU.mult))
        def channel_sum(src, bank):
            t = V(dve.tensor_tensor(acc[:, 0, :], src(0), src(1), ALU.add))
            for c in (2, 3):
                need(dve, t)
                t = V(dve.tensor_tensor(acc[:, 0, :], acc[:, 0, :], src(c), ALU.add))
            need(pe, t)
            return PE(pe.matmul(ps[:, bank, :], mat("ones"), acc[:, 0, :], start=True, stop=True))
        rendezvous()
        t = channel_sum(lambda c: cu[:, c, :], 6)
        need(dve, t)
        for c in range(4):
            t = V(dve.scalar_tensor_tensor(out=cu[:, c, :], in0=ps[:, 6, :], scalar=-1.0 / (4 * P), in1=cu[:, c, :],
                                           op0=ALU.mult, op1=ALU.add))
        need(act, t)
        for c in range(4):
            t = A(act.activation(up[:, c, 0:S], cu[:, c, :], ACT.Square))
        need(dve, t)
        t = channel_sum(lambda c: up[:, c, 0:S], 7)
        need(act, t)
        t = A(act.activation(rt[:, 0, :], ps[:, 7, :], ACT.Sqrt, bias=epsc[:, 0:1], scale=1.0 / (4 * P)))
        need(dve, t)
        t = V(dve.reciprocal(rt[:, 1, :], rt[:, 0, :]))
        need(dve, t)
        for c in range(4):
            t = V(dve.tensor_tensor(cu[:, c, :], cu[:, c, :], rt[:, 1, :], ALU.mult))
            need(act, t)
            t = A(act.activation(cu[:, c, :], cu[:, c, :], ACT.Silu, bias=lcl("ln_b", c), scale=lcl("ln_w", c)))
            need(dve, t)
            V(dve.tensor_tensor(cu[:, c, :], cu[:, c, :], zb[:, c, :], ALU.mult))
        rendezvous()
        m_prj.close()
        delta(qkv, gl, bt, o, levels)
        wide.close()
        for c in range(4):
            t = lane_scale(o[:, c, :], c % 2, float(P), C.now("dve") if c >= 2 else [])
            need(dve, t)
            t = V(dve.scalar_tensor_tensor(out=o[:, c, :], in0=o[:, c, :], scalar=lcl("dn_w"), in1=rt[:, c % 2, :],
                                           op0=ALU.mult, op1=ALU.mult))
            need(dve, t)
            V(dve.tensor_tensor(o[:, c, :], o[:, c, :], za[:, c, :], ALU.mult))
        need(act, *C.now("dve"))
        need(dve, *C.now("dve"))
        fh = sb("fh", [P, 8, S], F32R, wide, side="right")
        fl = sb("fl", [P, 8, S], F32R, wide, side="right")
        split_into(fh, fl, [o[:, c, :] for c in range(4)] + [cu[:, c, :] for c in range(4)])
        rendezvous()
        keep.close()
        merge("m2", fh, fl, lambda r, i: lcol[:, bass.ds(i * 4 + 8 * r + LCOLS["gate_b"][0], 4)])
        wide.close()

    def delta(qkv, gl, bt, o, levels):
        mem = ExitStack()
        bufs = [[sb(f"dl{d}_{n}", [P, DN_H, P], ctx=mem) for n in range(9)] + [
            rt[:, 2 * d + r, :].rearrange("p (h c) -> p h c", h=DN_H) for r in range(2)] for d in range(2)]
        sm = sb("dl_small", [P, 2, 8, DN_H], ctx=mem)

        def direction(d, i):
            KT, Y, T, DT, qd, kg, kdec, vt, U, AT, St = bufs[d]
            gs, be, gc, gtot, eg, et, ekd, tmp = (sm[:, d, r, :] for r in range(8))
            at = i * P if d == 0 else i * (-P) + (NT - 1) * P
            tile = i if d == 0 else i * (-1) + (NT - 1)
            tri = mat("tri_f" if d == 0 else "tri_b")
            strict = mat("negstrict_f" if d == 0 else "negstrict_b")
            B = [ps[:, 4 * d + r, :] for r in range(4)]
            B4 = [b.rearrange("p (h c) -> p h c", h=DN_H) for b in B]
            q, k, v_ = (qkv[:, 4 * r:4 * r + 4, bass.ds(at, P)] for r in range(3))

            def per_head(f):
                for hd in range(DN_H):
                    ins = f(hd)
                return PE(ins)

            tk = G(pool.tensor_copy(KT[:] if d < 2 else KT, k))
            tv = A(act.copy(Y[:], v_))
            V(dve.tensor_copy(gs, gl[:, tile, 4 * d:4 * d + 4]))
            tg = V(dve.tensor_copy(be, bt[:, tile, 4 * d:4 * d + 4]))
            need(dve, tg)
            tb = V(dve.tensor_copy(T[:], heads4(gs)))
            need(pe, tb, tk)
            t = per_head(lambda n: pe.matmul(B[0][:, n * P:(n + 1) * P], T[:, n, :], tri, start=True, stop=True))
            pe.matmul(B[1][:, 0:4], tri, gs, start=True, stop=True)
            t1 = PE(pe.matmul(B[1][:, 4:8], mat("ones"), gs, start=True, stop=True))
            tkk = per_head(lambda n: pe.matmul(B[2][:, n * P:(n + 1) * P], KT[:, n, :], KT[:, n, :], start=True,
                                               stop=True))
            tqk = per_head(lambda n: pe.matmul(B[3][:, n * P:(n + 1) * P], KT[:, n, :], q[:, n, :], start=True,
                                               stop=True))
            yield
            need(act, t1)
            A(act.copy(gc, B[1][:, 0:4]))
            t = A(act.copy(gtot, B[1][:, 4:8]))
            need(dve, t)
            ts = V(dve.tensor_tensor(DT[:], B4[0], heads4(gc), ALU.subtract))
            te = V(dve.tensor_tensor(tmp, gtot, gc, ALU.subtract))
            need(act, ts, te)
            tq = A(act.activation(qd[:], B4[0], ACT.Exp))
            A(act.activation(eg, gc, ACT.Exp))
            A(act.activation(et, gtot, ACT.Exp))
            tx = A(act.activation(ekd, tmp, ACT.Exp))
            need(dve, ts)
            t = V(dve.tensor_scalar(DT[:], DT[:], 0.0, None, ALU.min))
            need(act, t)
            t = A(act.activation(DT[:], DT[:], ACT.Exp))
            need(pe, tq, tv)
            ttk = per_head(lambda n: pe.transpose(B[0][:, n * P:(n + 1) * P], KT[:, n, :], mat("ident")))
            need(pe, t1, *C.now("act"))
            ttv = per_head(lambda n: pe.transpose(B[1][:, n * P:(n + 1) * P], Y[:, n, :], mat("ident")))
            yield
            need(dve, tx)
            t2 = V(dve.tensor_scalar(eg, eg, -1.0, None, ALU.mult))
            tq2 = V(dve.tensor_tensor(qd[:], qd[:], q, ALU.mult))
            need(dve, t)
            t = V(dve.tensor_tensor(DT[:], DT[:], all_heads(tri), ALU.mult))
            need(dve, t, tkk)
            ta = V(dve.tensor_tensor(AT[:], B4[2], DT[:], ALU.mult))
            need(dve, ta)
            ta = V(dve.tensor_tensor(AT[:], AT[:], all_heads(strict), ALU.mult))
            need(pe, ta)
            ta = per_head(lambda n: pe.transpose(B[2][:, n * P:(n + 1) * P], AT[:, n, :], mat("ident")))
            need(dve, tqk)
            tdt = V(dve.tensor_tensor(DT[:], B4[3], DT[:], ALU.mult))
            need(dve, ttk, t2)
            V(dve.tensor_tensor(kg[:], B4[0], heads4(eg), ALU.mult))
            tkd = V(dve.tensor_tensor(kdec[:], B4[0], heads4(ekd), ALU.mult))
            need(act, ttv)
            tv = A(act.copy(vt[:], B4[1]))
            yield
            ti = V(dve.tensor_copy(T[:], all_heads(mat("ident"))))
            need(dve, ta, tv)
            t = V(dve.tensor_tensor(Y[:], B4[2], heads4(be), ALU.mult))
            need(dve, t, ti)
            settle_dve(d)
            tt = V(dve.copy_predicated(T[:], all_heads(levels[:, d, 0, :]), Y[:]))
            for lv in range(1, len(LEVELS) + 1):
                need(pe, tt, tdt)
                tu = per_head(lambda n: pe.transpose(B[3][:, n * P:(n + 1) * P], T[:, n, :], mat("ident")))
                if lv < len(LEVELS):
                    need(pe, tkd)
                    ty = per_head(lambda n: pe.matmul(B[0][:, n * P:(n + 1) * P], AT[:, n, :], T[:, n, :],
                                                      start=True, stop=True))
                yield
                need(dve, tu)
                tu = V(dve.tensor_tensor(U[:], B4[3], heads4(be), ALU.mult))
                if lv == len(LEVELS):
                    break
                need(act, ty, tt)
                ty = A(act.copy(Y[:], B4[0]))
                yield
                need(pe, tu, ty, tv)
                t = per_head(lambda n: pe.matmul(B[1][:, n * P:(n + 1) * P], U[:, n, :], Y[:, n, :],
                                                 start=True, stop=True))
                yield
                need(dve, t)
                settle_dve(d)
                tt = V(dve.copy_predicated(T[:], all_heads(levels[:, d, lv, :]), B4[1]))
            need(pe, tu, tkd)
            t = per_head(lambda n: pe.matmul(B[0][:, n * P:(n + 1) * P], kg[:, n, :], U[:, n, :], start=True,
                                             stop=True))
            need(act, t)
            tkc = A(act.copy(KT[:], B4[0]))
            yield
            need(pe, tkc, tt)

            def v_new(n):
                out = B[1][:, n * P:(n + 1) * P]
                pe.matmul(out, U[:, n, :], vt[:, n, :], start=True, stop=False)
                return pe.matmul(out, KT[:, n, :], St[:, n, :], start=False, stop=True)
            t = per_head(v_new)
            need(act, t)
            tvn = A(act.copy(AT[:], B4[1]))
            yield
            need(pe, tvn, tq2)

            def out_(n):
                out = B[2][:, n * P:(n + 1) * P]
                pe.matmul(out, St[:, n, :], qd[:, n, :], start=True, stop=False)
                return pe.matmul(out, AT[:, n, :], DT[:, n, :], start=False, stop=True)
            t = per_head(out_)
            t2 = per_head(lambda n: pe.matmul(B[3][:, n * P:(n + 1) * P], kdec[:, n, :], AT[:, n, :], start=True,
                                              stop=True))
            yield
            need(dve, t)
            ov = o[:, :, bass.ds(at, P)]
            V(dve.tensor_tensor(ov, ov, B4[2], ALU.add))
            t = V(dve.tensor_tensor(St[:], St[:], heads4(et), ALU.mult))
            need(dve, t, t2)
            V(dve.tensor_tensor(St[:], St[:], B4[3], ALU.add))
            yield

        for d in range(2):
            V(dve.memset(bufs[d][10][:], 0.0))
        with C.loop("chunk", NT) as i:
            rendezvous()
            gens = [direction(0, i), direction(1, i)]
            live = True
            while live:
                live = False
                for g in gens:
                    if next(g, "end") != "end":
                        live = True
        rendezvous()
        mem.close()

    def finish():
        store_h()
        top.close()
        return C.found

    ffn("ffn1", "norm_ffn1")
    mixer()
    ffn("ffn2", "norm_ffn2")
    norm_h(lambda k: col("norm_final", k))
    wab = sb("wab", [P, N_LAYER, KD * 16])
    levels = sb("levels", [P, 2, len(LEVELS), P], U8)
    act.dma_start(wab[:], a["wab"].rearrange("l p k n -> p l (k n)")).then_inc(s_lpar, 16)
    with ExitStack() as mem:
        masks = sb("levels_f", [P, 2, len(LEVELS), P], ctx=mem)
        act.dma_start(masks[:], a["levels"]).then_inc(s_lpar, 16)
        for eng in (pe, act, dve, pool):
            eng.wait_ge(s_lpar, 112)
        V(dve.tensor_copy(levels[:], masks[:]))
        rendezvous()
    with C.loop("layer", N_LAYER) as l:
        layer(l, wab, levels)
    norm_h(lambda k: col("final2", k))
    return finish()


def build(nc, a):
    steps = {}
    for _ in range(6):
        scratch = a["fresh"]()
        found = program(scratch[0], scratch[1], steps)
        if found == steps:
            break
        steps = found
    assert program(nc, a, steps) == steps


def layout(x):
    f = np.float32

    def proj(w):
        k, n = w.shape
        return w.reshape(k // P, P, n // P, P).transpose(2, 1, 0, 3).reshape(n // P, P, k)

    def down(w):
        return w.reshape(w.shape[0] // P, P, D)

    def pairs(*ws):
        return np.stack(ws, 1).reshape(-1, P, ws[0].shape[-1])

    def ffn(g, u, d):
        return [pairs(proj(g), proj(u)), down(d)]

    units = ffn(x["ffn1_gate"][0], x["ffn1_up"][0], x["ffn1_down"][0])
    w = x["w_in"][0]
    widths = (512, 128, 128, 128, 128, 128, 128, 24, 512, 64, 64, 1024, 1024)
    nq, kc, vc, ksl, vsl, kwn, vwn, ng, sq, sk, sv, ga, gb = np.split(w, np.cumsum(widths)[:-1], axis=1)
    both = np.concatenate([sv, ng, sv[:, :40]], 1)
    units += [proj(nq), proj(sq), proj(ksl), proj(kwn), proj(np.concatenate([sk, sk], 1)), proj(kc), proj(vc),
              proj(vsl), proj(vwn), proj(both)]
    ab = np.concatenate([proj(x["w_branch_a"][0]), proj(x["w_branch_b"][0])], 2)
    units += [pairs(proj(ga), proj(gb), ab), proj(x["w_out"][0])]
    units += ffn(x["ffn2_gate"][0], x["ffn2_up"][0], x["ffn2_down"][0])
    wab = []
    for l in range(N_LAYER):
        w = x["w_in_2"][l]
        qkv, za, al, bl, val, glu, zb, gt = np.split(w, np.cumsum((1536, 512, 8, 8, 512, 512, 512)), axis=1)
        wab.append(np.concatenate([al, bl], 1).reshape(KD, P, 16).transpose(1, 0, 2))
        g = gt.reshape(D, 2, D)
        out = np.concatenate([proj(x["w_dn_out_2"][l]), proj(x["w_cf_out_2"][l])], 2)
        units += [pairs(proj(glu), proj(val)), proj(za), proj(zb), proj(qkv),
                  pairs(proj(g[:, 0]), proj(g[:, 1]), out), proj(x["w_out_2"][l])]
    stream = np.concatenate(units)
    assert stream.shape == (N_UNITS, P, UNIT), stream.shape
    stream = np.concatenate([stream, stream[:SPARE]])

    def c(v):
        return np.asarray(v).reshape(-1, P).T

    def wide(v):
        return np.broadcast_to(np.asarray(v).reshape(1, -1), (P, np.asarray(v).size))

    def pe2(v):
        return v.reshape(16, 2 * HD).T

    half = HD // 2
    inv = (np.float32(10000.0) ** (-np.arange(half, dtype=f) / f(half))).astype(f)
    parts = {"norm_ffn1": c(x["norm_ffn1"][0]), "norm_mix": c(x["norm_mix"][0]), "norm_ffn2": c(x["norm_ffn2"][0]),
             "norm_final": c(x["norm_final"]), "final2": c(x["final_norm_w_2"]), "sinks": wide(x["swa_sinks"][0]),
             "pe_k": pe2(x["cmp_pe_k"][0]), "pe_v": pe2(x["cmp_pe_v"][0]), "inv_freq": np.tile(inv, 4).reshape(P, 1)}
    cols = np.concatenate([parts[n] for n in COLS], 1).astype(f)
    lc = []
    for l in range(N_LAYER):
        parts = {"norm": c(x["norm_w_2"][l]),
                 "qkv_w": x["qkv_conv_w_2"][l].reshape(QKV_TAPS, 12, P).transpose(2, 1, 0).reshape(P, -1),
                 "cf_w": x["cf_conv_w_2"][l].reshape(CF_TAPS, 4, P).transpose(2, 1, 0).reshape(P, -1),
                 "cf_b": c(x["cf_conv_b_2"][l]), "ln_w": c(x["cf_ln_w_2"][l]), "ln_b": c(x["cf_ln_b_2"][l]),
                 "gate_b": c(x["gate_b_2"][l]), "dn_w": c(x["dn_norm_w_2"][l]),
                 "a_log": wide(x["a_log_2"][l]), "dt_bias": wide(x["dt_bias_2"][l])}
        lc.append(np.concatenate([parts[n] for n in LCOLS], 1))
    i = np.arange(P)
    rot = np.zeros((P, P), f)
    for m in range(P):
        if m % HD < half:
            rot[m + half, m] = -1
        else:
            rot[m - half, m] = 1
    m = {"ident": np.eye(P), "ones": np.ones((P, P)), "rot": rot,
         "tri_f": i[:, None] <= i[None, :], "tri_b": i[:, None] >= i[None, :],
         "negstrict_f": -1.0 * (i[:, None] < i[None, :]), "negstrict_b": -1.0 * (i[:, None] > i[None, :])}
    mats = np.stack([m[n] for n in MATS], 1).astype(f)
    lev = []
    for b in LEVELS:
        blk = i // b
        sib = (blk[:, None] // 2 == blk[None, :] // 2)
        lev.append(sib & (blk[:, None] > blk[None, :]))
    lev = np.stack(lev, 1)
    levels = np.stack([lev, lev.transpose(2, 1, 0)], 1).astype(f)
    q, s = i[:, None], i[None, :]
    causal = np.where(s > q, NEG, 0.0)
    s = np.arange(2 * P)[None, :]
    band = np.where((s - P <= q) & (s > q), 0.0, NEG)
    t = np.arange(S).reshape(NT, P).T[:, :, None]
    n = np.arange(32)[None, None, :]
    vis = np.where((16 * n + 31 <= t) & (n < CMP_N), 0.0, NEG).reshape(P, -1)
    valid = (np.arange(S).reshape(NT, P).T >= 31) * 1.0
    masks = np.concatenate([causal, band, vis, valid], 1).astype(f)
    w1 = [x[n][0].reshape(16, P, 2 * P).transpose(1, 0, 2) for n in ("cmp_k_w1", "cmp_v_w1")]
    w2 = [x[n][0].reshape(2, P, HD).transpose(1, 0, 2) for n in ("cmp_k_w2", "cmp_v_w2")]
    w2k = np.concatenate([w2[0], w2[0]], 2)
    ca = np.ascontiguousarray
    return {"stream": ca(stream), "xT": ca(x["x"][0].T.reshape(KD, P, S).transpose(1, 0, 2)), "cols": ca(cols),
            "lcols": ca(np.stack(lc, 1)), "mats": ca(mats), "levels": ca(levels), "masks": ca(masks),
            "w1": ca(np.stack(w1)), "w2k": ca(w2k), "w2v": ca(w2[1]), "wab": ca(np.stack(wab)),
            "pos": ca(np.tile(x["positions"].reshape(1, S), (P, 1)))}


def kernel(**inputs):
    import concourse.bacc as bacc
    from concourse.bass_utils import run_bass_kernel_spmd

    arrays = layout({k: np.asarray(v) for k, v in inputs.items()})

    def fresh():
        nc = bacc.Bacc("TRN2", target_bir_lowering=False, num_devices=1)
        a = {n: nc.dram_tensor("in_" + n, v.shape, mybir.dt.from_np(v.dtype), kind="ExternalInput").ap()
             for n, v in arrays.items()}
        a["outT"] = nc.dram_tensor("outT", (P, KD, S), F32, kind="ExternalOutput").ap()
        a["fresh"] = fresh
        return nc, a

    nc, a = fresh()
    build(nc, a)
    r = run_bass_kernel_spmd(nc, [{"in_" + n: v for n, v in arrays.items()}], core_ids=[0])
    out = r.results[0]["outT"]
    return np.ascontiguousarray(out.transpose(1, 0, 2).reshape(D, S).T).reshape(1, S, D)
```

```python
from contextlib import ExitStack, contextmanager

import numpy as np

import concourse.bass as bass
from concourse import mybir

F32 = mybir.dt.float32
F32R = mybir.dt.float32r
I32 = mybir.dt.int32
U8 = mybir.dt.uint8
ALU = mybir.AluOpType
ACT = mybir.ActivationFunctionType
AX = mybir.AxisListType

P = 128
S = 512
NT = S // P
D = 1024
KD = D // P
FF = 2816
NF = FF // P
HD = 64
EPS = 1e-6
NEG = -1e30
SCALE = HD ** -0.5
CMP_N = 31
DN_H = 4
CF_TAPS = 31
CF_PAD = CF_TAPS // 2
QKV_TAPS = 5
QKV_PAD = QKV_TAPS // 2
N_LAYER = 2

UNIT = 8 * P
RING = 4
AHEAD = 2
U_FFN = 3 * NF
U_MIX = 8 + 8 + 24 + 8
U_LAYER = 8 + 8 + 12 + 24 + 8
N_UNITS = 2 * U_FFN + U_MIX + N_LAYER * U_LAYER
SPARE = RING + AHEAD

COLS = {}
_at = 0
for _name, _n in (("norm_ffn1", 8), ("norm_mix", 8), ("norm_ffn2", 8), ("norm_final", 8), ("final2", 8),
                  ("sinks", 8), ("pe_k", 16), ("pe_v", 16), ("inv_freq", 1)):
    COLS[_name] = (_at, _n)
    _at += _n
N_COLS = _at
LCOLS = {}
_at = 0
for _name, _n in (("norm", 8), ("qkv_w", 12 * QKV_TAPS), ("cf_w", 4 * CF_TAPS), ("cf_b", 4), ("ln_w", 4),
                  ("ln_b", 4), ("gate_b", 16), ("dn_w", 1), ("a_log", 8), ("dt_bias", 8)):
    LCOLS[_name] = (_at, _n)
    _at += _n
N_LCOLS = _at
MATS = ["ident", "ones", "rot", "tri_f", "tri_b", "negstrict_f", "negstrict_b"]
LEVELS = [1, 2, 4, 8, 16, 32, 64]


class Lin:

    def __init__(self, const=0, terms=()):
        self.const, self.terms = const, tuple(terms)

    def add(self, n):
        return Lin(self.const + n, self.terms)

    def term(self, reg, n):
        return Lin(self.const, self.terms + ((reg, n),)) if n else self

    def value(self, div=1):
        v = self.const // div
        for reg, n in self.terms:
            assert n % div == 0
            v = reg * (n // div) + v
        return v


class Tok:

    def __init__(self, key, lin):
        self.key, self.lin = key, lin


class Counter:

    BIAS = 256

    def __init__(self, nc, sems, steps):
        self.nc, self.sems, self.steps = nc, sems, steps
        self.count = {k: Lin(self.BIAS) for k in sems}
        self.count["unit"] = Lin(0)
        self.loops = []
        self.settle = None
        self.found = {}

    def inc(self, key, ins, n=1):
        ins.then_inc(self.sems[key], n)
        self.count[key] = self.count[key].add(n)
        return Tok(key, self.count[key])

    def wait(self, eng, *toks):
        for t in toks:
            if t is not None:
                assert t.lin.const >= 0, (t.key, t.lin.const)
                eng.wait_ge(self.sems[t.key], t.lin.value())

    def now(self, *keys):
        return [Tok(k, self.count[k]) for k in keys]

    def mark(self, name, tok):
        start = self.loops[-1][1]
        self.loops[-1][2][name] = (tok.key, tok.lin.const - start[tok.key].const)

    def prev(self, name):
        loop, start, _, reg = self.loops[-1]
        key, off = self.steps.get(loop, {}).get("marks", {}).get(name, ("pe", 0))
        per = self.steps.get(loop, {}).get("per", {}).get(key, 0)
        return Tok(key, start[key].add(off - per).term(reg, per))

    @contextmanager
    def loop(self, name, n):
        per = self.steps.get(name, {}).get("per", {})
        start = dict(self.count)
        if self.loops:
            self.settle()
            start = dict(self.count)
        with self.nc.Fori(0, n) as reg:
            self.count = {k: c.term(reg, per.get(k, 0)) for k, c in start.items()}
            marks = {}
            self.loops.append((name, start, marks, reg))
            yield reg
            self.loops.pop()
            self.found[name] = {
                "per": {k: c.const - start[k].const for k, c in self.count.items()}, "marks": marks}
        self.count = {k: c.add(n * per.get(k, 0)) for k, c in start.items()}


def program(nc, a, steps):
    pe, act, dve, pool, sp = nc.tensor, nc.scalar, nc.vector, nc.gpsimd, nc.sync
    top = ExitStack()

    def sb(name, shape, dt=F32, ctx=None, side=None):
        return (ctx or top).enter_context(nc.sbuf_tensor(name, shape, dt, side=side))

    names = ["pe", "act", "dve", "pool", "whi", "wlo", "used", "tab"]
    sems = {k: top.enter_context(nc.semaphore("s_" + k)) for k in names}
    landed = [top.enter_context(nc.semaphore(f"s_landed{i}")) for i in range(RING)]
    s_h = [top.enter_context(nc.semaphore(f"s_h{i}")) for i in range(4)]
    s_par = top.enter_context(nc.semaphore("s_par"))
    s_lpar = top.enter_context(nc.semaphore("s_lpar"))
    s_aux = top.enter_context(nc.semaphore("s_aux"))
    s_out = top.enter_context(nc.semaphore("s_out"))
    C = Counter(nc, sems, steps)
    bias_eng = {"pe": pe, "used": pe, "act": act, "whi": act, "dve": dve, "tab": dve, "pool": pool, "wlo": pool}
    for k in names:
        bias_eng[k].sem_inc(sems[k], C.BIAS)

    C.settle = lambda: settle_all()

    def PE(ins): return C.inc("pe", ins)
    def A(ins): return C.inc("act", ins)
    def V(ins): return C.inc("dve", ins)
    def G(ins): return C.inc("pool", ins)
    def need(eng, *toks): C.wait(eng, *toks)

    def settle_all():
        settle_pe()
        settle_dve(2)
        G(pool.tensor_tensor(epsc[:, 5:6], epsc[:, 0:1], epsc[:, 0:1], ALU.add))

    def settle_pe():
        pe.matmul(ps[:, 7, 0:2], mat("ident"), mats[:, 0, 0:2], start=True, stop=True)

    def settle_dve(n):
        V(dve.tensor_copy(epsc[:, 2 + n:3 + n], epsc[:, 0:1]))

    def settle_act(n):
        A(act.copy(epsc[:, 6 + n:7 + n], epsc[:, 0:1]))

    def rendezvous():
        for eng, own in ((pe, "pe"), (act, "act"), (dve, "dve"), (pool, "pool")):
            need(eng, *C.now(*[k for k in ("pe", "act", "dve", "pool", "used")]))

    h = sb("h", [P, KD, S])
    xh = sb("xh", [P, KD, S], F32R)
    xl = sb("xl", [P, KD, S], F32R)
    raw = sb("raw", [P, RING, UNIT])
    whi = sb("whi", [P, RING, UNIT], F32R)
    wlo = sb("wlo", [P, RING, UNIT], F32R)
    cols = sb("cols", [P, N_COLS])
    mats = sb("mats", [P, len(MATS), P])
    lcol = sb("lcol", [P, N_LCOLS])
    lcols = sb("lcols", [P, N_LAYER, N_LCOLS])
    rt = sb("rt", [P, 4, S])
    epsc = sb("epsc", [P, 8])
    scl = sb("scl", [P, 8 * NT])
    ps = top.enter_context(nc.psum_tensor("ps", [P, 8, S], F32))

    def col(name, i=0, n=1):
        return cols[:, COLS[name][0] + i:COLS[name][0] + i + n]

    def lcl(name, i=0, n=1):
        return lcol[:, LCOLS[name][0] + i:LCOLS[name][0] + i + n]

    def mat(name):
        return mats[:, MATS.index(name), :]

    for i in range(RING):
        sp.dma_start(raw[:, i, :], a["stream"][i]).then_inc(landed[i], 16)
    for j in range(4):
        act.dma_start(h[:, 2 * j:2 * j + 2, :], a["xT"][:, 2 * j:2 * j + 2, :]).then_inc(s_h[j], 16)
    act.dma_start(cols[:], a["cols"]).then_inc(s_par, 16)
    act.dma_start(mats[:], a["mats"]).then_inc(s_par, 16)
    act.dma_start(lcols[:], a["lcols"]).then_inc(s_par, 16)
    m_msk, m_mlp = ExitStack(), ExitStack()
    msk = sb("msk", [P, 3 * P + NT * 32 + NT], ctx=m_msk, side="right")
    cosT = sb("cosT", [P, S], ctx=m_mlp, side="right")
    sinT = sb("sinT", [P, S], ctx=m_mlp, side="right")
    w1k = sb("w1k", [P, 16, 2 * P], ctx=m_mlp, side="right")
    w2k = sb("w2k", [P, 2, P], ctx=m_mlp, side="right")
    w2v = sb("w2v", [P, 2, HD], ctx=m_mlp, side="right")
    wab = sb("wab", [P, N_LAYER, KD * 16])
    levels = sb("levels", [P, 2, len(LEVELS), P], U8)
    c0 = V(dve.memset(epsc[:, 0:1], EPS))
    c0 = V(dve.memset(epsc[:, 1:2], 1.0))
    for eng in (pe, act, dve, pool):
        eng.wait_ge(s_par, 48)
        need(eng, c0)

    def split_unit(unit):
        slot = unit.const % RING
        act.wait_ge(landed[slot], unit.add(RING).value(RING) * 16)
        need(act, Tok("used", unit.add(C.BIAS + 1 - RING)))
        C.inc("whi", act.copy(whi[:, slot, :], raw[:, slot, :]))
        hi = Tok("whi", unit.add(C.BIAS + 1))
        need(pool, hi)
        C.inc("wlo", pool.tensor_tensor(wlo[:, slot, :], raw[:, slot, :], whi[:, slot, :].bitcast(F32),
                                        ALU.subtract))
        need(sp, Tok("wlo", unit.add(C.BIAS + 1)))
        sp.dma_start(raw[:, slot, :], a["stream"][unit.add(RING).value()]).then_inc(landed[slot], 16)

    for i in range(AHEAD):
        split_unit(Lin(i))

    def stream(tiles):
        for done in stream_tiles(tiles):
            pass
        return done

    def stream_tiles(tiles):
        unit = C.count["unit"]
        split_unit(unit.add(AHEAD))
        slot = unit.const % RING
        need(pe, Tok("wlo", unit.add(C.BIAS + 1)))
        for t, (out, hi, lo, first, last, waits) in enumerate(tiles):
            need(pe, *waits)
            wh, wl = whi[:, slot, t * P:(t + 1) * P], wlo[:, slot, t * P:(t + 1) * P]
            m = out.shape[0]
            pe.matmul(out, wh[:, 0:m], hi, start=first, stop=False)
            pe.matmul(out, wh[:, 0:m], lo, start=False, stop=False)
            ins = pe.matmul(out, wl[:, 0:m], hi, start=False, stop=last)
            if t < len(tiles) - 1:
                yield None
        C.count["unit"] = unit.add(1)
        yield C.inc("used", ins)

    def stream_x(out, waits=(), ready=None):
        return stream(x_tiles(out, waits, ready))

    def x_tiles(out, waits=(), ready=None):
        return [(out, xh[:, k, :], xl[:, k, :], k == 0, k == KD - 1,
                 (list(waits) if k == 0 else []) + ([ready[k]] if ready else [])) for k in range(KD)]

    def token_sums(out, squares, first, last):
        for j in range(NT):
            ins = pe.matmul(out[:, j:j + 1], squares[:, j * P:(j + 1) * P], mat("ones")[:, 0:1],
                            start=first and j == 0, stop=last, skip_group_check=True)
        return PE(ins)

    def spread(out, colsum):
        for j in range(NT):
            ins = pe.matmul(out[:, j * P:(j + 1) * P], colsum[:, j:j + 1].broadcast_to([P, P]), mat("ident"),
                            start=True, stop=True)
        return PE(ins)

    def inverse_root(dst, sums, total):
        t = A(act.activation(dst, sums, ACT.Sqrt, bias=epsc[:, 0:1], scale=1.0 / total))
        need(dve, t)
        return V(dve.reciprocal(dst, dst))

    def rms_scale(arrived=None):
        sums = []
        for k in range(KD):
            need(act, sums[k - 4] if k >= 4 else None)
            if arrived and k % 2 == 0:
                act.wait_ge(arrived[k // 2], 16)
            t = A(act.activation(rt[:, k % 4, :], h[:, k, :], ACT.Square))
            need(pe, t)
            sums.append(token_sums(ps[:, 6, 0:NT], rt[:, k % 4, :], k == 0, k == KD - 1))
        need(act, sums[-1])
        t = inverse_root(scl[:, 0:NT], ps[:, 6, 0:NT], D)
        need(pe, t)
        return spread(ps[:, 5, :], scl[:, 0:NT])

    def norm_to_x(gain, beside=None, arrived=None):
        rendezvous()
        if beside:
            beside()
        need(dve, rms_scale(arrived))
        lo, ready = [], []
        for k in range(KD):
            need(dve, lo[k - 4] if k >= 4 else None)
            y = V(dve.scalar_tensor_tensor(out=rt[:, k % 4, :], in0=h[:, k, :], scalar=gain(k),
                                           in1=ps[:, 5, :], op0=ALU.mult, op1=ALU.mult))
            need(act, y)
            hi = A(act.copy(xh[:, k, :], rt[:, k % 4, :]))
            eng, note = (dve, V) if k % 2 == 0 else (pool, G)
            need(eng, hi)
            lo.append(note(eng.tensor_tensor(xl[:, k, :], rt[:, k % 4, :], xh[:, k, :].bitcast(F32),
                                             ALU.subtract)))
            ready.append(lo[-1])
        return ready

    def split_into(hi, lo, srcs):
        for k, src in enumerate(srcs):
            t = A(act.copy(hi[:, k, :], src))
            need(dve, t)
            V(dve.tensor_tensor(lo[:, k, :], src, hi[:, k, :].bitcast(F32), ALU.subtract))

    def ffn(name, gain, arrived=None, beside=None):
        ready = norm_to_x(lambda k: col(gain, k), arrived=arrived)
        with ExitStack() as mem:
            mid = sb(name + "_mid", [P, NF, S], ctx=mem)
            sil = sb(name + "_sil", [P, 2, S], ctx=mem)
            mh = sb(name + "_mh", [P, 2, S], F32R, ctx=mem)
            ml = sb(name + "_ml", [P, 2, S], F32R, ctx=mem)
            last = None
            if beside:
                beside(mid)
            with C.loop(name + "_up", NF // 2) as i:
                for s in range(2):
                    g, u = ps[:, 2 * s, :], ps[:, 2 * s + 1, :]
                    free = C.prev(f"mid{s}")
                    tg = stream_x(g, [free], ready if s == 0 else None)
                    need(act, tg, free)
                    ts = A(act.activation(sil[:, s, :], g, ACT.Silu))
                    tu = stream_x(u)
                    need(dve, ts, tu)
                    last = V(dve.tensor_tensor(mid[:, i * 2 + s, :], sil[:, s, :], u, ALU.mult))
                    C.mark(f"mid{s}", last)
            rendezvous()

            def down(f, s, first, last_f, free):
                need(act, free)
                hi = A(act.copy(mh[:, s, :], mid[:, f, :]))
                need(dve, hi)
                lo = V(dve.tensor_tensor(ml[:, s, :], mid[:, f, :], mh[:, s, :].bitcast(F32), ALU.subtract))
                return stream([(ps[:, d, :], mh[:, s, :], ml[:, s, :], first, last_f, [lo] if d == 0 else [])
                               for d in range(KD)])

            down(0, 0, True, False, None)
            down(1, 1, False, False, None)
            with C.loop(name + "_down", (NF - 6) // 4) as i:
                t = []
                for s in range(4):
                    free = C.prev(f"u{s + 2}") if s < 2 else t[s - 2]
                    t.append(down(i * 4 + 2 + s, s % 2, False, False, free))
                    C.mark(f"u{s}", t[-1])
            used = C.count["used"]
            t = [Tok("used", used.add(-1)), Tok("used", used)]
            for s in range(4):
                t.append(down(NF - 4 + s, s % 2, False, s == 3, t[s]))
            done = C.now("used")
            for d in range(KD):
                need(dve, *done)
                V(dve.scalar_tensor_tensor(out=h[:, d, :], in0=ps[:, d, :], scalar=0.5, in1=h[:, d, :],
                                           op0=ALU.mult, op1=ALU.add))
            rendezvous()

    def store_h():
        rendezvous()
        need(sp, *C.now("pe", "act", "dve", "pool"))
        sp.dma_start(a["outT"], h[:]).then_inc(s_out, 16)
        sp.wait_ge(s_out, 16)
        for i in range(RING):
            sp.wait_ge(landed[i], 16 * ((C.count["unit"].const + SPARE - 1 - i) // RING + 1))

    def early(mid):
        flat = mid[:].rearrange("p f s -> p (f s)")
        n_lev = 2 * len(LEVELS) * P
        levels_f = flat[:, NF * S - n_lev:NF * S].rearrange("p (d l n) -> p d l n", d=2, l=len(LEVELS))
        tmp = mid[:, 12:16, :]
        posi = tmp[:, 0, :].bitcast(I32)
        sp.dma_start(posi, a["pos"]).then_inc(s_aux, 16)
        sp.dma_start(levels_f, a["levels"]).then_inc(s_aux, 16)
        sp.dma_start(msk[:], a["masks"]).then_inc(s_lpar, 16)
        sp.dma_start(w2k[:], a["w2k"]).then_inc(s_lpar, 16)
        sp.dma_start(w2v[:], a["w2v"]).then_inc(s_lpar, 16)
        sp.dma_start(wab[:], a["wab"].rearrange("l p k n -> p l (k n)")).then_inc(s_lpar, 16)
        sp.dma_start(w1k[:], a["w1"][0]).then_inc(s_lpar, 16)
        dve.wait_ge(s_aux, 32)
        C.inc("tab", dve.tensor_copy(levels[:], levels_f))
        rope_tables(cosT[:], sinT[:], tmp)
        need(dve, *C.now("act", "tab"))

    def rope_tables(cosT, sinT, tmp):
        posi = tmp[:, 0, :].bitcast(I32)
        t = C.inc("tab", dve.tensor_copy(tmp[:, 1, :], posi))
        need(dve, t)
        t = C.inc("tab", dve.tensor_scalar(tmp[:, 1, :], tmp[:, 1, :], col("inv_freq"), None, ALU.mult))
        need(dve, t)
        two_pi = 2 * np.pi
        c1 = float(np.float32(6.28125))
        c2 = float(np.float32(two_pi - c1))
        c3 = float(np.float32(two_pi - c1 - float(np.float32(c2))))
        magic = 1.5 * 2.0 ** 23
        for out, shift in ((sinT, 0.0), (cosT, 0.25)):
            t = C.inc("tab", dve.tensor_scalar(tmp[:, 2, :], tmp[:, 1, :], 1 / two_pi, shift, ALU.mult, ALU.add))
            need(dve, t)
            t = C.inc("tab", dve.tensor_scalar(tmp[:, 2, :], tmp[:, 2, :], magic, -magic, ALU.add, ALU.add))
            need(dve, t)
            src = tmp[:, 1, :]
            for cc in (c1, c2, c3):
                t = C.inc("tab", dve.scalar_tensor_tensor(out=tmp[:, 3, :], in0=tmp[:, 2, :], scalar=-cc, in1=src,
                                               op0=ALU.mult, op1=ALU.add))
                need(dve, t)
                src = tmp[:, 3, :]
            t = C.inc("tab", dve.tensor_scalar(tmp[:, 3, :], tmp[:, 3, :], shift * two_pi, float(np.float32(np.pi)),
                                    ALU.add, ALU.min))
            need(dve, t)
            t = C.inc("tab", dve.tensor_scalar(tmp[:, 3, :], tmp[:, 3, :], -float(np.float32(np.pi)), None, ALU.max))
            need(act, t)
            t = A(act.activation(out, tmp[:, 3, :], ACT.Sin))
            need(dve, t)

    def mixer():
        ready = norm_to_x(lambda k: col("norm_mix", k))
        need(dve, *C.now("tab"))
        need(pe, *C.now("tab"))
        mem = ExitStack()
        qall = sb("qall", [P, 8, S], ctx=mem)
        m_att = ExitStack()
        kd = sb("kd", [P, 5, S], ctx=m_att)
        kcc = sb("kcc", [P, 2, 32], ctx=m_att)
        vcc = sb("vcc", [32, 2, HD], ctx=m_att)
        vtok = sb("vtok", [P, NT, 2, P], ctx=m_att)
        vsw = sb("vsw", [P, NT, P], ctx=m_att)
        gts = sb("gts", [P, NT, 24], ctx=m_att)
        causal, band = msk[:, 0:P], msk[:, P:3 * P]
        vis = msk[:, 3 * P:3 * P + NT * 32].rearrange("p (t n) -> p t n", t=NT)
        valid = msk[:, 3 * P + NT * 32:]
        m_prj = ExitStack()
        w1v = sb("w1v", [P, 16, 2 * P], ctx=m_prj)
        kc2 = sb("kc2", [P, 2, 2, S // 2], ctx=m_prj)
        blk = sb("blk", [P, 16, 2, 32], ctx=m_prj)
        hid = sb("hid", [P, 2, 64], ctx=m_prj)
        hid2 = sb("hid2", [P, 2, 64], ctx=m_prj)
        hid3 = sb("hid3", [P, 2, 64], ctx=m_prj)
        xr = sb("xr", [P, 2, S], ctx=m_prj)
        tmp = sb("tmpp", [P, 4, S], ctx=m_prj)
        act.dma_start(w1v[:], a["w1"][1]).then_inc(s_lpar, 16)

        def rope(src, out, s, freed):
            t = A(act.copy(xr[:, s, :], src))
            need(pe, t, freed)
            r = PE(pe.matmul(ps[:, 4 + s, :], mat("rot"), xr[:, s, :], start=True, stop=True))
            need(dve, t, freed)
            t1 = V(dve.tensor_tensor(tmp[:, 2 * s, :], xr[:, s, :], cosT[:], ALU.mult))
            need(dve, r)
            t2 = V(dve.tensor_tensor(tmp[:, 2 * s + 1, :], ps[:, 4 + s, :], sinT[:], ALU.mult))
            need(dve, t1, t2)
            return out(tmp[:, 2 * s, :], tmp[:, 2 * s + 1, :])

        with C.loop("q_proj", 2) as i:
            done = []
            for s in range(4):
                free = C.prev(f"q{s}")
                t = stream_x(ps[:, s, :], [free], ready if s == 0 else None)
                need(act, t, done[s - 2] if s >= 2 else C.prev(f"q{s + 2}"))
                done.append(rope(ps[:, s, :], lambda x, y: V(dve.tensor_tensor(
                    qall[:, i * 4 + s, :], x, y, ALU.add)), s % 2, done[s - 2] if s >= 2 else C.prev(f"q{s + 2}")))
                C.mark(f"q{s}", done[-1])
        rendezvous()
        done = []
        for s in range(3):
            t = stream_x(ps[:, s, :])
            free = done[s - 2] if s >= 2 else None
            need(act, t, free)

            def out(x, y, s=s):
                if s == 2:
                    return V(dve.tensor_tensor(kd[:, 4, :], x, y, ALU.add))
                for g in range(2):
                    for half in range(2):
                        t = V(dve.tensor_tensor(kd[64 * half:64 * half + 64, 2 * s + g, :],
                                                x[64 * g:64 * g + 64, :], y[64 * g:64 * g + 64, :], ALU.add))
                return t
            done.append(rope(ps[:, s, :], out, s % 2, free))
        for s in range(2):
            t = stream_x(ps[:, 3 * (1 - s), :], [done[0]] if s else [])
            need(act, t)
            for g in range(2):
                for par in range(2):
                    A(act.copy(kc2[64 * par:64 * par + 64, s, g, :],
                               ps[64 * g:64 * g + 64, 3 * (1 - s), par:S:2]))
        kc_ready = C.now("act")
        for s in range(3):
            t = stream_x(ps[:, 1 + s, :], [done[1 if s == 0 else 2]] + kc_ready)
            need(act, t, *done, *C.now("pe"))
            t = A(act.copy(xr[:, s % 2, :], ps[:, 1 + s, :]))
            need(pe, t, *C.now("act", "dve"))
            for j in range(NT):
                t = PE(pe.transpose(ps[:, 4 + s, j * P:(j + 1) * P], xr[:, s % 2, j * P:(j + 1) * P], mat("ident")))
            need(act, t)
            pt = ps[:, 4 + s, :].rearrange("p (j c) -> p j c", j=NT)
            A(act.copy(vtok[:, :, s, :] if s < 2 else vsw[:], pt))
        for eng in (pe, act, dve, pool):
            eng.wait_ge(s_lpar, 96)
        need(act, *C.now("act"))
        t = A(act.activation(gts[:], vsw[:, :, HD:HD + 24], ACT.Sigmoid))
        need(dve, t)
        for j in range(NT):
            V(dve.tensor_scalar(gts[:, j, 0:8], gts[:, j, 0:8], valid[:, j:j + 1], None, ALU.mult))

        for w, w1 in enumerate((w1k, w1v)):
            need(dve, *C.now("act", "pe"))
            for g in range(2):
                for lp in range(16):
                    V(dve.tensor_scalar(blk[:, lp, g, 0:CMP_N], kc2[:, w, g, lp:lp + 8 * (CMP_N - 1) + 1:8],
                                        col("pe_k" if w == 0 else "pe_v", lp), None, ALU.add))
            need(pe, *C.now("dve", "act"))
            for m in range(2):
                for lp in range(16):
                    ins = pe.matmul(ps[:, 7, m * 64:m * 64 + 62], w1[:, lp, m * P:(m + 1) * P],
                                    blk[:, lp, :, 0:CMP_N], start=lp == 0, stop=lp == 15)
                t = PE(ins)
            z = ps[:, 7, 0:128].rearrange("p (m n) -> p m n", m=2)[:, :, 0:62]
            x1, x2, x3 = hid[:, :, 0:62], hid2[:, :, 0:62], hid3[:, :, 0:62]
            need(act, t)
            t = A(act.copy(x1, z))
            need(dve, t)
            t = V(dve.tensor_tensor(x2, x1, x1, ALU.mult))
            need(dve, t)
            t = V(dve.tensor_scalar(x2, x2, 0.044715, 1.0, ALU.mult, ALU.add))
            need(dve, t)
            t = V(dve.tensor_tensor(x2, x2, x1, ALU.mult))
            need(act, t)
            t = A(act.activation(x3, x2, ACT.Tanh, scale=float(np.sqrt(2 / np.pi))))
            need(dve, t)
            t = V(dve.tensor_scalar(x3, x3, 0.5, 0.5, ALU.mult, ALU.add))
            need(dve, t)
            t = V(dve.tensor_tensor(x1, x3, x1, ALU.mult))
            need(pe, t)
            if w == 0:
                for m in range(2):
                    ins = pe.matmul(ps[:, 6, 0:62], w2k[:, m, :], hid[:, m, 0:62], start=m == 0, stop=m == 1)
                t = PE(ins)
                need(act, t)
                t = A(act.copy(xr[:, 0, 0:62], ps[:, 6, 0:62]))
                need(pe, t)
                r = PE(pe.matmul(ps[:, 6, 64:126], mat("rot"), xr[:, 0, 0:62], start=True, stop=True))
                need(dve, r)
                for g in range(2):
                    o = 31 * g
                    t1 = V(dve.tensor_tensor(tmp[:, 0, o:o + 31], xr[:, 0, o:o + 31], cosT[:, 31:S:16], ALU.mult))
                    t2 = V(dve.tensor_tensor(tmp[:, 1, o:o + 31], ps[:, 6, 64 + o:64 + o + 31],
                                             sinT[:, 31:S:16], ALU.mult))
                    need(dve, t1, t2)
                    V(dve.tensor_tensor(kcc[:, g, 0:31], tmp[:, 0, o:o + 31], tmp[:, 1, o:o + 31], ALU.add))
            else:
                for g in range(2):
                    for m in range(2):
                        ins = pe.matmul(ps[0:31, 5 - g, 0:HD], hid[:, m, 31 * g:31 * g + 31],
                                        w2v[:, m, :], start=m == 0, stop=m == 1)
                    t = PE(ins)
                    need(act, t)
                    A(act.copy(vcc[0:31, g, :], ps[0:31, 5 - g, 0:HD]))
        rendezvous()
        m_prj.close()
        m_mlp.close()
        m_gates = ExitStack()
        gates = sb("gates", [P, 2 * KD, S], ctx=m_gates, side="right")
        pr = sb("pr", [P, 2, 2 * S], ctx=m_att)
        pt = sb("pt", [P, 2, 2, S], ctx=m_att)
        ptc = sb("ptc", [32, 2, S], ctx=m_att)
        ce = sb("ce", [P, 2, 2, NT, 32], ctx=m_att)
        cst = sb("cst", [P, 3, 4 * NT], ctx=m_att)
        qS, kS = (rt[:, 0, :], rt[:, 3, :]), rt[:, 1:3, :]
        kcS = sb("kcS", [P, 32], ctx=m_att)
        vS = sb("vS", [P, NT, 2, HD], ctx=m_att)
        vcS = sb("vcS", [32, HD], ctx=m_att)
        gS = sb("gS", [P, 2, NT, 3, 2], ctx=m_att)
        skS = sb("skS", [P, 4], ctx=m_att)
        st = sb("st", [P, 2, 5, 4], ctx=m_att)

        def two_pairs(nsa, chunk):
            steps_ = [(pair, hh, i) for pair in range(2) for hh in range(2) for i in range(NT)]
            n_steps = len(steps_)
            nb = 2 if nsa else 1
            scored, expd, probs, turned, evacd, pved = {}, {}, {}, {}, {}, {}
            bank4 = C.now("dve", "act")

            def gate_tiles():
                free = bank4
                for n in range(4):
                    for t in stream_tiles(x_tiles(ps[:, 4, :], free)):
                        if t is None:
                            yield
                    need(act, t)
                    settle_act(0)
                    free = [A(act.copy(gates[:, chunk * 2 + n, :], ps[:, 4, :]))]
                    yield
            filler = gate_tiles()

            def fill(n):
                for _ in range(n):
                    next(filler, None)

            def spans(i):
                return (0, i + 1) if nsa else (max(i - 1, 0), i + 1)

            def score(n):
                pair, hh, i = steps_[n]
                b, p = 64 * hh, n % 2
                j0, j1 = spans(i)
                if n >= 2:
                    need(pe, expd[n - 2])
                q = qS[pair][b:b + 64, i * P:(i + 1) * P]
                for br in range(nb):
                    ins = pe.matmul(ps[:, 2 * p + br, 0:(j1 - j0) * P], q, kS[b:b + 64, br, j0 * P:j1 * P],
                                    start=True, stop=True)
                scored[n] = PE(ins)

            def exponents(n):
                pair, hh, i = steps_[n]
                p = n % 2
                j0, j1 = spans(i)
                w = (j1 - j0) * P
                sk = skS[:, 2 * pair + hh:2 * pair + hh + 1]
                if n >= 2:
                    need(dve, probs[n - 2])
                    need(act, turned[n - 2])
                need(dve, scored[n])
                if nsa:
                    banks = ps[:, 2 * p:2 * p + 2, :]
                    last = banks[:, :, w - P:w]
                    mask = causal.unsqueeze(1).broadcast_to([P, 2, P])
                else:
                    banks = ps[:, 2 * p:2 * p + 1, :]
                    last = banks[:, 0, 0:w]
                    mask = band[:, 2 * P - w:]
                mx, nm, sm = (st[:, p, r, :] for r in range(3))
                t = V(dve.tensor_tensor(last, last, mask, ALU.add))
                need(dve, t)
                t = V(dve.tensor_reduce(mx[:, 0:nb], banks[:, :, 0:w], AX.X, ALU.max))
                need(dve, t)
                if nsa:
                    t = V(dve.tensor_scalar(nm[:, 0:nb], mx[:, 0:nb], -SCALE, None, ALU.mult))
                else:
                    t = V(dve.tensor_scalar(mx[:, 1:2], mx[:, 0:1], SCALE, sk, ALU.mult, ALU.max))
                    need(dve, t)
                    t = V(dve.tensor_scalar(nm[:, 0:1], mx[:, 1:2], -1.0, None, ALU.mult))
                need(act, t)
                for br in range(nb):
                    t = A(act.activation(pr[:, p, br * S:br * S + w], ps[:, 2 * p + br, 0:w], ACT.Exp,
                                         bias=nm[:, br:br + 1], scale=SCALE, accum_out=sm[:, br:br + 1]))
                if not nsa:
                    t = A(act.activation(sm[:, 1:2], sk, ACT.Exp, bias=nm[:, 0:1]))
                expd[n] = t

            def weights(n):
                pair, hh, i = steps_[n]
                p = n % 2
                j0, j1 = spans(i)
                w = (j1 - j0) * P
                sm, rs, wt = (st[:, p, r, :] for r in range(2, 5))
                need(dve, expd[n])
                if not nsa:
                    t = V(dve.tensor_tensor(sm[:, 0:1], sm[:, 0:1], sm[:, 1:2], ALU.add))
                    need(dve, t)
                t = V(dve.reciprocal(rs[:, 0:nb], sm[:, 0:nb]))
                need(dve, t)
                if nsa:
                    t = V(dve.tensor_tensor(wt[:, 0:nb], rs[:, 0:nb], gS[:, pair, i, 0:2, hh], ALU.mult))
                    need(dve, t)
                for br in range(nb):
                    dst = pr[:, p, br * S:br * S + w]
                    sc = wt[:, br:br + 1] if nsa else rs[:, 0:1]
                    t = V(dve.tensor_scalar(dst, dst, sc, None, ALU.mult))
                probs[n] = t

            def turn(n):
                pair, hh, i = steps_[n]
                p = n % 2
                j0, j1 = spans(i)
                need(pe, probs[n])
                if n >= 1:
                    need(pe, *evacd[n - 1])
                for br in range(nb):
                    for j in range(j1 - j0):
                        ins = pe.transpose(ps[:, 5 + br, j * P:(j + 1) * P],
                                           pr[:, p, br * S + j * P:br * S + (j + 1) * P], mat("ident"))
                turned[n] = PE(ins)

            def evacuate(n):
                pair, hh, i = steps_[n]
                p = n % 2
                j0, j1 = spans(i)
                w = (j1 - j0) * P
                need(act, turned[n], pved.get(n - 2))
                evacd[n] = [A(act.copy(pt[:, p, 0, 0:w], ps[:, 5, 0:w]))]
                if nsa:
                    need(dve, turned[n], pved.get(n - 2))
                    evacd[n].append(V(dve.tensor_copy(pt[:, p, 1, 0:w], ps[:, 6, 0:w])))

            def apply(n, free):
                pair, hh, i = steps_[n]
                b, p = 64 * hh, n % 2
                j0, j1 = spans(i)
                need(pe, *evacd[n], *free)
                out = ps[b:b + 64, 7, i * P:(i + 1) * P]
                terms = [(vS[:, j0 + j, br, :], pt[:, p, br, j * P:(j + 1) * P])
                         for br in range(nb) for j in range(j1 - j0)]
                if nsa:
                    terms.append((vcS[0:31, :], ptc[0:31, hh, i * P:(i + 1) * P]))
                for k, (v, w) in enumerate(terms):
                    ins = pe.matmul(out, v, w, start=k == 0, stop=k == len(terms) - 1)
                pved[n] = PE(ins)

            def compressed_scores():
                for pair in range(2):
                    for hh in range(2):
                        for i in range(NT):
                            c = P * pair + 32 * i
                            ins = pe.matmul(ps[:, 4 + 3 * hh, c:c + CMP_N],
                                            qS[pair][64 * hh:64 * hh + 64, i * P:(i + 1) * P],
                                            kcS[64 * hh:64 * hh + 64, 0:CMP_N], start=True, stop=True)
                need(dve, PE(ins))
                for pair in range(2):
                    for hh in range(2):
                        src = ps[:, 4 + 3 * hh, P * pair:P * pair + P].rearrange("p (i n) -> p i n", i=NT)
                        t = V(dve.tensor_tensor(ce[:, pair, hh, :, 0:CMP_N], src[:, :, 0:CMP_N],
                                                vis[:, :, 0:CMP_N], ALU.add))
                return t

            def compressed_softmax(t):
                e = ce[:].rearrange("p c h i n -> p (c h i) n")[:, :, 0:CMP_N]
                bc = lambda r: cst[:, r, :].unsqueeze(2).broadcast_to([P, 4 * NT, CMP_N])
                need(dve, t)
                t = V(dve.tensor_reduce(cst[:, 0, :], e, AX.X, ALU.max))
                need(dve, t)
                t = V(dve.tensor_tensor(e, e, bc(0), ALU.subtract))
                need(act, t)
                t = A(act.activation(e, e, ACT.Exp, scale=SCALE))
                need(dve, t)
                t = V(dve.tensor_reduce(cst[:, 1, :], e, AX.X, ALU.add))
                need(dve, t)
                t = V(dve.reciprocal(cst[:, 2, :], cst[:, 1, :]))
                need(dve, t)
                for pair in range(2):
                    n = 2 * NT * pair
                    t = V(dve.tensor_tensor(cst[:, 1, n:n + 2 * NT].rearrange("p (h t) -> p h t", h=2),
                                            cst[:, 2, n:n + 2 * NT].rearrange("p (h t) -> p h t", h=2),
                                            gS[:, pair, :, 2, :].rearrange("p t h -> p h t"), ALU.mult))
                need(dve, t)
                return V(dve.tensor_tensor(e, e, bc(1), ALU.mult))

            def compressed_turn(pair, waits):
                need(pe, *waits)
                for hh in range(2):
                    for i in range(NT):
                        ins = pe.transpose(ps[0:31, 5 + hh, i * P:(i + 1) * P], ce[:, pair, hh, i, 0:CMP_N],
                                           mat("ident"))
                need(act, PE(ins))
                for hh in range(2):
                    t = A(act.copy(ptc[0:31, hh, :], ps[0:31, 5 + hh, :]))
                need(pe, t)

            if nsa:
                bank4 = [compressed_scores()]
            score(0)
            score(1)
            if nsa:
                t = compressed_softmax(bank4[0])
            exponents(0)
            exponents(1)
            weights(0)
            fill(8)
            if nsa:
                compressed_turn(0, [t])
            freed = []
            for n in range(n_steps):
                turn(n)
                if n + 2 < n_steps:
                    score(n + 2)
                evacuate(n)
                if n + 1 < n_steps:
                    weights(n + 1)
                if n + 2 < n_steps:
                    exponents(n + 2)
                fill(2 - n % 2)
                apply(n, freed)
                freed = []
                if n % 8 == 7:
                    pair = n // 8
                    need(act, pved[n])
                    settle_act(1)
                    freed = [A(act.copy(qall[:, chunk + pair, :], ps[:, 7, :]))]
                    if nsa and pair == 0:
                        compressed_turn(1, evacd[n])
            fill(36)

        gts_v = gts[:].rearrange("p t (b h) -> p t b h", b=3)
        vtok_v = vtok[:].rearrange("p t b (g d) -> p t b g d", g=2)
        with C.loop("nsa_group", 2) as g:
            rendezvous()
            for pair in range(2):
                A(act.copy(qS[pair], qall[:, g * 2 + pair, :]))
                for dst, br in ((2, 0), (0, 1), (1, 2)):
                    G(pool.tensor_copy(gS[:, pair, :, dst, :], gts_v[:, :, br, bass.ds(g * 4 + pair * 2, 2)]))
            V(dve.tensor_copy(kS[:, 0, :], kd[:, g, :]))
            V(dve.tensor_copy(kS[:, 1, :], kd[:, g + 2, :]))
            V(dve.tensor_copy(kcS[:, 0:CMP_N], kcc[:, g, 0:CMP_N]))
            V(dve.tensor_copy(vcS[0:31, :], vcc[0:31, g, :]))
            for br in range(2):
                V(dve.tensor_copy(vS[:, :, br, :], vtok_v[:, :, br, g, :]))
            rendezvous()
            two_pairs(True, g * 2)
        rendezvous()
        V(dve.tensor_copy(kS[:, 0, :], kd[:, 4, :]))
        V(dve.tensor_copy(vS[:, :, 0, :], vsw[:, :, 0:HD]))
        with C.loop("swa_pairs", 2) as c:
            rendezvous()
            for pair in range(2):
                A(act.copy(qS[pair], qall[:, c * 2 + 4 + pair, :]))
            V(dve.tensor_copy(skS[:], cols[:, bass.ds(c * 4 + COLS["sinks"][0], 4)]))
            rendezvous()
            two_pairs(False, c * 2 + 4)
        rendezvous()
        m_att.close()
        split_into(xh, xl, [qall[:, c, :] for c in range(8)])
        merge("m1", xh, xl, None, gates)
        m_gates.close()
        m_msk.close()
        mem.close()

    def merge(name, fh, fl, gate_b, gates=None):
        with ExitStack() as mem:
            if gates is None:
                yh_all = sb(name + "_yh", [P, KD, S], F32R, mem)
                yl_all = sb(name + "_yl", [P, KD, S], F32R, mem)
                gb = sb(name + "_gb", [P, 2, 4], ctx=mem)
                yh, yl = (lambda c: yh_all[:, c, :]), (lambda c: yl_all[:, c, :])
            else:
                g_r = gates[:].bitcast(F32R)
                yh, yl = (lambda c: g_r[:, c * 2, :]), (lambda c: g_r[:, c * 2 + 1, :])
            sg = sb(name + "_sg", [P, 2, 2, S], ctx=mem)
            ym = rt
            rendezvous()
            with C.loop(name + "_gate", 2) as i:
                if gate_b:
                    for r in range(2):
                        need(dve, *C.now("act"))
                        tb = V(dve.tensor_copy(gb[:, r, :], gate_b(r, i)))
                    need(act, tb)
                done = []
                for s in range(4):
                    p = s % 2
                    free = done[s - 2] if s >= 2 else C.prev(f"y{s + 2}")
                    bank = 4 * p
                    for r in range(2):
                        if gates is None:
                            need(act, stream_x(ps[:, bank + r, :], [free]))
                        need(act, free)
                        src = ps[:, bank + r, :] if gates is None else gates[:, i * 8 + 2 * s + r, :]
                        ts = A(act.activation(sg[:, p, r, :], src, ACT.Sigmoid,
                                              bias=gb[:, r, s:s + 1] if gate_b else 0.0))
                    tiles = [(ps[:, bank + 2 + r, :], fh[:, 4 * r + k, :], fl[:, 4 * r + k, :], k == 0, k == 3,
                              [free] if k == 0 else []) for r in range(2) for k in range(4)]
                    t = stream(tiles)
                    need(dve, ts, t)
                    t0 = V(dve.tensor_tensor(sg[:, p, 0, :], sg[:, p, 0, :], ps[:, bank + 2, :], ALU.mult))
                    t1 = V(dve.tensor_tensor(sg[:, p, 1, :], sg[:, p, 1, :], ps[:, bank + 3, :], ALU.mult))
                    need(dve, t0, t1)
                    t0 = V(dve.tensor_tensor(ym[:, p, :], sg[:, p, 0, :], sg[:, p, 1, :], ALU.add))
                    need(act, t0)
                    t = A(act.copy(yh(i * 4 + s), ym[:, p, :]))
                    need(dve, t)
                    done.append(V(dve.tensor_tensor(yl(i * 4 + s), ym[:, p, :], yh(i * 4 + s).bitcast(F32),
                                                    ALU.subtract)))
                    C.mark(f"y{s}", done[-1])
            rendezvous()
            with C.loop(name + "_out", 2) as i:
                for s in range(4):
                    t = stream([(ps[:, s, :], yh(k), yl(k), k == 0, k == KD - 1,
                                 [C.prev(f"h{s}")] if k == 0 else []) for k in range(KD)])
                    need(dve, t)
                    C.mark(f"h{s}", V(dve.tensor_tensor(h[:, i * 4 + s, :], h[:, i * 4 + s, :], ps[:, s, :],
                                                        ALU.add)))
            rendezvous()

    def norm_h(gain):
        rendezvous()
        need(dve, rms_scale())
        for k in range(KD):
            V(dve.scalar_tensor_tensor(out=h[:, k, :], in0=h[:, k, :], scalar=gain(k), in1=ps[:, 5, :],
                                       op0=ALU.mult, op1=ALU.mult))
        rendezvous()

    def chunk_sums(c, src, bank, deps=()):
        need(act, *deps)
        t = A(act.activation(rt[:, c % 4, :], src, ACT.Square))
        need(pe, t)
        return token_sums(ps[:, bank, c * NT:(c + 1) * NT], rt[:, c % 4, :], True, True)

    def heads4(row):
        return row.unsqueeze(2).broadcast_to([P, DN_H, P])

    def all_heads(m):
        return m.unsqueeze(1).broadcast_to([P, DN_H, P])

    def layer(l, wab, levels):
        keep, wide, m_prj = ExitStack(), ExitStack(), ExitStack()
        za = sb("za", [P, 4, S], ctx=keep)
        zb = sb("zb", [P, 4, S], ctx=keep)
        cu = sb("cu", [P, 4, S], ctx=keep)
        o = sb("o", [P, 4, S], ctx=keep)
        small = sb("small", [P, 10, NT, 8], ctx=keep)
        gl, bt = small[:, 8], small[:, 9]
        qkv = sb("qkv", [P, 12, S], ctx=wide, side="right")
        up = sb("up", [P, 4, S + 2 * CF_PAD], ctx=m_prj)
        cp = sb("cp", [P, 2, S + 2 * QKV_PAD], ctx=m_prj)
        acc = sb("acc", [P, 4, S], ctx=m_prj)
        ws = sb("ws", [P, KD, 16], ctx=m_prj)
        wabh = sb("wabh", [P, KD, 16], F32R, m_prj)
        wabl = sb("wabl", [P, KD, 16], F32R, m_prj)
        tap = sb("tap", [P, 4 * QKV_TAPS], ctx=m_prj)
        tap2 = sb("tap2", [P, 17], ctx=m_prj)

        def beside():
            t = G(pool.tensor_copy(lcol[:], lcols[:, l, :]))
            for pad, buf in ((CF_PAD, up), (QKV_PAD, cp)):
                G(pool.memset(buf[:, :, 0:pad], 0.0))
                G(pool.memset(buf[:, :, pad + S:], 0.0))
            wsrc = wab[:, l, :].rearrange("p (k n) -> p k n", k=KD)
            G(pool.tensor_copy(ws[:], wsrc))
            t = G(pool.tensor_copy(wabh[:], wsrc))
            need(pool, t)
            G(pool.tensor_tensor(wabl[:], ws[:], wabh[:].bitcast(F32), ALU.subtract))
            G(pool.memset(o[:], 0.0))
            for eng in (act, dve, pe):
                need(eng, *C.now("pool"))

        ready = norm_to_x(lambda k: lcl("norm", k), beside)

        with C.loop("glu", 2) as i:
            for s in range(2):
                free = C.prev(f"u{s}")
                tg = stream_x(ps[:, 2 * s, :], [free], ready if s == 0 else None)
                need(act, tg, free)
                ts = A(act.activation(acc[:, s, :], ps[:, 2 * s, :], ACT.Sigmoid))
                tv = stream_x(ps[:, 2 * s + 1, :])
                need(dve, ts, tv)
                C.mark(f"u{s}", V(dve.tensor_tensor(up[:, i * 2 + s, CF_PAD:CF_PAD + S], acc[:, s, :],
                                                    ps[:, 2 * s + 1, :], ALU.mult)))
        for j in range(NT):
            out = ps[:, 6, 16 * j:16 * j + 16]
            for k in range(KD):
                xa, xb = xh[:, k, j * P:(j + 1) * P], xl[:, k, j * P:(j + 1) * P]
                pe.matmul(out, xa, wabh[:, k, :], start=k == 0, stop=False)
                pe.matmul(out, xa, wabl[:, k, :], start=False, stop=False)
                ins = pe.matmul(out, xb, wabh[:, k, :], start=False, stop=k == KD - 1)
        ab_done = PE(ins)
        raw_ab = ps[:, 6, 0:16 * NT].rearrange("p (t n) -> p t n", t=NT)
        v = [small[:, n] for n in range(8)]
        tok8 = lambda c: c.unsqueeze(1).broadcast_to([P, NT, 8])
        need(act, ab_done)
        A(act.activation(bt, raw_ab[:, :, 8:16], ACT.Sigmoid))
        t = A(act.activation(v[7][:, 0, :], lcl("a_log", 0, 8), ACT.Exp))
        need(dve, t)
        chain = [
            lambda: V(dve.tensor_tensor(v[0], raw_ab[:, :, 0:8], tok8(lcl("dt_bias", 0, 8)), ALU.add)),
            lambda: V(dve.tensor_scalar(v[1], v[0], -1.0, None, ALU.mult)),
            lambda: V(dve.tensor_tensor(v[1], v[0], v[1], ALU.max)),
            lambda: A(act.activation(v[2], v[1], ACT.Exp, scale=-1.0)),
            lambda: V(dve.tensor_scalar(v[3], v[2], 1.0, None, ALU.add)),
            lambda: V(dve.tensor_scalar(v[4], v[3], -1.0, 1e-30, ALU.add, ALU.add)),
            lambda: V(dve.reciprocal(v[4], v[4])),
            lambda: A(act.activation(v[5], v[3], ACT.Ln)),
            lambda: V(dve.scalar_tensor_tensor(out=v[5], in0=v[5], scalar=1e-30, in1=v[4], op0=ALU.add,
                                               op1=ALU.mult)),
            lambda: V(dve.tensor_tensor(v[5], v[5], v[2], ALU.mult)),
            lambda: V(dve.scalar_tensor_tensor(out=v[5], in0=v[0], scalar=0.0, in1=v[5], op0=ALU.max, op1=ALU.add)),
            lambda: V(dve.scalar_tensor_tensor(out=gl, in0=v[5], scalar=-1.0, in1=tok8(v[7][:, 0, :]), op0=ALU.mult,
                                               op1=ALU.mult)),
        ]
        for f in chain:
            t = f()
            need(act, t)
            need(dve, t)

        last = {}

        def cf_tap(c, k, w=None, bias=None):
            src, dst, w = up[:, c, k:k + S], cu[:, c, :], lcl("cf_w", CF_TAPS * c + k) if w is None else w
            need(dve, last.get("cf"))
            if k == 0:
                t = V(dve.tensor_scalar(dst, src, w, lcl("cf_b", c) if bias is None else bias, ALU.mult, ALU.add))
            else:
                t = V(dve.scalar_tensor_tensor(out=dst, in0=src, scalar=w, in1=dst, op0=ALU.mult, op1=ALU.add))
            last["cf"] = t

        need(pe, *C.now("dve"))
        with C.loop("qkv", 3) as i:
            need(dve, *C.now("act", "dve"))
            V(dve.tensor_copy(tap[:, 0:4 * QKV_TAPS],
                              lcol[:, bass.ds(i * (4 * QKV_TAPS) + LCOLS["qkv_w"][0], 4 * QKV_TAPS)]))
            V(dve.tensor_copy(tap2[:, 0:16], lcol[:, bass.ds(i * CF_TAPS + LCOLS["cf_w"][0], 16)]))
            tw = V(dve.tensor_copy(tap2[:, 16:17], lcol[:, bass.ds(i + LCOLS["cf_b"][0], 1)]))
            need(dve, tw)
            last.clear()
            conv, outs = [], []
            for s in range(4):
                p = s % 2
                t = stream_x(ps[:, s, :], [C.prev(f"cp{s}")])
                need(act, t, conv[s - 2] if s >= 2 else C.prev(f"conv{s + 2}"))
                t = A(act.copy(cp[:, p, QKV_PAD:QKV_PAD + S], ps[:, s, :]))
                C.mark(f"cp{s}", t)
                need(dve, t, outs[s - 2] if s >= 2 else C.prev(f"out{s + 2}"))
                for k in range(QKV_TAPS):
                    w = tap[:, s * QKV_TAPS + k:s * QKV_TAPS + k + 1]
                    if k == 0:
                        t = V(dve.tensor_scalar(acc[:, p, :], cp[:, p, k:k + S], w, None, ALU.mult))
                    else:
                        need(dve, t)
                        t = V(dve.scalar_tensor_tensor(out=acc[:, p, :], in0=cp[:, p, k:k + S], scalar=w,
                                                       in1=acc[:, p, :], op0=ALU.mult, op1=ALU.add))
                    if k < 4:
                        n = 4 * s + k
                        cf_tap(i, n, tap2[:, n:n + 1], tap2[:, 16:17])
                conv.append(t)
                C.mark(f"conv{s}", t)
                need(act, t)
                outs.append(A(act.activation(qkv[:, i * 4 + s, :], acc[:, p, :], ACT.Silu)))
                C.mark(f"out{s}", outs[-1])
        last.clear()
        last["cf"] = C.now("dve")[0]
        taps = [(c, k) for k in range(16, CF_TAPS) for c in range(3)] + [(3, k) for k in range(CF_TAPS)]
        n_taps = -(-len(taps) // 8)
        banks, squares = {}, []
        for n in range(8):
            z, s = (za, zb)[n // 4], n % 4
            t = stream_x(ps[:, s, :], [banks[s] if n >= 4 else C.now("act")[0]])
            squares.append(chunk_sums(n, qkv[:, n, :], 6, [squares[n - 4]] if n >= 4 else []))
            need(act, t)
            banks[s] = A(act.activation(z[:, s, :], ps[:, s, :], ACT.Silu))
            for c, k in taps[n * n_taps:(n + 1) * n_taps]:
                cf_tap(c, k)
        need(act, squares[-1])
        need(dve, *C.now("dve"))
        t = inverse_root(scl[:], ps[:, 6, 0:8 * NT], 1.0)
        need(pe, t)
        scaled = []
        for c in range(8):
            if c >= 2:
                need(pe, scaled[c - 2])
            need(dve, spread(ps[:, 4 + c % 2, :], scl[:, c * NT:(c + 1) * NT]))
            scaled.append(V(dve.scalar_tensor_tensor(
                out=qkv[:, c, :], in0=qkv[:, c, :], scalar=P ** -0.5 if c < 4 else 1.0, in1=ps[:, 4 + c % 2, :],
                op0=ALU.mult, op1=ALU.mult)))
        need(pe, *C.now("dve", "act"))
        for c in range(4):
            t = token_sums(ps[:, 6, 0:NT], cu[:, c, :], c == 0, c == 3)
        need(act, t)
        t = A(act.mul(scl[:, 0:NT], ps[:, 6, 0:NT], -1.0 / (4 * P)))
        need(pe, t)
        t = spread(ps[:, 7, :], scl[:, 0:NT])
        need(dve, t)
        for c in range(4):
            t = V(dve.tensor_tensor(cu[:, c, :], ps[:, 7, :], cu[:, c, :], ALU.add))
            need(act, t)
            t = A(act.activation(rt[:, c, :], cu[:, c, :], ACT.Square))
            need(pe, t)
            t = token_sums(ps[:, 6, 0:NT], rt[:, c, :], c == 0, c == 3)
        need(act, t)
        t = inverse_root(scl[:, 0:NT], ps[:, 6, 0:NT], 4 * P)
        need(pe, t)
        t = spread(ps[:, 5, :], scl[:, 0:NT])
        need(dve, t)
        done = []
        for c in range(4):
            t = V(dve.tensor_tensor(cu[:, c, :], cu[:, c, :], ps[:, 5, :], ALU.mult))
            need(act, t)
            done.append(A(act.activation(cu[:, c, :], cu[:, c, :], ACT.Silu, bias=lcl("ln_b", c),
                                         scale=lcl("ln_w", c))))
        for c in range(4):
            need(dve, done[c])
            V(dve.tensor_tensor(cu[:, c, :], cu[:, c, :], zb[:, c, :], ALU.mult))
        rendezvous()
        m_prj.close()
        delta(qkv, gl, bt, o, levels)
        wide.close()
        for c in range(4):
            t = chunk_sums(c, o[:, c, :], 6)
        need(act, t)
        t = inverse_root(scl[:, 0:4 * NT], ps[:, 6, 0:4 * NT], P)
        need(pe, t)
        for c in range(4):
            t = spread(ps[:, c, :], scl[:, c * NT:(c + 1) * NT])
            need(dve, t)
            t = V(dve.scalar_tensor_tensor(out=o[:, c, :], in0=o[:, c, :], scalar=lcl("dn_w"), in1=ps[:, c, :],
                                           op0=ALU.mult, op1=ALU.mult))
            need(dve, t)
            V(dve.tensor_tensor(o[:, c, :], o[:, c, :], za[:, c, :], ALU.mult))
        need(act, *C.now("dve"))
        need(dve, *C.now("dve"))
        fh = sb("fh", [P, 8, S], F32R, wide, side="right")
        fl = sb("fl", [P, 8, S], F32R, wide, side="right")
        split_into(fh, fl, [o[:, c, :] for c in range(4)] + [cu[:, c, :] for c in range(4)])
        rendezvous()
        keep.close()
        merge("m2", fh, fl, lambda r, i: lcol[:, bass.ds(i * 4 + 8 * r + LCOLS["gate_b"][0], 4)])
        wide.close()

    def delta(qkv, gl, bt, o, levels):
        mem = ExitStack()
        bufs = [[sb(f"dl{d}_{n}", [P, DN_H, P], ctx=mem) for n in range(9)] + [
            rt[:, 2 * d + r, :].rearrange("p (h c) -> p h c", h=DN_H) for r in range(2)] for d in range(2)]
        sm = sb("dl_small", [P, 2, 8, DN_H], ctx=mem)

        def direction(d, i):
            KT, Y, T, DT, qd, kg, kdec, vt, U, AT, St = bufs[d]
            gs, be, gc, gtot, eg, et, ekd, tmp = (sm[:, d, r, :] for r in range(8))
            at = i * P if d == 0 else i * (-P) + (NT - 1) * P
            tile = i if d == 0 else i * (-1) + (NT - 1)
            tri = mat("tri_f" if d == 0 else "tri_b")
            strict = mat("negstrict_f" if d == 0 else "negstrict_b")
            B = [ps[:, 4 * d + r, :] for r in range(4)]
            B4 = [b.rearrange("p (h c) -> p h c", h=DN_H) for b in B]
            q, k, v_ = (qkv[:, 4 * r:4 * r + 4, bass.ds(at, P)] for r in range(3))

            def per_head(f):
                for hd in range(DN_H):
                    ins = f(hd)
                return PE(ins)

            tk = G(pool.tensor_copy(KT[:] if d < 2 else KT, k))
            tv = A(act.copy(Y[:], v_))
            V(dve.tensor_copy(gs, gl[:, tile, 4 * d:4 * d + 4]))
            tg = V(dve.tensor_copy(be, bt[:, tile, 4 * d:4 * d + 4]))
            need(dve, tg)
            tb = V(dve.tensor_copy(T[:], heads4(gs)))
            need(pe, tb, tk)
            t = per_head(lambda n: pe.matmul(B[0][:, n * P:(n + 1) * P], T[:, n, :], tri, start=True, stop=True))
            pe.matmul(B[1][:, 0:4], tri, gs, start=True, stop=True)
            t1 = PE(pe.matmul(B[1][:, 4:8], mat("ones"), gs, start=True, stop=True))
            tkk = per_head(lambda n: pe.matmul(B[2][:, n * P:(n + 1) * P], KT[:, n, :], KT[:, n, :], start=True,
                                               stop=True))
            tqk = per_head(lambda n: pe.matmul(B[3][:, n * P:(n + 1) * P], KT[:, n, :], q[:, n, :], start=True,
                                               stop=True))
            yield
            need(act, t1)
            A(act.copy(gc, B[1][:, 0:4]))
            t = A(act.copy(gtot, B[1][:, 4:8]))
            need(dve, t)
            ts = V(dve.tensor_tensor(DT[:], B4[0], heads4(gc), ALU.subtract))
            te = V(dve.tensor_tensor(tmp, gtot, gc, ALU.subtract))
            need(act, ts, te)
            tq = A(act.activation(qd[:], B4[0], ACT.Exp))
            A(act.activation(eg, gc, ACT.Exp))
            A(act.activation(et, gtot, ACT.Exp))
            tx = A(act.activation(ekd, tmp, ACT.Exp))
            need(dve, ts)
            t = V(dve.tensor_scalar(DT[:], DT[:], 0.0, None, ALU.min))
            need(act, t)
            t = A(act.activation(DT[:], DT[:], ACT.Exp))
            need(pe, tq, tv)
            ttk = per_head(lambda n: pe.transpose(B[0][:, n * P:(n + 1) * P], KT[:, n, :], mat("ident")))
            need(pe, t1, *C.now("act"))
            ttv = per_head(lambda n: pe.transpose(B[1][:, n * P:(n + 1) * P], Y[:, n, :], mat("ident")))
            yield
            need(dve, tx)
            t2 = V(dve.tensor_scalar(eg, eg, -1.0, None, ALU.mult))
            tq2 = V(dve.tensor_tensor(qd[:], qd[:], q, ALU.mult))
            need(dve, t)
            t = V(dve.tensor_tensor(DT[:], DT[:], all_heads(tri), ALU.mult))
            need(dve, t, tkk)
            ta = V(dve.tensor_tensor(AT[:], B4[2], DT[:], ALU.mult))
            need(dve, ta)
            ta = V(dve.tensor_tensor(AT[:], AT[:], all_heads(strict), ALU.mult))
            need(pe, ta)
            ta = per_head(lambda n: pe.transpose(B[2][:, n * P:(n + 1) * P], AT[:, n, :], mat("ident")))
            need(dve, tqk)
            tdt = V(dve.tensor_tensor(DT[:], B4[3], DT[:], ALU.mult))
            need(dve, ttk, t2)
            V(dve.tensor_tensor(kg[:], B4[0], heads4(eg), ALU.mult))
            tkd = V(dve.tensor_tensor(kdec[:], B4[0], heads4(ekd), ALU.mult))
            need(act, ttv)
            tv = A(act.copy(vt[:], B4[1]))
            yield
            ti = V(dve.tensor_copy(T[:], all_heads(mat("ident"))))
            need(dve, ta, tv)
            t = V(dve.tensor_tensor(Y[:], B4[2], heads4(be), ALU.mult))
            need(dve, t, ti)
            settle_dve(d)
            tt = V(dve.copy_predicated(T[:], all_heads(levels[:, d, 0, :]), Y[:]))
            for lv in range(1, len(LEVELS) + 1):
                need(pe, tt, tdt)
                tu = per_head(lambda n: pe.transpose(B[3][:, n * P:(n + 1) * P], T[:, n, :], mat("ident")))
                if lv < len(LEVELS):
                    need(pe, tkd)
                    ty = per_head(lambda n: pe.matmul(B[0][:, n * P:(n + 1) * P], AT[:, n, :], T[:, n, :],
                                                      start=True, stop=True))
                yield
                need(dve, tu)
                tu = V(dve.tensor_tensor(U[:], B4[3], heads4(be), ALU.mult))
                if lv == len(LEVELS):
                    break
                need(act, ty, tt)
                ty = A(act.copy(Y[:], B4[0]))
                yield
                need(pe, tu, ty, tv)
                t = per_head(lambda n: pe.matmul(B[1][:, n * P:(n + 1) * P], U[:, n, :], Y[:, n, :],
                                                 start=True, stop=True))
                yield
                need(dve, t)
                settle_dve(d)
                tt = V(dve.copy_predicated(T[:], all_heads(levels[:, d, lv, :]), B4[1]))
            need(pe, tu, tkd)
            t = per_head(lambda n: pe.matmul(B[0][:, n * P:(n + 1) * P], kg[:, n, :], U[:, n, :], start=True,
                                             stop=True))
            need(act, t)
            tkc = A(act.copy(KT[:], B4[0]))
            yield
            need(pe, tkc, tt)

            def v_new(n):
                out = B[1][:, n * P:(n + 1) * P]
                pe.matmul(out, U[:, n, :], vt[:, n, :], start=True, stop=False)
                return pe.matmul(out, KT[:, n, :], St[:, n, :], start=False, stop=True)
            t = per_head(v_new)
            need(act, t)
            tvn = A(act.copy(AT[:], B4[1]))
            yield
            need(pe, tvn, tq2)

            def out_(n):
                out = B[2][:, n * P:(n + 1) * P]
                pe.matmul(out, St[:, n, :], qd[:, n, :], start=True, stop=False)
                return pe.matmul(out, AT[:, n, :], DT[:, n, :], start=False, stop=True)
            t = per_head(out_)
            t2 = per_head(lambda n: pe.matmul(B[3][:, n * P:(n + 1) * P], kdec[:, n, :], AT[:, n, :], start=True,
                                              stop=True))
            yield
            need(dve, t)
            ov = o[:, :, bass.ds(at, P)]
            V(dve.tensor_tensor(ov, ov, B4[2], ALU.add))
            t = V(dve.tensor_tensor(St[:], St[:], heads4(et), ALU.mult))
            need(dve, t, t2)
            V(dve.tensor_tensor(St[:], St[:], B4[3], ALU.add))
            yield

        for d in range(2):
            V(dve.memset(bufs[d][10][:], 0.0))
        with C.loop("chunk", NT) as i:
            rendezvous()
            gens = [direction(0, i), direction(1, i)]
            live = True
            while live:
                live = False
                for g in gens:
                    if next(g, "end") != "end":
                        live = True
        rendezvous()
        mem.close()

    def finish():
        store_h()
        top.close()
        return C.found

    ffn("ffn1", "norm_ffn1", s_h, early)
    mixer()
    ffn("ffn2", "norm_ffn2")
    norm_h(lambda k: col("norm_final", k))
    with C.loop("layer", N_LAYER) as l:
        layer(l, wab, levels)
    norm_h(lambda k: col("final2", k))
    return finish()


def build(nc, a):
    steps = {}
    for _ in range(6):
        scratch = a["fresh"]()
        found = program(scratch[0], scratch[1], steps)
        if found == steps:
            break
        steps = found
    assert program(nc, a, steps) == steps


def layout(x):
    f = np.float32

    def proj(w):
        k, n = w.shape
        return w.reshape(k // P, P, n // P, P).transpose(2, 1, 0, 3).reshape(n // P, P, k)

    def down(w):
        return w.reshape(w.shape[0] // P, P, D)

    def pairs(*ws):
        return np.stack(ws, 1).reshape(-1, P, ws[0].shape[-1])

    def ffn(g, u, d):
        return [pairs(proj(g), proj(u)), down(d)]

    units = ffn(x["ffn1_gate"][0], x["ffn1_up"][0], x["ffn1_down"][0])
    w = x["w_in"][0]
    widths = (512, 128, 128, 128, 128, 128, 128, 24, 512, 64, 64, 1024, 1024)
    nq, kc, vc, ksl, vsl, kwn, vwn, ng, sq, sk, sv, ga, gb = np.split(w, np.cumsum(widths)[:-1], axis=1)
    both = np.concatenate([sv, ng, sv[:, :40]], 1)
    units += [proj(nq), proj(sq), proj(ksl), proj(kwn), proj(np.concatenate([sk, sk], 1)), proj(kc), proj(vc),
              proj(vsl), proj(vwn), proj(both)]
    ab = np.concatenate([proj(x["w_branch_a"][0]), proj(x["w_branch_b"][0])], 2)
    units += [pairs(proj(ga), proj(gb)), ab, proj(x["w_out"][0])]
    units += ffn(x["ffn2_gate"][0], x["ffn2_up"][0], x["ffn2_down"][0])
    wab = []
    for l in range(N_LAYER):
        w = x["w_in_2"][l]
        qkv, za, al, bl, val, glu, zb, gt = np.split(w, np.cumsum((1536, 512, 8, 8, 512, 512, 512)), axis=1)
        wab.append(np.concatenate([al, bl], 1).reshape(KD, P, 16).transpose(1, 0, 2))
        g = gt.reshape(D, 2, D)
        out = np.concatenate([proj(x["w_dn_out_2"][l]), proj(x["w_cf_out_2"][l])], 2)
        units += [pairs(proj(glu), proj(val)), proj(qkv), proj(za), proj(zb),
                  pairs(proj(g[:, 0]), proj(g[:, 1]), out), proj(x["w_out_2"][l])]
    stream = np.concatenate(units)
    assert stream.shape == (N_UNITS, P, UNIT), stream.shape
    stream = np.concatenate([stream, stream[:SPARE]])

    def c(v):
        return np.asarray(v).reshape(-1, P).T

    def wide(v):
        return np.broadcast_to(np.asarray(v).reshape(1, -1), (P, np.asarray(v).size))

    def pe2(v):
        return v.reshape(16, 2 * HD).T

    half = HD // 2
    inv = (np.float32(10000.0) ** (-np.arange(half, dtype=f) / f(half))).astype(f)
    parts = {"norm_ffn1": c(x["norm_ffn1"][0]), "norm_mix": c(x["norm_mix"][0]), "norm_ffn2": c(x["norm_ffn2"][0]),
             "norm_final": c(x["norm_final"]), "final2": c(x["final_norm_w_2"]), "sinks": wide(x["swa_sinks"][0]),
             "pe_k": pe2(x["cmp_pe_k"][0]), "pe_v": pe2(x["cmp_pe_v"][0]), "inv_freq": np.tile(inv, 4).reshape(P, 1)}
    cols = np.concatenate([parts[n] for n in COLS], 1).astype(f)
    lc = []
    for l in range(N_LAYER):
        parts = {"norm": c(x["norm_w_2"][l]),
                 "qkv_w": x["qkv_conv_w_2"][l].reshape(QKV_TAPS, 12, P).transpose(2, 1, 0).reshape(P, -1),
                 "cf_w": x["cf_conv_w_2"][l].reshape(CF_TAPS, 4, P).transpose(2, 1, 0).reshape(P, -1),
                 "cf_b": c(x["cf_conv_b_2"][l]), "ln_w": c(x["cf_ln_w_2"][l]), "ln_b": c(x["cf_ln_b_2"][l]),
                 "gate_b": c(x["gate_b_2"][l]), "dn_w": c(x["dn_norm_w_2"][l]),
                 "a_log": wide(x["a_log_2"][l]), "dt_bias": wide(x["dt_bias_2"][l])}
        lc.append(np.concatenate([parts[n] for n in LCOLS], 1))
    i = np.arange(P)
    rot = np.zeros((P, P), f)
    for m in range(P):
        if m % HD < half:
            rot[m + half, m] = -1
        else:
            rot[m - half, m] = 1
    m = {"ident": np.eye(P), "ones": np.ones((P, P)), "rot": rot,
         "tri_f": i[:, None] <= i[None, :], "tri_b": i[:, None] >= i[None, :],
         "negstrict_f": -1.0 * (i[:, None] < i[None, :]), "negstrict_b": -1.0 * (i[:, None] > i[None, :])}
    mats = np.stack([m[n] for n in MATS], 1).astype(f)
    lev = []
    for b in LEVELS:
        blk = i // b
        sib = (blk[:, None] // 2 == blk[None, :] // 2)
        lev.append(sib & (blk[:, None] > blk[None, :]))
    lev = np.stack(lev, 1)
    levels = np.stack([lev, lev.transpose(2, 1, 0)], 1).astype(f)
    q, s = i[:, None], i[None, :]
    causal = np.where(s > q, NEG, 0.0)
    s = np.arange(2 * P)[None, :]
    band = np.where((s - P <= q) & (s > q), 0.0, NEG)
    t = np.arange(S).reshape(NT, P).T[:, :, None]
    n = np.arange(32)[None, None, :]
    vis = np.where((16 * n + 31 <= t) & (n < CMP_N), 0.0, NEG).reshape(P, -1)
    valid = (np.arange(S).reshape(NT, P).T >= 31) * 1.0
    masks = np.concatenate([causal, band, vis, valid], 1).astype(f)
    w1 = [x[n][0].reshape(16, P, 2 * P).transpose(1, 0, 2) for n in ("cmp_k_w1", "cmp_v_w1")]
    w2 = [x[n][0].reshape(2, P, HD).transpose(1, 0, 2) for n in ("cmp_k_w2", "cmp_v_w2")]
    w2k = np.concatenate([w2[0], w2[0]], 2)
    ca = np.ascontiguousarray
    return {"stream": ca(stream), "xT": ca(x["x"][0].T.reshape(KD, P, S).transpose(1, 0, 2)), "cols": ca(cols),
            "lcols": ca(np.stack(lc, 1)), "mats": ca(mats), "levels": ca(levels), "masks": ca(masks),
            "w1": ca(np.stack(w1)), "w2k": ca(w2k), "w2v": ca(w2[1]), "wab": ca(np.stack(wab)),
            "pos": ca(np.tile(x["positions"].reshape(1, S), (P, 1)))}


def kernel(**inputs):
    import concourse.bacc as bacc
    from concourse.bass_utils import run_bass_kernel_spmd

    arrays = layout({k: np.asarray(v) for k, v in inputs.items()})

    def fresh():
        nc = bacc.Bacc("TRN2", target_bir_lowering=False, num_devices=1)
        a = {n: nc.dram_tensor("in_" + n, v.shape, mybir.dt.from_np(v.dtype), kind="ExternalInput").ap()
             for n, v in arrays.items()}
        a["outT"] = nc.dram_tensor("outT", (P, KD, S), F32, kind="ExternalOutput").ap()
        a["fresh"] = fresh
        return nc, a

    nc, a = fresh()
    build(nc, a)
    r = run_bass_kernel_spmd(nc, [{"in_" + n: v for n, v in arrays.items()}], core_ids=[0])
    out = r.results[0]["outT"]
    return np.ascontiguousarray(out.transpose(1, 0, 2).reshape(D, S).T).reshape(1, S, D)
```

```python
from contextlib import ExitStack, contextmanager

import numpy as np

import concourse.bass as bass
from concourse import mybir

F32 = mybir.dt.float32
F32R = mybir.dt.float32r
I32 = mybir.dt.int32
U8 = mybir.dt.uint8
ALU = mybir.AluOpType
ACT = mybir.ActivationFunctionType
AX = mybir.AxisListType

P = 128
S = 512
NT = S // P
D = 1024
KD = D // P
FF = 2816
NF = FF // P
HD = 64
EPS = 1e-6
NEG = -1e30
SCALE = HD ** -0.5
CMP_N = 31
DN_H = 4
CF_TAPS = 31
CF_PAD = CF_TAPS // 2
QKV_TAPS = 5
QKV_PAD = QKV_TAPS // 2
N_LAYER = 2

UNIT = 8 * P
RING = 4
AHEAD = 2
U_FFN = 3 * NF
U_MIX = 8 + 8 + 24 + 8
U_LAYER = 8 + 8 + 12 + 24 + 8
N_UNITS = 2 * U_FFN + U_MIX + N_LAYER * U_LAYER
SPARE = RING + AHEAD

COLS = {}
_at = 0
for _name, _n in (("norm_ffn1", 8), ("norm_mix", 8), ("norm_ffn2", 8), ("norm_final", 8), ("final2", 8),
                  ("sinks", 8), ("pe_k", 16), ("pe_v", 16), ("inv_freq", 1)):
    COLS[_name] = (_at, _n)
    _at += _n
N_COLS = _at
LCOLS = {}
_at = 0
for _name, _n in (("norm", 8), ("qkv_w", 12 * QKV_TAPS), ("cf_w", 4 * CF_TAPS), ("cf_b", 4), ("ln_w", 4),
                  ("ln_b", 4), ("gate_b", 16), ("dn_w", 1), ("a_log", 8), ("dt_bias", 8)):
    LCOLS[_name] = (_at, _n)
    _at += _n
N_LCOLS = _at
MATS = ["ident", "ones", "rot", "tri_f", "tri_b", "negstrict_f", "negstrict_b"]
LEVELS = [1, 2, 4, 8, 16, 32, 64]


class Lin:

    def __init__(self, const=0, terms=()):
        self.const, self.terms = const, tuple(terms)

    def add(self, n):
        return Lin(self.const + n, self.terms)

    def term(self, reg, n):
        return Lin(self.const, self.terms + ((reg, n),)) if n else self

    def value(self, div=1):
        v = self.const // div
        for reg, n in self.terms:
            assert n % div == 0
            v = reg * (n // div) + v
        return v


class Tok:

    def __init__(self, key, lin):
        self.key, self.lin = key, lin


class Counter:

    BIAS = 256

    def __init__(self, nc, sems, steps):
        self.nc, self.sems, self.steps = nc, sems, steps
        self.count = {k: Lin(self.BIAS) for k in sems}
        self.count["unit"] = Lin(0)
        self.loops = []
        self.settle = None
        self.found = {}

    def inc(self, key, ins, n=1):
        ins.then_inc(self.sems[key], n)
        self.count[key] = self.count[key].add(n)
        return Tok(key, self.count[key])

    def wait(self, eng, *toks):
        for t in toks:
            if t is not None:
                assert t.lin.const >= 0, (t.key, t.lin.const)
                eng.wait_ge(self.sems[t.key], t.lin.value())

    def now(self, *keys):
        return [Tok(k, self.count[k]) for k in keys]

    def mark(self, name, tok):
        start = self.loops[-1][1]
        self.loops[-1][2][name] = (tok.key, tok.lin.const - start[tok.key].const)

    def prev(self, name):
        loop, start, _, reg = self.loops[-1]
        key, off = self.steps.get(loop, {}).get("marks", {}).get(name, ("pe", 0))
        per = self.steps.get(loop, {}).get("per", {}).get(key, 0)
        return Tok(key, start[key].add(off - per).term(reg, per))

    @contextmanager
    def loop(self, name, n):
        per = self.steps.get(name, {}).get("per", {})
        start = dict(self.count)
        if self.loops:
            self.settle()
            start = dict(self.count)
        with self.nc.Fori(0, n) as reg:
            self.count = {k: c.term(reg, per.get(k, 0)) for k, c in start.items()}
            marks = {}
            self.loops.append((name, start, marks, reg))
            yield reg
            self.loops.pop()
            self.found[name] = {
                "per": {k: c.const - start[k].const for k, c in self.count.items()}, "marks": marks}
        self.count = {k: c.add(n * per.get(k, 0)) for k, c in start.items()}


def program(nc, a, steps):
    pe, act, dve, pool, sp = nc.tensor, nc.scalar, nc.vector, nc.gpsimd, nc.sync
    top = ExitStack()

    def sb(name, shape, dt=F32, ctx=None, side=None):
        return (ctx or top).enter_context(nc.sbuf_tensor(name, shape, dt, side=side))

    names = ["pe", "act", "dve", "pool", "whi", "wlo", "used", "tab"]
    sems = {k: top.enter_context(nc.semaphore("s_" + k)) for k in names}
    landed = [top.enter_context(nc.semaphore(f"s_landed{i}")) for i in range(RING)]
    s_h = [top.enter_context(nc.semaphore(f"s_h{i}")) for i in range(4)]
    s_par = top.enter_context(nc.semaphore("s_par"))
    s_lpar = top.enter_context(nc.semaphore("s_lpar"))
    s_aux = top.enter_context(nc.semaphore("s_aux"))
    s_out = top.enter_context(nc.semaphore("s_out"))
    C = Counter(nc, sems, steps)
    bias_eng = {"pe": pe, "used": pe, "act": act, "whi": act, "dve": dve, "tab": dve, "pool": pool, "wlo": pool}
    for k in names:
        bias_eng[k].sem_inc(sems[k], C.BIAS)

    C.settle = lambda: settle_all()

    def PE(ins): return C.inc("pe", ins)
    def A(ins): return C.inc("act", ins)
    def V(ins): return C.inc("dve", ins)
    def G(ins): return C.inc("pool", ins)
    def need(eng, *toks): C.wait(eng, *toks)

    def settle_all():
        settle_pe()
        settle_dve(2)
        G(pool.tensor_tensor(epsc[:, 5:6], epsc[:, 0:1], epsc[:, 0:1], ALU.add))

    def settle_pe():
        pe.matmul(ps[:, 7, 0:2], mat("ident"), mats[:, 0, 0:2], start=True, stop=True)

    def settle_dve(n):
        C.inc("tab" if n == 2 else "dve", dve.tensor_copy(epsc[:, 2 + n:3 + n], epsc[:, 0:1]))

    def settle_act(n):
        A(act.copy(epsc[:, 6 + n:7 + n], epsc[:, 0:1]))

    def rendezvous():
        for eng in (pe, act, dve, pool):
            need(eng, *C.now("pe", "act", "dve", "pool", "used", "tab"))

    h = sb("h", [P, KD, S])
    xh = sb("xh", [P, KD, S], F32R)
    xl = sb("xl", [P, KD, S], F32R)
    raw = sb("raw", [P, RING, UNIT])
    whi = sb("whi", [P, RING, UNIT], F32R)
    wlo = sb("wlo", [P, RING, UNIT], F32R)
    cols = sb("cols", [P, N_COLS])
    mats = sb("mats", [P, len(MATS), P])
    lcol = sb("lcol", [P, N_LCOLS])
    lcols = sb("lcols", [P, N_LAYER, N_LCOLS])
    rt = sb("rt", [P, 4, S])
    epsc = sb("epsc", [P, 13])
    scl = sb("scl", [P, 8 * NT])
    ps = top.enter_context(nc.psum_tensor("ps", [P, 8, S], F32))

    def col(name, i=0, n=1):
        return cols[:, COLS[name][0] + i:COLS[name][0] + i + n]

    def lcl(name, i=0, n=1):
        return lcol[:, LCOLS[name][0] + i:LCOLS[name][0] + i + n]

    def mat(name):
        return mats[:, MATS.index(name), :]

    for j in range(4):
        (act, sp)[j % 2].dma_start(h[:, 2 * j:2 * j + 2, :], a["xT"][:, 2 * j:2 * j + 2, :]).then_inc(s_h[j], 16)
    for i in range(RING):
        sp.dma_start(raw[:, i, :], a["stream"][i]).then_inc(landed[i], 16)
    act.dma_start(cols[:], a["cols"]).then_inc(s_par, 16)
    act.dma_start(mats[:], a["mats"]).then_inc(s_par, 16)
    act.dma_start(lcols[:], a["lcols"]).then_inc(s_par, 16)
    m_msk, m_mlp = ExitStack(), ExitStack()
    msk = sb("msk", [P, 3 * P + NT * 32 + NT], ctx=m_msk, side="right")
    cosT = sb("cosT", [P, S], ctx=m_mlp, side="right")
    sinT = sb("sinT", [P, S], ctx=m_mlp, side="right")
    w1k = sb("w1k", [P, 16, 2 * P], ctx=m_mlp, side="right")
    w2k = sb("w2k", [P, 2, P], ctx=m_mlp, side="right")
    w2v = sb("w2v", [P, 2, HD], ctx=m_mlp, side="right")
    wab = sb("wab", [P, N_LAYER, KD * 16])
    levels = sb("levels", [P, 2, len(LEVELS), P], U8)
    c0 = V(dve.memset(epsc[:, 0:1], EPS))
    for eng in (pe, act, dve, pool):
        eng.wait_ge(s_par, 48)
        need(eng, c0)

    def split_unit(unit):
        slot = unit.const % RING
        act.wait_ge(landed[slot], unit.add(RING).value(RING) * 16)
        need(act, Tok("used", unit.add(C.BIAS + 1 - RING)))
        C.inc("whi", act.copy(whi[:, slot, :], raw[:, slot, :]))
        hi = Tok("whi", unit.add(C.BIAS + 1))
        need(pool, hi)
        C.inc("wlo", pool.tensor_tensor(wlo[:, slot, :], raw[:, slot, :], whi[:, slot, :].bitcast(F32),
                                        ALU.subtract))
        need(sp, Tok("wlo", unit.add(C.BIAS + 1)))
        sp.dma_start(raw[:, slot, :], a["stream"][unit.add(RING).value()]).then_inc(landed[slot], 16)


    def stream(tiles):
        for done in stream_tiles(tiles):
            pass
        return done

    def stream_tiles(tiles):
        unit = C.count["unit"]
        split_unit(unit.add(AHEAD))
        slot = unit.const % RING
        need(pe, Tok("wlo", unit.add(C.BIAS + 1)))
        for t, (out, hi, lo, first, last, waits) in enumerate(tiles):
            need(pe, *waits)
            wh, wl = whi[:, slot, t * P:(t + 1) * P], wlo[:, slot, t * P:(t + 1) * P]
            m = out.shape[0]
            pe.matmul(out, wh[:, 0:m], hi, start=first, stop=False)
            pe.matmul(out, wh[:, 0:m], lo, start=False, stop=False)
            ins = pe.matmul(out, wl[:, 0:m], hi, start=False, stop=last)
            if t < len(tiles) - 1:
                yield None
        C.count["unit"] = unit.add(1)
        yield C.inc("used", ins)

    def stream_x(out, waits=(), ready=None):
        return stream(x_tiles(out, waits, ready))

    def x_tiles(out, waits=(), ready=None):
        return [(out, xh[:, k, :], xl[:, k, :], k == 0, k == KD - 1,
                 (list(waits) if k == 0 else []) + ([ready[k]] if ready else [])) for k in range(KD)]

    def token_sums(out, squares, first, last):
        for j in range(NT):
            ins = pe.matmul(out[:, j:j + 1], squares[:, j * P:(j + 1) * P], mat("ones")[:, 0:1],
                            start=first and j == 0, stop=last, skip_group_check=True)
        return PE(ins)

    def spread(out, colsum):
        for j in range(NT):
            ins = pe.matmul(out[:, j * P:(j + 1) * P], colsum[:, j:j + 1].broadcast_to([P, P]), mat("ident"),
                            start=True, stop=True)
        return PE(ins)

    def inverse_root(dst, sums, total):
        t = A(act.activation(dst, sums, ACT.Sqrt, bias=epsc[:, 0:1], scale=1.0 / total))
        need(dve, t)
        return V(dve.reciprocal(dst, dst))

    h_sums, h_squares = [], []

    def square_sum(n, k, ready):
        if n == 0:
            h_sums.clear()
            h_squares.clear()
        need(act, ready, h_sums[n // 2 - 2] if n >= 4 else None)
        h_squares.append(A(act.activation(rt[:, n % 4, :], h[:, k, :], ACT.Square)))

        def pair(m):
            need(dve, h_squares[m])
            t = V(dve.tensor_tensor(rt[:, m % 4, :], rt[:, m % 4, :], rt[:, (m - 1) % 4, :], ALU.add))
            need(pe, t)
            h_sums.append(token_sums(ps[:, 6, 0:NT], rt[:, m % 4, :], m == 1, m == KD - 1))
        if n % 2 == 0 and n:
            pair(n - 1)
        if n == KD - 1:
            pair(n)

    def rms_scale():
        need(act, *C.now("pe"))
        t = inverse_root(scl[:, 0:NT], ps[:, 6, 0:NT], D)
        need(pe, t)
        return spread(ps[:, 5, :], scl[:, 0:NT])

    def norm_to_x(gain, beside=None):
        rendezvous()
        if beside:
            beside()
        need(dve, rms_scale())
        lo, ready = [], []
        for k in range(KD):
            need(dve, lo[k - 4] if k >= 4 else None)
            y = C.inc("tab", dve.scalar_tensor_tensor(out=rt[:, k % 4, :], in0=h[:, k, :], scalar=gain(k),
                                                      in1=ps[:, 5, :], op0=ALU.mult, op1=ALU.mult))
            need(act, y)
            hi = A(act.copy(xh[:, k, :], rt[:, k % 4, :]))
            eng, key = (dve, "tab") if k % 2 == 0 else (pool, "pool")
            need(eng, hi)
            lo.append(C.inc(key, eng.tensor_tensor(xl[:, k, :], rt[:, k % 4, :], xh[:, k, :].bitcast(F32),
                                             ALU.subtract)))
            ready.append(lo[-1])
        return ready

    def split_into(hi, lo, srcs):
        for k, src in enumerate(srcs):
            t = A(act.copy(hi[:, k, :], src))
            need(dve, t)
            V(dve.tensor_tensor(lo[:, k, :], src, hi[:, k, :].bitcast(F32), ALU.subtract))

    def ffn(name, gain, beside=None):
        ready = norm_to_x(lambda k: col(gain, k))
        with ExitStack() as mem:
            mid = sb(name + "_mid", [P, NF, S], ctx=mem)
            sil = sb(name + "_sil", [P, 2, S], ctx=mem)
            mh = sb(name + "_mh", [P, 2, S], F32R, ctx=mem)
            ml = sb(name + "_ml", [P, 2, S], F32R, ctx=mem)
            last = None
            if beside:
                beside(mid)
            with C.loop(name + "_up", NF // 2) as i:
                for s in range(2):
                    g, u = ps[:, 2 * s, :], ps[:, 2 * s + 1, :]
                    free = C.prev(f"mid{s}")
                    tg = stream_x(g, [free], ready if s == 0 else None)
                    need(act, tg, free)
                    ts = A(act.activation(sil[:, s, :], g, ACT.Silu))
                    tu = stream_x(u)
                    need(dve, ts, tu)
                    last = V(dve.tensor_tensor(mid[:, i * 2 + s, :], sil[:, s, :], u, ALU.mult))
                    C.mark(f"mid{s}", last)
            rendezvous()

            def down(f, s, first, last_f, free):
                need(act, free)
                hi = A(act.copy(mh[:, s, :], mid[:, f, :]))
                need(dve, hi)
                lo = V(dve.tensor_tensor(ml[:, s, :], mid[:, f, :], mh[:, s, :].bitcast(F32), ALU.subtract))
                return stream([(ps[:, d, :], mh[:, s, :], ml[:, s, :], first, last_f, [lo] if d == 0 else [])
                               for d in range(KD)])

            down(0, 0, True, False, None)
            down(1, 1, False, False, None)
            with C.loop(name + "_down", (NF - 6) // 4) as i:
                t = []
                for s in range(4):
                    free = C.prev(f"u{s + 2}") if s < 2 else t[s - 2]
                    t.append(down(i * 4 + 2 + s, s % 2, False, False, free))
                    C.mark(f"u{s}", t[-1])
            used = C.count["used"]
            t = [Tok("used", used.add(-1)), Tok("used", used)]
            for s in range(4):
                t.append(down(NF - 4 + s, s % 2, False, s == 3, t[s]))
            done = C.now("used")
            need(dve, *done)
            for n, d in enumerate([6] + [d for d in range(KD) if d != 6]):
                t = V(dve.scalar_tensor_tensor(out=h[:, d, :], in0=ps[:, d, :], scalar=0.5, in1=h[:, d, :],
                                               op0=ALU.mult, op1=ALU.add))
                square_sum(n, d, t)
            rendezvous()

    def finish():
        sp.wait_ge(s_out, 16 * KD // 2)
        for i in range(RING):
            sp.wait_ge(landed[i], 16 * ((C.count["unit"].const + SPARE - 1 - i) // RING + 1))
        top.close()
        return C.found

    def early(mid):
        flat = mid[:].rearrange("p f s -> p (f s)")
        n_lev = 2 * len(LEVELS) * P
        levels_f = flat[:, NF * S - n_lev:NF * S].rearrange("p (d l n) -> p d l n", d=2, l=len(LEVELS))
        tmp = mid[:, 12:16, :]
        posi = tmp[:, 0, :].bitcast(I32)
        sp.dma_start(posi, a["pos"]).then_inc(s_aux, 16)
        sp.dma_start(levels_f, a["levels"]).then_inc(s_aux, 16)
        sp.dma_start(msk[:], a["masks"]).then_inc(s_lpar, 16)
        sp.dma_start(w2k[:], a["w2k"]).then_inc(s_lpar, 16)
        sp.dma_start(w2v[:], a["w2v"]).then_inc(s_lpar, 16)
        sp.dma_start(wab[:], a["wab"].rearrange("l p k n -> p l (k n)")).then_inc(s_lpar, 16)
        sp.dma_start(w1k[:], a["w1"][0]).then_inc(s_lpar, 16)
        dve.wait_ge(s_aux, 32)
        C.inc("tab", dve.tensor_copy(levels[:], levels_f))
        rope_tables(cosT[:], sinT[:], tmp)
        need(dve, *C.now("act", "tab"))

    def rope_tables(cosT, sinT, tmp):
        posi = tmp[:, 0, :].bitcast(I32)
        t = C.inc("tab", dve.tensor_copy(tmp[:, 1, :], posi))
        need(dve, t)
        t = C.inc("tab", dve.tensor_scalar(tmp[:, 1, :], tmp[:, 1, :], col("inv_freq"), None, ALU.mult))
        need(dve, t)
        two_pi = 2 * np.pi
        c1 = float(np.float32(6.28125))
        c2 = float(np.float32(two_pi - c1))
        c3 = float(np.float32(two_pi - c1 - float(np.float32(c2))))
        magic = 1.5 * 2.0 ** 23
        for out, shift in ((sinT, 0.0), (cosT, 0.25)):
            t = C.inc("tab", dve.tensor_scalar(tmp[:, 2, :], tmp[:, 1, :], 1 / two_pi, shift, ALU.mult, ALU.add))
            need(dve, t)
            t = C.inc("tab", dve.tensor_scalar(tmp[:, 2, :], tmp[:, 2, :], magic, -magic, ALU.add, ALU.add))
            need(dve, t)
            src = tmp[:, 1, :]
            for cc in (c1, c2, c3):
                t = C.inc("tab", dve.scalar_tensor_tensor(out=tmp[:, 3, :], in0=tmp[:, 2, :], scalar=-cc, in1=src,
                                               op0=ALU.mult, op1=ALU.add))
                need(dve, t)
                src = tmp[:, 3, :]
            t = C.inc("tab", dve.tensor_scalar(tmp[:, 3, :], tmp[:, 3, :], shift * two_pi, float(np.float32(np.pi)),
                                    ALU.add, ALU.min))
            need(dve, t)
            t = C.inc("tab", dve.tensor_scalar(tmp[:, 3, :], tmp[:, 3, :], -float(np.float32(np.pi)), None, ALU.max))
            need(act, t)
            t = A(act.activation(out, tmp[:, 3, :], ACT.Sin))
            need(dve, t)

    def mixer():
        ready = norm_to_x(lambda k: col("norm_mix", k))
        mem = ExitStack()
        qall = sb("qall", [P, 8, S], ctx=mem)
        m_att = ExitStack()
        kd = sb("kd", [P, 5, S], ctx=m_att)
        kcc = sb("kcc", [P, 2, 32], ctx=m_att)
        vcc = sb("vcc", [32, 2, HD], ctx=m_att)
        vtok = sb("vtok", [P, NT, 2, P], ctx=m_att)
        vsw = sb("vsw", [P, NT, P], ctx=m_att)
        gts = sb("gts", [P, NT, 24], ctx=m_att)
        causal, band = msk[:, 0:P], msk[:, P:3 * P]
        vis = msk[:, 3 * P:3 * P + NT * 32].rearrange("p (t n) -> p t n", t=NT)
        valid = msk[:, 3 * P + NT * 32:]
        m_prj = ExitStack()
        w1v = sb("w1v", [P, 16, 2 * P], ctx=m_prj)
        kc2 = sb("kc2", [P, 2, 2, S // 2], ctx=m_prj)
        blk = sb("blk", [P, 16, 2, 32], ctx=m_prj)
        hid = sb("hid", [P, 2, 64], ctx=m_prj)
        hid2 = sb("hid2", [P, 2, 64], ctx=m_prj)
        hid3 = sb("hid3", [P, 2, 64], ctx=m_prj)
        xr = sb("xr", [P, 2, S], ctx=m_prj)
        tmp = sb("tmpp", [P, 4, S], ctx=m_prj)
        act.dma_start(w1v[:], a["w1"][1]).then_inc(s_lpar, 16)

        def rope(src, out, s, freed):
            t = A(act.copy(xr[:, s, :], src))
            need(pe, t, freed)
            r = PE(pe.matmul(ps[:, 4 + s, :], mat("rot"), xr[:, s, :], start=True, stop=True))
            need(dve, t, freed)
            t1 = V(dve.tensor_tensor(tmp[:, 2 * s, :], xr[:, s, :], cosT[:], ALU.mult))
            need(dve, r)
            t2 = V(dve.tensor_tensor(tmp[:, 2 * s + 1, :], ps[:, 4 + s, :], sinT[:], ALU.mult))
            need(dve, t1, t2)
            return out(tmp[:, 2 * s, :], tmp[:, 2 * s + 1, :])

        with C.loop("q_proj", 2) as i:
            done = []
            for s in range(4):
                free = C.prev(f"q{s}")
                t = stream_x(ps[:, s, :], [free], ready if s == 0 else None)
                need(act, t, done[s - 2] if s >= 2 else C.prev(f"q{s + 2}"))
                done.append(rope(ps[:, s, :], lambda x, y: V(dve.tensor_tensor(
                    qall[:, i * 4 + s, :], x, y, ALU.add)), s % 2, done[s - 2] if s >= 2 else C.prev(f"q{s + 2}")))
                C.mark(f"q{s}", done[-1])
        rendezvous()
        done = []
        for s in range(3):
            t = stream_x(ps[:, s, :])
            free = done[s - 2] if s >= 2 else None
            need(act, t, free)

            def out(x, y, s=s):
                if s == 2:
                    return V(dve.tensor_tensor(kd[:, 4, :], x, y, ALU.add))
                for g in range(2):
                    for half in range(2):
                        t = V(dve.tensor_tensor(kd[64 * half:64 * half + 64, 2 * s + g, :],
                                                x[64 * g:64 * g + 64, :], y[64 * g:64 * g + 64, :], ALU.add))
                return t
            done.append(rope(ps[:, s, :], out, s % 2, free))
        for s in range(2):
            t = stream_x(ps[:, 3 * (1 - s), :], [done[0]] if s else [])
            need(act, t)
            for g in range(2):
                for par in range(2):
                    A(act.copy(kc2[64 * par:64 * par + 64, s, g, :],
                               ps[64 * g:64 * g + 64, 3 * (1 - s), par:S:2]))
        kc_ready = C.now("act")
        def compress(w, w1):
            need(dve, *C.now("act", "pe"))
            for g in range(2):
                for lp in range(16):
                    V(dve.tensor_scalar(blk[:, lp, g, 0:CMP_N], kc2[:, w, g, lp:lp + 8 * (CMP_N - 1) + 1:8],
                                        col("pe_k" if w == 0 else "pe_v", lp), None, ALU.add))
            blocks = C.now("dve")
            yield
            need(pe, *blocks, *C.now("act"))
            for m in range(2):
                for lp in range(16):
                    ins = pe.matmul(ps[:, 7, m * 64:m * 64 + 62], w1[:, lp, m * P:(m + 1) * P],
                                    blk[:, lp, :, 0:CMP_N], start=lp == 0, stop=lp == 15)
                t = PE(ins)
            z = ps[:, 7, 0:128].rearrange("p (m n) -> p m n", m=2)[:, :, 0:62]
            x1, x2, x3 = hid[:, :, 0:62], hid2[:, :, 0:62], hid3[:, :, 0:62]
            need(act, t, *C.now("dve"))
            t = A(act.copy(x1, z))
            need(dve, t)
            t = V(dve.tensor_tensor(x2, x1, x1, ALU.mult))
            need(dve, t)
            t = V(dve.tensor_scalar(x2, x2, 0.044715, 1.0, ALU.mult, ALU.add))
            need(dve, t)
            t = V(dve.tensor_tensor(x2, x2, x1, ALU.mult))
            need(act, t)
            t = A(act.activation(x3, x2, ACT.Tanh, scale=float(np.sqrt(2 / np.pi))))
            need(dve, t)
            t = V(dve.tensor_scalar(x3, x3, 0.5, 0.5, ALU.mult, ALU.add))
            need(dve, t)
            hidden = V(dve.tensor_tensor(x1, x3, x1, ALU.mult))
            yield
            need(pe, hidden)
            if w == 0:
                for m in range(2):
                    ins = pe.matmul(ps[:, 0, 0:62], w2k[:, m, :], hid[:, m, 0:62], start=m == 0, stop=m == 1)
                need(act, PE(ins))
                t = A(act.copy(hid2[:, 0, 0:62], ps[:, 0, 0:62]))
                need(pe, t)
                need(dve, PE(pe.matmul(ps[:, 0, 64:126], mat("rot"), hid2[:, 0, 0:62], start=True, stop=True)))
                for g in range(2):
                    o = 31 * g
                    t1 = V(dve.tensor_tensor(hid3[:, 0, o:o + 31], hid2[:, 0, o:o + 31], cosT[:, 31:S:16], ALU.mult))
                    t2 = V(dve.tensor_tensor(hid3[:, 1, o:o + 31], ps[:, 0, 64 + o:64 + o + 31],
                                             sinT[:, 31:S:16], ALU.mult))
                    need(dve, t1, t2)
                    V(dve.tensor_tensor(kcc[:, g, 0:31], hid3[:, 0, o:o + 31], hid3[:, 1, o:o + 31], ALU.add))
            else:
                for g in range(2):
                    for m in range(2):
                        ins = pe.matmul(ps[0:31, g, 0:HD], hid[:, m, 31 * g:31 * g + 31],
                                        w2v[:, m, :], start=m == 0, stop=m == 1)
                    need(act, PE(ins))
                    A(act.copy(vcc[0:31, g, :], ps[0:31, g, 0:HD]))
            yield

        def values(s):
            t = stream_x(ps[:, 1 + s, :], [done[1 if s == 0 else 2]] + kc_ready)
            need(act, t, *done, *C.now("pe"))
            t = A(act.copy(xr[:, s % 2, :], ps[:, 1 + s, :]))
            need(pe, t)
            for j in range(NT):
                t = PE(pe.transpose(ps[:, 4 + s, j * P:(j + 1) * P], xr[:, s % 2, j * P:(j + 1) * P], mat("ident")))
            need(act, t)
            pt = ps[:, 4 + s, :].rearrange("p (j c) -> p j c", j=NT)
            return A(act.copy(vtok[:, :, s, :] if s < 2 else vsw[:], pt))

        for eng in (pe, act, dve, pool):
            eng.wait_ge(s_lpar, 96)
        keys, vals = compress(0, w1k), compress(1, w1v)
        next(keys)
        values(0)
        next(keys)
        next(vals)
        values(1)
        next(keys)
        next(vals)
        need(act, values(2))
        t = A(act.activation(gts[:], vsw[:, :, HD:HD + 24], ACT.Sigmoid))
        need(dve, t)
        for j in range(NT):
            V(dve.tensor_scalar(gts[:, j, 0:8], gts[:, j, 0:8], valid[:, j:j + 1], None, ALU.mult))
        next(vals)
        rendezvous()
        m_prj.close()
        m_mlp.close()
        m_gates = ExitStack()
        gates = sb("gates", [P, 2 * KD, S], ctx=m_gates, side="right")
        pr = sb("pr", [P, 2, 2 * S], ctx=m_att)
        pt = sb("pt", [P, 2, 2, S], ctx=m_att)
        ptc = sb("ptc", [32, 2, S], ctx=m_att)
        ce = sb("ce", [P, 2, 2, NT, 32], ctx=m_att)
        cst = sb("cst", [P, 3, 4 * NT], ctx=m_att)
        qS, kS = (rt[:, 0, :], rt[:, 3, :]), rt[:, 1:3, :]
        kcS = sb("kcS", [P, 32], ctx=m_att)
        vS = sb("vS", [P, NT, 2, HD], ctx=m_att)
        vcS = sb("vcS", [32, HD], ctx=m_att)
        gS = sb("gS", [P, 2, NT, 3, 2], ctx=m_att)
        skS = sb("skS", [P, 4], ctx=m_att)
        st = sb("st", [P, 2, 5, 4], ctx=m_att)

        def two_pairs(nsa, chunk):
            tiles = [(pair, hh, i) for pair in range(2) for hh in range(2) for i in range(NT)]
            n_steps = len(tiles)
            nb = 2 if nsa else 1
            scored, expd, probs, turned, evacd, pved = {}, {}, {}, {}, {}, {}
            bank4 = C.now("dve", "act")

            def gate_tiles():
                free = bank4
                for n in range(4):
                    for t in stream_tiles(x_tiles(ps[:, 4, :], free)):
                        if t is None:
                            yield False
                    need(act, t)
                    settle_act(0)
                    free = [A(act.copy(gates[:, chunk * 2 + n, :], ps[:, 4, :]))]
                    yield True
            filler = gate_tiles()

            def fill(n):
                for _ in range(n):
                    if next(filler, True):
                        break

            def spans(i):
                return (0, i + 1) if nsa else (max(i - 1, 0), i + 1)

            def score(n):
                pair, hh, i = tiles[n]
                b, p = 64 * hh, n % 2
                j0, j1 = spans(i)
                if n >= 2:
                    need(pe, expd[n - 2])
                q = qS[pair][b:b + 64, i * P:(i + 1) * P]
                for br in range(nb):
                    ins = pe.matmul(ps[:, 2 * p + br, 0:(j1 - j0) * P], q, kS[b:b + 64, br, j0 * P:j1 * P],
                                    start=True, stop=True)
                scored[n] = PE(ins)

            def exponents(n):
                pair, hh, i = tiles[n]
                p = n % 2
                j0, j1 = spans(i)
                w = (j1 - j0) * P
                sk = skS[:, 2 * pair + hh:2 * pair + hh + 1]
                if n >= 2:
                    need(dve, probs[n - 2])
                    need(act, turned[n - 2])
                need(dve, scored[n])
                if nsa:
                    banks = ps[:, 2 * p:2 * p + 2, :]
                    last = banks[:, :, w - P:w]
                    mask = causal.unsqueeze(1).broadcast_to([P, 2, P])
                else:
                    banks = ps[:, 2 * p:2 * p + 1, :]
                    last = banks[:, 0, 0:w]
                    mask = band[:, 2 * P - w:]
                mx, nm, sm = (st[:, p, r, :] for r in range(3))
                t = V(dve.tensor_tensor(last, last, mask, ALU.add))
                need(dve, t)
                t = V(dve.tensor_reduce(mx[:, 0:nb], banks[:, :, 0:w], AX.X, ALU.max))
                need(dve, t)
                if nsa:
                    t = V(dve.tensor_scalar(nm[:, 0:nb], mx[:, 0:nb], -SCALE, None, ALU.mult))
                else:
                    t = V(dve.tensor_scalar(mx[:, 1:2], mx[:, 0:1], SCALE, sk, ALU.mult, ALU.max))
                    need(dve, t)
                    t = V(dve.tensor_scalar(nm[:, 0:1], mx[:, 1:2], -1.0, None, ALU.mult))
                need(act, t)
                for br in range(nb):
                    t = A(act.activation(pr[:, p, br * S:br * S + w], ps[:, 2 * p + br, 0:w], ACT.Exp,
                                         bias=nm[:, br:br + 1], scale=SCALE, accum_out=sm[:, br:br + 1]))
                if not nsa:
                    t = A(act.activation(sm[:, 1:2], sk, ACT.Exp, bias=nm[:, 0:1]))
                expd[n] = t

            def weights(n):
                pair, hh, i = tiles[n]
                p = n % 2
                j0, j1 = spans(i)
                w = (j1 - j0) * P
                sm, rs, wt = (st[:, p, r, :] for r in range(2, 5))
                need(dve, expd[n])
                if not nsa:
                    t = V(dve.tensor_tensor(sm[:, 0:1], sm[:, 0:1], sm[:, 1:2], ALU.add))
                    need(dve, t)
                t = V(dve.reciprocal(rs[:, 0:nb], sm[:, 0:nb]))
                need(dve, t)
                if nsa:
                    t = V(dve.tensor_tensor(wt[:, 0:nb], rs[:, 0:nb], gS[:, pair, i, 0:2, hh], ALU.mult))
                    need(dve, t)
                for br in range(nb):
                    dst = pr[:, p, br * S:br * S + w]
                    sc = wt[:, br:br + 1] if nsa else rs[:, 0:1]
                    t = V(dve.tensor_scalar(dst, dst, sc, None, ALU.mult))
                probs[n] = t

            def turn(n):
                pair, hh, i = tiles[n]
                p = n % 2
                j0, j1 = spans(i)
                need(pe, probs[n])
                if n >= 1:
                    need(pe, *evacd[n - 1])
                for br in range(nb):
                    for j in range(j1 - j0):
                        ins = pe.transpose(ps[:, 5 + br, j * P:(j + 1) * P],
                                           pr[:, p, br * S + j * P:br * S + (j + 1) * P], mat("ident"))
                turned[n] = PE(ins)

            def evacuate(n):
                pair, hh, i = tiles[n]
                p = n % 2
                j0, j1 = spans(i)
                w = (j1 - j0) * P
                need(act, turned[n], pved.get(n - 2))
                evacd[n] = [A(act.copy(pt[:, p, 0, 0:w], ps[:, 5, 0:w]))]
                if nsa:
                    need(dve, turned[n], pved.get(n - 2))
                    evacd[n].append(V(dve.tensor_copy(pt[:, p, 1, 0:w], ps[:, 6, 0:w])))

            def apply(n, free):
                pair, hh, i = tiles[n]
                b, p = 64 * hh, n % 2
                j0, j1 = spans(i)
                need(pe, *evacd[n], *free)
                out = ps[b:b + 64, 7, i * P:(i + 1) * P]
                terms = [(vS[:, j0 + j, br, :], pt[:, p, br, j * P:(j + 1) * P])
                         for br in range(nb) for j in range(j1 - j0)]
                if nsa:
                    terms.append((vcS[0:31, :], ptc[0:31, hh, i * P:(i + 1) * P]))
                for k, (v, w) in enumerate(terms):
                    ins = pe.matmul(out, v, w, start=k == 0, stop=k == len(terms) - 1)
                pved[n] = PE(ins)

            def compressed_scores():
                for pair in range(2):
                    for hh in range(2):
                        for i in range(NT):
                            c = P * pair + 32 * i
                            ins = pe.matmul(ps[:, 4 + 3 * hh, c:c + CMP_N],
                                            qS[pair][64 * hh:64 * hh + 64, i * P:(i + 1) * P],
                                            kcS[64 * hh:64 * hh + 64, 0:CMP_N], start=True, stop=True)
                need(dve, PE(ins))
                for pair in range(2):
                    for hh in range(2):
                        src = ps[:, 4 + 3 * hh, P * pair:P * pair + P].rearrange("p (i n) -> p i n", i=NT)
                        t = V(dve.tensor_tensor(ce[:, pair, hh, :, 0:CMP_N], src[:, :, 0:CMP_N],
                                                vis[:, :, 0:CMP_N], ALU.add))
                return t

            def compressed_softmax(t):
                e = ce[:].rearrange("p c h i n -> p (c h i) n")[:, :, 0:CMP_N]
                bc = lambda r: cst[:, r, :].unsqueeze(2).broadcast_to([P, 4 * NT, CMP_N])
                need(dve, t)
                t = V(dve.tensor_reduce(cst[:, 0, :], e, AX.X, ALU.max))
                need(dve, t)
                t = V(dve.tensor_tensor(e, e, bc(0), ALU.subtract))
                need(act, t)
                t = A(act.activation(e, e, ACT.Exp, scale=SCALE))
                need(dve, t)
                t = V(dve.tensor_reduce(cst[:, 1, :], e, AX.X, ALU.add))
                need(dve, t)
                t = V(dve.reciprocal(cst[:, 2, :], cst[:, 1, :]))
                need(dve, t)
                for pair in range(2):
                    n = 2 * NT * pair
                    t = V(dve.tensor_tensor(cst[:, 1, n:n + 2 * NT].rearrange("p (h t) -> p h t", h=2),
                                            cst[:, 2, n:n + 2 * NT].rearrange("p (h t) -> p h t", h=2),
                                            gS[:, pair, :, 2, :].rearrange("p t h -> p h t"), ALU.mult))
                need(dve, t)
                return V(dve.tensor_tensor(e, e, bc(1), ALU.mult))

            def compressed_turn(pair, waits):
                need(pe, *waits)
                for hh in range(2):
                    for i in range(NT):
                        ins = pe.transpose(ps[0:31, 5 + hh, i * P:(i + 1) * P], ce[:, pair, hh, i, 0:CMP_N],
                                           mat("ident"))
                need(act, PE(ins))
                for hh in range(2):
                    t = A(act.copy(ptc[0:31, hh, :], ps[0:31, 5 + hh, :]))
                need(pe, t)

            if nsa:
                bank4 = [compressed_scores()]
            score(0)
            score(1)
            if nsa:
                t = compressed_softmax(bank4[0])
            exponents(0)
            exponents(1)
            weights(0)
            fill(8)
            if nsa:
                compressed_turn(0, [t])
            freed = []
            for n in range(n_steps):
                turn(n)
                if n + 2 < n_steps:
                    score(n + 2)
                evacuate(n)
                if n + 1 < n_steps:
                    weights(n + 1)
                if n + 2 < n_steps:
                    exponents(n + 2)
                fill(1 if n % 3 == 2 else 2)
                apply(n, freed)
                freed = []
                if n % 8 == 7:
                    pair = n // 8
                    need(act, pved[n])
                    settle_act(1)
                    freed = [A(act.copy(qall[:, chunk + pair, :], ps[:, 7, :]))]
                    if nsa and pair == 0:
                        compressed_turn(1, evacd[n])
            for _ in range(4):
                fill(8)

        gts_v = gts[:].rearrange("p t (b h) -> p t b h", b=3)
        vtok_v = vtok[:].rearrange("p t b (g d) -> p t b g d", g=2)
        with C.loop("nsa_group", 2) as g:
            rendezvous()
            for pair in range(2):
                A(act.copy(qS[pair], qall[:, g * 2 + pair, :]))
                for dst, br in ((2, 0), (0, 1), (1, 2)):
                    G(pool.tensor_copy(gS[:, pair, :, dst, :], gts_v[:, :, br, bass.ds(g * 4 + pair * 2, 2)]))
            V(dve.tensor_copy(kS[:, 0, :], kd[:, g, :]))
            V(dve.tensor_copy(kS[:, 1, :], kd[:, g + 2, :]))
            V(dve.tensor_copy(kcS[:, 0:CMP_N], kcc[:, g, 0:CMP_N]))
            V(dve.tensor_copy(vcS[0:31, :], vcc[0:31, g, :]))
            for br in range(2):
                V(dve.tensor_copy(vS[:, :, br, :], vtok_v[:, :, br, g, :]))
            rendezvous()
            two_pairs(True, g * 2)
        rendezvous()
        V(dve.tensor_copy(kS[:, 0, :], kd[:, 4, :]))
        V(dve.tensor_copy(vS[:, :, 0, :], vsw[:, :, 0:HD]))
        with C.loop("swa_pairs", 2) as c:
            rendezvous()
            for pair in range(2):
                A(act.copy(qS[pair], qall[:, c * 2 + 4 + pair, :]))
            V(dve.tensor_copy(skS[:], cols[:, bass.ds(c * 4 + COLS["sinks"][0], 4)]))
            rendezvous()
            two_pairs(False, c * 2 + 4)
        rendezvous()
        m_att.close()
        split_into(xh, xl, [qall[:, c, :] for c in range(8)])
        merge("m1", xh, xl, None, gates)
        m_gates.close()
        m_msk.close()
        mem.close()

    def merge(name, fh, fl, gate_b, gates=None):
        with ExitStack() as mem:
            if gates is None:
                yh_all = sb(name + "_yh", [P, KD, S], F32R, mem)
                yl_all = sb(name + "_yl", [P, KD, S], F32R, mem)
                gb = sb(name + "_gb", [P, 2, 4], ctx=mem)
                yh, yl = (lambda c: yh_all[:, c, :]), (lambda c: yl_all[:, c, :])
            else:
                g_r = gates[:].bitcast(F32R)
                yh, yl = (lambda c: g_r[:, c * 2, :]), (lambda c: g_r[:, c * 2 + 1, :])
            sg = sb(name + "_sg", [P, 2, 2, S], ctx=mem)
            ym = rt
            rendezvous()
            with C.loop(name + "_gate", 2) as i:
                if gate_b:
                    for r in range(2):
                        need(dve, *C.now("act"))
                        tb = V(dve.tensor_copy(gb[:, r, :], gate_b(r, i)))
                    need(act, tb)
                done = []
                for s in range(4):
                    p = s % 2
                    free = done[s - 2] if s >= 2 else C.prev(f"y{s + 2}")
                    bank = 4 * p
                    for r in range(2):
                        if gates is None:
                            need(act, stream_x(ps[:, bank + r, :], [free]))
                        need(act, free)
                        src = ps[:, bank + r, :] if gates is None else gates[:, i * 8 + 2 * s + r, :]
                        ts = A(act.activation(sg[:, p, r, :], src, ACT.Sigmoid,
                                              bias=gb[:, r, s:s + 1] if gate_b else 0.0))
                    tiles = [(ps[:, bank + 2 + r, :], fh[:, 4 * r + k, :], fl[:, 4 * r + k, :], k == 0, k == 3,
                              [free] if k == 0 else []) for r in range(2) for k in range(4)]
                    t = stream(tiles)
                    need(dve, ts, t)
                    t0 = V(dve.tensor_tensor(sg[:, p, 0, :], sg[:, p, 0, :], ps[:, bank + 2, :], ALU.mult))
                    t1 = V(dve.tensor_tensor(sg[:, p, 1, :], sg[:, p, 1, :], ps[:, bank + 3, :], ALU.mult))
                    need(dve, t0, t1)
                    t0 = V(dve.tensor_tensor(ym[:, p, :], sg[:, p, 0, :], sg[:, p, 1, :], ALU.add))
                    need(act, t0)
                    t = A(act.copy(yh(i * 4 + s), ym[:, p, :]))
                    need(dve, t)
                    done.append(V(dve.tensor_tensor(yl(i * 4 + s), ym[:, p, :], yh(i * 4 + s).bitcast(F32),
                                                    ALU.subtract)))
                    C.mark(f"y{s}", done[-1])
            rendezvous()
            with C.loop(name + "_out", 2) as i:
                for s in range(4):
                    t = stream([(ps[:, s, :], yh(k), yl(k), k == 0, k == KD - 1,
                                 [C.prev(f"h{s}")] if k == 0 else []) for k in range(KD)])
                    need(dve, t)
                    C.mark(f"h{s}", V(dve.tensor_tensor(h[:, i * 4 + s, :], h[:, i * 4 + s, :], ps[:, s, :],
                                                        ALU.add)))
            added = C.count["dve"]
            for k in range(KD):
                square_sum(k, k, Tok("dve", added.add(k + 1 - KD)))

    def norm_h(gain, store=False):
        rendezvous()
        need(dve, rms_scale())
        for k in range(KD):
            t = V(dve.scalar_tensor_tensor(out=h[:, k, :], in0=h[:, k, :], scalar=gain(k), in1=ps[:, 5, :],
                                           op0=ALU.mult, op1=ALU.mult))
            if not store:
                square_sum(k, k, t)
            elif k % 2 == 1:
                need(sp, t)
                sp.dma_start(a["outT"][:, k - 1:k + 1, :], h[:, k - 1:k + 1, :]).then_inc(s_out, 16)

    def chunk_sums(c, src, bank, deps=()):
        need(act, *deps)
        t = A(act.activation(rt[:, c % 4, :], src, ACT.Square))
        need(pe, t)
        return token_sums(ps[:, bank, c * NT:(c + 1) * NT], rt[:, c % 4, :], True, True)

    def heads4(row):
        return row.unsqueeze(2).broadcast_to([P, DN_H, P])

    def all_heads(m):
        return m.unsqueeze(1).broadcast_to([P, DN_H, P])

    def layer(l, wab, levels):
        keep, wide, m_prj = ExitStack(), ExitStack(), ExitStack()
        za = sb("za", [P, 4, S], ctx=keep)
        zb = sb("zb", [P, 4, S], ctx=keep)
        cu = sb("cu", [P, 4, S], ctx=keep)
        o = sb("o", [P, 4, S], ctx=keep)
        small = sb("small", [P, 10, NT, 8], ctx=keep)
        gl, bt = small[:, 8], small[:, 9]
        qkv = sb("qkv", [P, 12, S], ctx=wide, side="right")
        up = sb("up", [P, 4, S + 2 * CF_PAD], ctx=m_prj)
        cp = sb("cp", [P, 2, S + 2 * QKV_PAD], ctx=m_prj)
        acc = sb("acc", [P, 4, S], ctx=m_prj)
        ws = sb("ws", [P, KD, 16], ctx=m_prj)
        wabh = sb("wabh", [P, KD, 16], F32R, m_prj)
        wabl = sb("wabl", [P, KD, 16], F32R, m_prj)
        tap = sb("tap", [P, 4 * QKV_TAPS], ctx=m_prj)
        tap2 = sb("tap2", [P, 17], ctx=m_prj)

        def beside():
            vectors = G(pool.tensor_copy(lcol[:], lcols[:, l, :]))
            for pad, buf in ((CF_PAD, up), (QKV_PAD, cp)):
                G(pool.memset(buf[:, :, 0:pad], 0.0))
                G(pool.memset(buf[:, :, pad + S:], 0.0))
            wsrc = wab[:, l, :].rearrange("p (k n) -> p k n", k=KD)
            G(pool.tensor_copy(ws[:], wsrc))
            t = G(pool.tensor_copy(wabh[:], wsrc))
            need(pool, t)
            G(pool.tensor_tensor(wabl[:], ws[:], wabh[:].bitcast(F32), ALU.subtract))
            G(pool.memset(o[:], 0.0))
            need(dve, vectors)

        ready = norm_to_x(lambda k: lcl("norm", k), beside)
        for eng in (act, dve):
            need(eng, *C.now("pool"))

        with C.loop("glu", 2) as i:
            for s in range(2):
                free = C.prev(f"u{s}")
                tg = stream_x(ps[:, 2 * s, :], [free], ready if s == 0 else None)
                need(act, tg, free)
                ts = A(act.activation(acc[:, s, :], ps[:, 2 * s, :], ACT.Sigmoid))
                tv = stream_x(ps[:, 2 * s + 1, :])
                need(dve, ts, tv)
                C.mark(f"u{s}", V(dve.tensor_tensor(up[:, i * 2 + s, CF_PAD:CF_PAD + S], acc[:, s, :],
                                                    ps[:, 2 * s + 1, :], ALU.mult)))
        for k in range(KD):
            out = ps[0:16, 4, :]
            pe.matmul(out, wabh[:, k, :], xh[:, k, :], start=k == 0, stop=False)
            pe.matmul(out, wabl[:, k, :], xh[:, k, :], start=False, stop=False)
            ins = pe.matmul(out, wabh[:, k, :], xl[:, k, :], start=False, stop=k == KD - 1)
        need(act, PE(ins))
        ab_done = A(act.copy(acc[0:16, 2, :], ps[0:16, 4, :]))

        last = {}

        def cf_tap(c, k, w=None, bias=None, own="cf", dst=None, first=0):
            src, w = up[:, c, k:k + S], lcl("cf_w", CF_TAPS * c + k) if w is None else w
            dst = cu[:, c, :] if dst is None else dst
            need(dve, last.get(own))
            if k == first:
                bias = 0.0 if first else bias
                t = V(dve.tensor_scalar(dst, src, w, bias, ALU.mult, ALU.add))
            else:
                t = V(dve.scalar_tensor_tensor(out=dst, in0=src, scalar=w, in1=dst, op0=ALU.mult, op1=ALU.add))
            last[own] = t

        need(pe, *C.now("dve"))
        with C.loop("qkv", 3) as i:
            need(dve, *C.now("act", "dve"))
            V(dve.tensor_copy(tap[:, 0:4 * QKV_TAPS],
                              lcol[:, bass.ds(i * (4 * QKV_TAPS) + LCOLS["qkv_w"][0], 4 * QKV_TAPS)]))
            V(dve.tensor_copy(tap2[:, 0:16], lcol[:, bass.ds(i * CF_TAPS + LCOLS["cf_w"][0], 16)]))
            tw = V(dve.tensor_copy(tap2[:, 16:17], lcol[:, bass.ds(i + LCOLS["cf_b"][0], 1)]))
            need(dve, tw)
            last.clear()
            conv, outs = [], []

            def silu(s):
                need(act, conv[s])
                outs.append(A(act.activation(qkv[:, i * 4 + s, :], acc[:, s % 2, :], ACT.Silu)))
                C.mark(f"out{s}", outs[-1])

            for s in range(4):
                p = s % 2
                t = stream_x(ps[:, s, :], [C.prev(f"cp{s}")])
                need(act, t, conv[s - 2] if s >= 2 else C.prev(f"conv{s + 2}"))
                t = A(act.copy(cp[:, p, QKV_PAD:QKV_PAD + S], ps[:, s, :]))
                C.mark(f"cp{s}", t)
                if s:
                    silu(s - 1)
                need(dve, t, outs[s - 2] if s >= 2 else C.prev(f"out{s + 2}"))
                for k in range(QKV_TAPS):
                    w = tap[:, s * QKV_TAPS + k:s * QKV_TAPS + k + 1]
                    if k == 0:
                        t = V(dve.tensor_scalar(acc[:, p, :], cp[:, p, k:k + S], w, None, ALU.mult))
                    else:
                        need(dve, t)
                        t = V(dve.scalar_tensor_tensor(out=acc[:, p, :], in0=cp[:, p, k:k + S], scalar=w,
                                                       in1=acc[:, p, :], op0=ALU.mult, op1=ALU.add))
                    if k < 4:
                        n = 4 * s + k
                        cf_tap(i, n, tap2[:, n:n + 1], tap2[:, 16:17])
                conv.append(t)
                C.mark(f"conv{s}", t)
            silu(3)
        conv_end = C.now("act")[0]
        need(pe, ab_done)
        settle_pe()
        for j in range(NT):
            ins = pe.transpose(ps[:, 5, 16 * j:16 * j + 16], acc[0:16, 2, j * P:(j + 1) * P], mat("ident")[0:16, 0:16])
        raw_ab = ps[:, 5, 0:16 * NT].rearrange("p (t n) -> p t n", t=NT)
        v = [small[:, n] for n in range(8)]
        tok8 = lambda c: c.unsqueeze(1).broadcast_to([P, NT, 8])
        need(act, PE(ins))
        A(act.activation(bt, raw_ab[:, :, 8:16], ACT.Sigmoid))
        t = A(act.activation(v[7][:, 0, :], lcl("a_log", 0, 8), ACT.Exp))
        need(dve, t)
        chain = [
            lambda: V(dve.tensor_tensor(v[0], raw_ab[:, :, 0:8], tok8(lcl("dt_bias", 0, 8)), ALU.add)),
            lambda: V(dve.tensor_scalar(v[1], v[0], -1.0, None, ALU.mult)),
            lambda: V(dve.tensor_tensor(v[1], v[0], v[1], ALU.max)),
            lambda: A(act.activation(v[2], v[1], ACT.Exp, scale=-1.0)),
            lambda: V(dve.tensor_scalar(v[3], v[2], 1.0, None, ALU.add)),
            lambda: V(dve.tensor_scalar(v[4], v[3], -1.0, 1e-30, ALU.add, ALU.add)),
            lambda: V(dve.reciprocal(v[4], v[4])),
            lambda: A(act.activation(v[5], v[3], ACT.Ln)),
            lambda: V(dve.scalar_tensor_tensor(out=v[5], in0=v[5], scalar=1e-30, in1=v[4], op0=ALU.add,
                                               op1=ALU.mult)),
            lambda: V(dve.tensor_tensor(v[5], v[5], v[2], ALU.mult)),
            lambda: V(dve.scalar_tensor_tensor(out=v[5], in0=v[0], scalar=0.0, in1=v[5], op0=ALU.max, op1=ALU.add)),
            lambda: V(dve.scalar_tensor_tensor(out=gl, in0=v[5], scalar=-1.0, in1=tok8(v[7][:, 0, :]), op0=ALU.mult,
                                               op1=ALU.mult)),
        ]
        last.clear()
        last["cf"] = C.now("dve")[0]
        need(pool, *C.now("dve"))
        pool_taps = 18
        need(act, *C.now("act", "pe"))
        added = []

        def shared_tap(k):
            src, w = up[:, 3, k:k + S], lcl("cf_w", CF_TAPS * 3 + k)
            if k == 0:
                added.append(A(act.activation(cu[:, 3, :], src, ACT.Identity, bias=lcl("cf_b", 3), scale=w)))
                return
            need(act, added[k - 2] if k >= 2 else None)
            product = acc[:, 2 + k % 2, :]
            t = A(act.activation(product, src, ACT.Copy, scale=w))
            need(pool, t, added[-1])
            added.append(G(pool.tensor_tensor(cu[:, 3, :], cu[:, 3, :], product, ALU.add)))

        rest = acc[:, 0, :]
        need(dve, *C.now("act"))
        last.update({c: C.now("dve")[0] for c in range(4)})
        taps = [(c, k) for n in range(CF_TAPS - 16) for c, k in enumerate([16 + n] * 3 + [pool_taps + n])
                if k < CF_TAPS]
        beside_units = 6
        n_taps = -(-len(taps) // beside_units)
        banks, squares, link = {}, [], t

        def z_unit(n):
            z, s = (za, zb)[n // 4], n % 4
            t = stream_x(ps[:, s, :], [banks[s] if n >= 4 else conv_end])

            def evacuate():
                need(act, t)
                banks[s] = A(act.activation(z[:, s, :], ps[:, s, :], ACT.Silu))
            return evacuate

        def unit_square(n):
            squares.append(chunk_sums(n, qkv[:, n, :], 6, [squares[n - 4]] if n >= 4 else []))

        for n in range(beside_units):
            evacuate = z_unit(n)
            unit_square(n)
            evacuate()
            for m, (c, k) in enumerate(taps[n * n_taps:(n + 1) * n_taps]):
                if c < 3:
                    cf_tap(c, k, own=c)
                else:
                    cf_tap(c, k, own=c, dst=rest, first=pool_taps)
                if n and m in (1, 3, 5) and chain:
                    need(dve, link)
                    need(act, link)
                    link = chain.pop(0)()
            for k in range(3 * n, 3 * n + 3):
                shared_tap(k)
        for n in range(beside_units, 8):
            unit_square(n)
        assert len(added) == pool_taps
        need(dve, added[-1], last[3])
        V(dve.tensor_tensor(cu[:, 3, :], cu[:, 3, :], rest, ALU.add))
        assert not chain
        def four_sums(out, rows, waits):
            need(dve, *waits)
            V(dve.tensor_tensor(rt[:, 0, :], rows[0], rows[1], ALU.add))
            t = V(dve.tensor_tensor(rt[:, 2, :], rows[2], rows[3], ALU.add))
            need(dve, t)
            t = V(dve.tensor_tensor(rt[:, 0, :], rt[:, 0, :], rt[:, 2, :], ALU.add))
            need(pe, t)
            return token_sums(out, rt[:, 0, :], True, True)

        need(act, squares[-1])
        t = inverse_root(scl[:], ps[:, 6, 0:8 * NT], 1.0)
        evacuate = z_unit(6)
        mean_sums = four_sums(ps[:, 7, 0:NT], [cu[:, c, :] for c in range(4)], C.now("dve", "pool", "pe"))
        need(act, mean_sums)
        tm = A(act.mul(epsc[:, 9:13], ps[:, 7, 0:NT], -1.0 / (4 * P)))
        need(pe, t)
        scaled = []
        for c in range(8):
            if c >= 2:
                need(pe, scaled[c - 2])
            need(dve, spread(ps[:, 4 + c % 2, :], scl[:, c * NT:(c + 1) * NT]))
            scaled.append(V(dve.scalar_tensor_tensor(
                out=qkv[:, c, :], in0=qkv[:, c, :], scalar=P ** -0.5 if c < 4 else 1.0, in1=ps[:, 4 + c % 2, :],
                op0=ALU.mult, op1=ALU.mult)))
        evacuate()
        need(pe, tm)
        t = spread(ps[:, 7, :], epsc[:, 9:13])
        evacuate = z_unit(7)
        need(dve, t)
        sq = []
        for c in range(4):
            t = V(dve.tensor_tensor(cu[:, c, :], ps[:, 7, :], cu[:, c, :], ALU.add))
            need(act, t)
            sq.append(A(act.activation(rt[:, c, :], cu[:, c, :], ACT.Square)))
        t = four_sums(ps[:, 6, 0:NT], [rt[:, c, :] for c in range(4)], sq)
        evacuate()
        need(act, t)
        t = inverse_root(scl[:, 0:NT], ps[:, 6, 0:NT], 4 * P)
        need(pe, t)
        t = spread(ps[:, 5, :], scl[:, 0:NT])
        need(dve, t)
        done = []
        for c in range(4):
            t = V(dve.tensor_tensor(cu[:, c, :], cu[:, c, :], ps[:, 5, :], ALU.mult))
            need(act, t)
            done.append(A(act.activation(cu[:, c, :], cu[:, c, :], ACT.Silu, bias=lcl("ln_b", c),
                                         scale=lcl("ln_w", c))))
        for c in range(4):
            need(dve, done[c])
            V(dve.tensor_tensor(cu[:, c, :], cu[:, c, :], zb[:, c, :], ALU.mult))
        rendezvous()
        m_prj.close()
        delta(qkv, gl, bt, o, levels)
        wide.close()
        for c in range(4):
            t = chunk_sums(c, o[:, c, :], 6)
        need(act, t)
        t = inverse_root(scl[:, 0:4 * NT], ps[:, 6, 0:4 * NT], P)
        need(pe, t)
        for c in range(4):
            t = spread(ps[:, c, :], scl[:, c * NT:(c + 1) * NT])
            need(dve, t)
            t = V(dve.scalar_tensor_tensor(out=o[:, c, :], in0=o[:, c, :], scalar=lcl("dn_w"), in1=ps[:, c, :],
                                           op0=ALU.mult, op1=ALU.mult))
            need(dve, t)
            V(dve.tensor_tensor(o[:, c, :], o[:, c, :], za[:, c, :], ALU.mult))
        need(act, *C.now("dve"))
        need(dve, *C.now("dve"))
        fh = sb("fh", [P, 8, S], F32R, wide, side="right")
        fl = sb("fl", [P, 8, S], F32R, wide, side="right")
        split_into(fh, fl, [o[:, c, :] for c in range(4)] + [cu[:, c, :] for c in range(4)])
        rendezvous()
        keep.close()
        merge("m2", fh, fl, lambda r, i: lcol[:, bass.ds(i * 4 + 8 * r + LCOLS["gate_b"][0], 4)])
        wide.close()

    def delta(qkv, gl, bt, o, levels):
        mem = ExitStack()
        bufs = [[sb(f"dl{d}_{n}", [P, DN_H, P], ctx=mem) for n in range(9)] + [
            rt[:, 2 * d + r, :].rearrange("p (h c) -> p h c", h=DN_H) for r in range(2)] for d in range(2)]
        sm = sb("dl_small", [P, 2, 8, DN_H], ctx=mem)

        def direction(d, i):
            KT, Y, T, DT, qd, kg, kdec, vt, U, AT, St = bufs[d]
            gs, be, gc, gtot, eg, et, ekd, tmp = (sm[:, d, r, :] for r in range(8))
            at = i * P if d == 0 else i * (-P) + (NT - 1) * P
            tile = i if d == 0 else i * (-1) + (NT - 1)
            tri = mat("tri_f" if d == 0 else "tri_b")
            strict = mat("negstrict_f" if d == 0 else "negstrict_b")
            B = [ps[:, 4 * d + r, :] for r in range(4)]
            B4 = [b.rearrange("p (h c) -> p h c", h=DN_H) for b in B]
            q, k, v_ = (qkv[:, 4 * r:4 * r + 4, bass.ds(at, P)] for r in range(3))

            def per_head(f):
                for hd in range(DN_H):
                    ins = f(hd)
                return PE(ins)

            tk = A(act.copy(KT[:], k))
            tv = G(pool.tensor_copy(Y[:], v_))
            V(dve.tensor_copy(gs, gl[:, tile, 4 * d:4 * d + 4]))
            tg = V(dve.tensor_copy(be, bt[:, tile, 4 * d:4 * d + 4]))
            need(pe, tg)
            t = per_head(lambda n: pe.matmul(B[0][:, n * P:(n + 1) * P], gs[:, n:n + 1].broadcast_to([P, P]), tri,
                                             start=True, stop=True))
            pe.matmul(B[1][:, 0:4], tri, gs, start=True, stop=True)
            t1 = PE(pe.matmul(B[1][:, 4:8], mat("ones"), gs, start=True, stop=True))
            need(pe, tk)
            tkk = per_head(lambda n: pe.matmul(B[2][:, n * P:(n + 1) * P], KT[:, n, :], KT[:, n, :], start=True,
                                               stop=True))
            tqk = per_head(lambda n: pe.matmul(B[3][:, n * P:(n + 1) * P], KT[:, n, :], q[:, n, :], start=True,
                                               stop=True))
            yield
            need(act, t1)
            A(act.copy(gc, B[1][:, 0:4]))
            t = A(act.copy(gtot, B[1][:, 4:8]))
            need(dve, t)
            ts = V(dve.tensor_tensor(DT[:], B4[0], heads4(gc), ALU.subtract))
            te = V(dve.tensor_tensor(tmp, gtot, gc, ALU.subtract))
            need(act, ts, te)
            tq = A(act.activation(qd[:], B4[0], ACT.Exp))
            A(act.activation(eg, gc, ACT.Exp))
            A(act.activation(et, gtot, ACT.Exp))
            tx = A(act.activation(ekd, tmp, ACT.Exp))
            need(dve, ts)
            t = V(dve.tensor_scalar(DT[:], DT[:], 0.0, None, ALU.min))
            need(act, t)
            t = A(act.activation(DT[:], DT[:], ACT.Exp))
            need(pe, tq, tv)
            ttk = per_head(lambda n: pe.transpose(B[0][:, n * P:(n + 1) * P], KT[:, n, :], mat("ident")))
            need(pe, t1, *C.now("act"))
            ttv = per_head(lambda n: pe.transpose(B[1][:, n * P:(n + 1) * P], Y[:, n, :], mat("ident")))
            yield
            need(dve, tx)
            t2 = V(dve.tensor_scalar(eg, eg, -1.0, None, ALU.mult))
            need(dve, t)
            t = V(dve.tensor_tensor(DT[:], DT[:], all_heads(tri), ALU.mult))
            need(dve, t, tkk)
            ta = V(dve.tensor_tensor(AT[:], B4[2], DT[:], ALU.mult))
            need(dve, ta)
            ta = V(dve.tensor_tensor(AT[:], AT[:], all_heads(strict), ALU.mult))
            need(pe, ta)
            ta = per_head(lambda n: pe.transpose(B[2][:, n * P:(n + 1) * P], AT[:, n, :], mat("ident")))
            need(dve, tqk)
            tdt = V(dve.tensor_tensor(DT[:], B4[3], DT[:], ALU.mult))
            need(act, t2, ttk)
            for hd in range(DN_H):
                A(act.activation(kg[:, hd, :], B4[0][:, hd, :], ACT.Copy, scale=eg[:, hd:hd + 1]))
            for hd in range(DN_H):
                tkd = A(act.activation(kdec[:, hd, :], B4[0][:, hd, :], ACT.Copy, scale=ekd[:, hd:hd + 1]))
            need(act, ttv)
            tv = A(act.copy(vt[:], B4[1]))
            yield
            ti = V(dve.tensor_copy(T[:], all_heads(mat("ident"))))
            need(dve, ta, tv)
            t = V(dve.tensor_tensor(Y[:], B4[2], heads4(be), ALU.mult))
            need(dve, t, ti)
            settle_dve(d)
            tt = V(dve.copy_predicated(T[:], all_heads(levels[:, d, 0, :]), Y[:]))
            for lv in range(1, len(LEVELS) + 1):
                need(pe, tt, tdt)
                tu = per_head(lambda n: pe.transpose(B[3][:, n * P:(n + 1) * P], T[:, n, :], mat("ident")))
                if lv < len(LEVELS):
                    need(pe, tkd)
                    ty = per_head(lambda n: pe.matmul(B[0][:, n * P:(n + 1) * P], AT[:, n, :], T[:, n, :],
                                                      start=True, stop=True))
                yield
                need(dve, tu)
                tu = V(dve.tensor_tensor(U[:], B4[3], heads4(be), ALU.mult))
                if lv == 1:
                    tq2 = V(dve.tensor_tensor(qd[:], qd[:], q, ALU.mult))
                if lv == len(LEVELS):
                    break
                need(act, ty, tt)
                ty = A(act.copy(Y[:], B4[0]))
                yield
                need(pe, tu, ty, tv)
                t = per_head(lambda n: pe.matmul(B[1][:, n * P:(n + 1) * P], U[:, n, :], Y[:, n, :],
                                                 start=True, stop=True))
                yield
                need(dve, t)
                settle_dve(d)
                tt = V(dve.copy_predicated(T[:], all_heads(levels[:, d, lv, :]), B4[1]))
            need(pe, tu, tkd)
            t = per_head(lambda n: pe.matmul(B[0][:, n * P:(n + 1) * P], kg[:, n, :], U[:, n, :], start=True,
                                             stop=True))
            need(act, t)
            tkc = A(act.copy(KT[:], B4[0]))
            yield
            need(pe, tkc, tt)

            def v_new(n):
                out = B[1][:, n * P:(n + 1) * P]
                pe.matmul(out, U[:, n, :], vt[:, n, :], start=True, stop=False)
                return pe.matmul(out, KT[:, n, :], St[:, n, :], start=False, stop=True)
            t = per_head(v_new)
            need(act, t)
            tvn = A(act.copy(AT[:], B4[1]))
            yield
            need(pe, tvn, tq2)

            def out_(n):
                out = B[2][:, n * P:(n + 1) * P]
                pe.matmul(out, St[:, n, :], qd[:, n, :], start=True, stop=False)
                return pe.matmul(out, AT[:, n, :], DT[:, n, :], start=False, stop=True)
            t = per_head(out_)
            t2 = per_head(lambda n: pe.matmul(B[3][:, n * P:(n + 1) * P], kdec[:, n, :], AT[:, n, :], start=True,
                                              stop=True))
            yield
            need(dve, t)
            ov = o[:, :, bass.ds(at, P)]
            V(dve.tensor_tensor(ov, ov, B4[2], ALU.add))
            t = V(dve.tensor_tensor(St[:], St[:], heads4(et), ALU.mult))
            need(dve, t, t2)
            V(dve.tensor_tensor(St[:], St[:], B4[3], ALU.add))
            yield

        for d in range(2):
            V(dve.memset(bufs[d][10][:], 0.0))
        with C.loop("chunk", NT) as i:
            rendezvous()
            gens = [direction(0, i), direction(1, i)]
            live = True
            while live:
                live = False
                for g in gens:
                    if next(g, "end") != "end":
                        live = True
        rendezvous()
        mem.close()

    for k in range(KD):
        if k % 2 == 0:
            act.wait_ge(s_h[k // 2], 16)
        square_sum(k, k, None)
    for i in range(AHEAD):
        split_unit(Lin(i))
    ffn("ffn1", "norm_ffn1", early)
    mixer()
    ffn("ffn2", "norm_ffn2")
    norm_h(lambda k: col("norm_final", k))
    with C.loop("layer", N_LAYER) as l:
        layer(l, wab, levels)
    norm_h(lambda k: col("final2", k), store=True)
    return finish()


def build(nc, a):
    steps = {}
    for _ in range(6):
        scratch = a["fresh"]()
        found = program(scratch[0], scratch[1], steps)
        if found == steps:
            break
        steps = found
    assert program(nc, a, steps) == steps


def layout(x):
    f = np.float32

    def proj(w):
        k, n = w.shape
        return w.reshape(k // P, P, n // P, P).transpose(2, 1, 0, 3).reshape(n // P, P, k)

    def down(w):
        return w.reshape(w.shape[0] // P, P, D)

    def pairs(*ws):
        return np.stack(ws, 1).reshape(-1, P, ws[0].shape[-1])

    def ffn(g, u, d):
        return [pairs(proj(g), proj(u)), down(d)]

    units = ffn(x["ffn1_gate"][0], x["ffn1_up"][0], x["ffn1_down"][0])
    w = x["w_in"][0]
    widths = (512, 128, 128, 128, 128, 128, 128, 24, 512, 64, 64, 1024, 1024)
    nq, kc, vc, ksl, vsl, kwn, vwn, ng, sq, sk, sv, ga, gb = np.split(w, np.cumsum(widths)[:-1], axis=1)
    both = np.concatenate([sv, ng, sv[:, :40]], 1)
    units += [proj(nq), proj(sq), proj(ksl), proj(kwn), proj(np.concatenate([sk, sk], 1)), proj(kc), proj(vc),
              proj(vsl), proj(vwn), proj(both)]
    ab = np.concatenate([proj(x["w_branch_a"][0]), proj(x["w_branch_b"][0])], 2)
    units += [pairs(proj(ga), proj(gb)), ab, proj(x["w_out"][0])]
    units += ffn(x["ffn2_gate"][0], x["ffn2_up"][0], x["ffn2_down"][0])
    wab = []
    for l in range(N_LAYER):
        w = x["w_in_2"][l]
        qkv, za, al, bl, val, glu, zb, gt = np.split(w, np.cumsum((1536, 512, 8, 8, 512, 512, 512)), axis=1)
        wab.append(np.concatenate([al, bl], 1).reshape(KD, P, 16).transpose(1, 0, 2))
        g = gt.reshape(D, 2, D)
        out = np.concatenate([proj(x["w_dn_out_2"][l]), proj(x["w_cf_out_2"][l])], 2)
        units += [pairs(proj(glu), proj(val)), proj(qkv), proj(za), proj(zb),
                  pairs(proj(g[:, 0]), proj(g[:, 1]), out), proj(x["w_out_2"][l])]
    stream = np.concatenate(units)
    assert stream.shape == (N_UNITS, P, UNIT), stream.shape
    stream = np.concatenate([stream, stream[:SPARE]])

    def c(v):
        return np.asarray(v).reshape(-1, P).T

    def wide(v):
        return np.broadcast_to(np.asarray(v).reshape(1, -1), (P, np.asarray(v).size))

    def pe2(v):
        return v.reshape(16, 2 * HD).T

    half = HD // 2
    inv = (np.float32(10000.0) ** (-np.arange(half, dtype=f) / f(half))).astype(f)
    parts = {"norm_ffn1": c(x["norm_ffn1"][0]), "norm_mix": c(x["norm_mix"][0]), "norm_ffn2": c(x["norm_ffn2"][0]),
             "norm_final": c(x["norm_final"]), "final2": c(x["final_norm_w_2"]), "sinks": wide(x["swa_sinks"][0]),
             "pe_k": pe2(x["cmp_pe_k"][0]), "pe_v": pe2(x["cmp_pe_v"][0]), "inv_freq": np.tile(inv, 4).reshape(P, 1)}
    cols = np.concatenate([parts[n] for n in COLS], 1).astype(f)
    lc = []
    for l in range(N_LAYER):
        parts = {"norm": c(x["norm_w_2"][l]),
                 "qkv_w": x["qkv_conv_w_2"][l].reshape(QKV_TAPS, 12, P).transpose(2, 1, 0).reshape(P, -1),
                 "cf_w": x["cf_conv_w_2"][l].reshape(CF_TAPS, 4, P).transpose(2, 1, 0).reshape(P, -1),
                 "cf_b": c(x["cf_conv_b_2"][l]), "ln_w": c(x["cf_ln_w_2"][l]), "ln_b": c(x["cf_ln_b_2"][l]),
                 "gate_b": c(x["gate_b_2"][l]), "dn_w": c(x["dn_norm_w_2"][l]),
                 "a_log": wide(x["a_log_2"][l]), "dt_bias": wide(x["dt_bias_2"][l])}
        lc.append(np.concatenate([parts[n] for n in LCOLS], 1))
    i = np.arange(P)
    rot = np.zeros((P, P), f)
    for m in range(P):
        if m % HD < half:
            rot[m + half, m] = -1
        else:
            rot[m - half, m] = 1
    m = {"ident": np.eye(P), "ones": np.ones((P, P)), "rot": rot,
         "tri_f": i[:, None] <= i[None, :], "tri_b": i[:, None] >= i[None, :],
         "negstrict_f": -1.0 * (i[:, None] < i[None, :]), "negstrict_b": -1.0 * (i[:, None] > i[None, :])}
    mats = np.stack([m[n] for n in MATS], 1).astype(f)
    lev = []
    for b in LEVELS:
        blk = i // b
        sib = (blk[:, None] // 2 == blk[None, :] // 2)
        lev.append(sib & (blk[:, None] > blk[None, :]))
    lev = np.stack(lev, 1)
    levels = np.stack([lev, lev.transpose(2, 1, 0)], 1).astype(f)
    q, s = i[:, None], i[None, :]
    causal = np.where(s > q, NEG, 0.0)
    s = np.arange(2 * P)[None, :]
    band = np.where((s - P <= q) & (s > q), 0.0, NEG)
    t = np.arange(S).reshape(NT, P).T[:, :, None]
    n = np.arange(32)[None, None, :]
    vis = np.where((16 * n + 31 <= t) & (n < CMP_N), 0.0, NEG).reshape(P, -1)
    valid = (np.arange(S).reshape(NT, P).T >= 31) * 1.0
    masks = np.concatenate([causal, band, vis, valid], 1).astype(f)
    w1 = [x[n][0].reshape(16, P, 2 * P).transpose(1, 0, 2) for n in ("cmp_k_w1", "cmp_v_w1")]
    w2 = [x[n][0].reshape(2, P, HD).transpose(1, 0, 2) for n in ("cmp_k_w2", "cmp_v_w2")]
    w2k = np.concatenate([w2[0], w2[0]], 2)
    ca = np.ascontiguousarray
    return {"stream": ca(stream), "xT": ca(x["x"][0].T.reshape(KD, P, S).transpose(1, 0, 2)), "cols": ca(cols),
            "lcols": ca(np.stack(lc, 1)), "mats": ca(mats), "levels": ca(levels), "masks": ca(masks),
            "w1": ca(np.stack(w1)), "w2k": ca(w2k), "w2v": ca(w2[1]), "wab": ca(np.stack(wab)),
            "pos": ca(np.tile(x["positions"].reshape(1, S), (P, 1)))}


def kernel(**inputs):
    import concourse.bacc as bacc
    from concourse.bass_utils import run_bass_kernel_spmd

    arrays = layout({k: np.asarray(v) for k, v in inputs.items()})

    def fresh():
        nc = bacc.Bacc("TRN2", target_bir_lowering=False, num_devices=1)
        a = {n: nc.dram_tensor("in_" + n, v.shape, mybir.dt.from_np(v.dtype), kind="ExternalInput").ap()
             for n, v in arrays.items()}
        a["outT"] = nc.dram_tensor("outT", (P, KD, S), F32, kind="ExternalOutput").ap()
        a["fresh"] = fresh
        return nc, a

    nc, a = fresh()
    build(nc, a)
    r = run_bass_kernel_spmd(nc, [{"in_" + n: v for n, v in arrays.items()}], core_ids=[0])
    out = r.results[0]["outT"]
    return np.ascontiguousarray(out.transpose(1, 0, 2).reshape(D, S).T).reshape(1, S, D)
```
